# Optimizing a Trainium2 kernel written in Bass

```python
import jax
import jax.numpy as jnp
from jax import lax
import numpy as np
import math
import jax, jax.numpy as jnp

D_MODEL = 2048
BATCH = 1
SEQ = 512
DEPTH = 1

CHUNK = 64
Q_BLOCK = 128
ROPE_THETA = 10000.0
EPS = 1e-6
MIX_WIDTH = D_MODEL
HEAD_DIM = 128
A_WIDTH = MIX_WIDTH // 2
B_WIDTH = MIX_WIDTH - A_WIDTH
A_HEADS = A_WIDTH // HEAD_DIM
B_HEADS = B_WIDTH // HEAD_DIM
IDX_HEADS = 16
IDX_DIM = 64
TOPK_MAX = 256
SPLITS = (A_WIDTH, A_WIDTH, A_WIDTH, A_WIDTH, IDX_HEADS * IDX_DIM, IDX_DIM, IDX_HEADS,
          B_WIDTH, B_WIDTH, B_WIDTH, B_WIDTH)
N_IN = sum(SPLITS)


def rms_norm(t, g):
    tf = t.astype(jnp.float32)
    y = tf * lax.rsqrt(jnp.mean(tf * tf, axis=-1, keepdims=True) + EPS)
    return (y * g.astype(jnp.float32)).astype(t.dtype)

def rope(t, pos):
    half = t.shape[-1] // 2
    inv_freq = ROPE_THETA ** (-jnp.arange(half, dtype=jnp.float32) / half)
    ang = pos.astype(jnp.float32)[:, :, None, None] * inv_freq
    cos, sin = jnp.cos(ang), jnp.sin(ang)
    tf = t.astype(jnp.float32)
    t1, t2 = tf[..., :half], tf[..., half:]
    return jnp.concatenate([t1 * cos - t2 * sin, t2 * cos + t1 * sin], axis=-1).astype(t.dtype)

def dsa_sparse_attention(q, k, v, q_idx, k_idx, w_idx):
    bsz, seq, n_heads, head_dim = q.shape
    n_sel = min(TOPK_MAX, seq // 4)
    key_pos = jnp.arange(seq)
    idx_scale = IDX_DIM ** -0.5
    att_scale = head_dim ** -0.5
    k_idx32 = k_idx.astype(jnp.float32)

    def one_block(blk):
        start = blk * Q_BLOCK
        qb = lax.dynamic_slice_in_dim(q, start, Q_BLOCK, axis=1)
        qib = lax.dynamic_slice_in_dim(q_idx, start, Q_BLOCK, axis=1).astype(jnp.float32)
        wb = lax.dynamic_slice_in_dim(w_idx, start, Q_BLOCK, axis=1).astype(jnp.float32)
        q_pos = start + jnp.arange(Q_BLOCK)
        limit = (q_pos // CHUNK + 1) * CHUNK
        admissible = key_pos[None, :] < limit[:, None]
        logits = jnp.einsum('bqhd,bsd->bqhs', qib, k_idx32) * idx_scale
        score = jnp.einsum('bqhs,bqh->bqs', jax.nn.relu(logits), wb)
        score = jnp.where(admissible[None], score, -jnp.inf)
        _, sel = lax.top_k(score, n_sel)
        sel_ok = sel < limit[None, :, None]
        kg = jax.vmap(lambda kk, ii: kk[ii])(k, sel)
        vg = jax.vmap(lambda vv, ii: vv[ii])(v, sel)
        s = jnp.einsum('bqhd,bqnhd->bqhn', qb, kg).astype(jnp.float32) * att_scale
        s = jnp.where(sel_ok[:, :, None, :], s, -jnp.inf)
        p = jax.nn.softmax(s, axis=-1)
        return jnp.einsum('bqhn,bqnhd->bqhd', p.astype(v.dtype), vg)

    out = lax.map(one_block, jnp.arange(seq // Q_BLOCK))
    return jnp.moveaxis(out, 0, 1).reshape(bsz, seq, n_heads, head_dim)

def hgrn2_recurrence(q, f_pre, i_in, lower_bound):
    bsz, seq, n_heads, d = q.shape
    n_chunks = seq // CHUNK

    def to_chunks(t):
        return t.astype(jnp.float32).reshape(bsz, n_chunks, CHUNK, n_heads, d).transpose(0, 3, 1, 2, 4)

    lb = lower_bound.astype(jnp.float32)[None, :, None, None, :]
    qc = jax.nn.silu(to_chunks(q))
    forget = lb + (1.0 - lb) * jax.nn.sigmoid(to_chunks(f_pre))
    kc = 1.0 - forget
    vc = to_chunks(i_in)
    b = jnp.cumsum(jnp.log(forget), axis=3)
    b_mid = b[:, :, :, CHUNK // 2 - 1:CHUNK // 2, :]
    b_last = b[:, :, :, -1:, :]
    causal = jnp.tril(jnp.ones((CHUNK, CHUNK), dtype=bool))
    a = jnp.einsum('bhncd,bhnsd->bhncs', qc * jnp.exp(b - b_mid), kc * jnp.exp(b_mid - b))
    a = jnp.where(causal, a, 0.0)
    o_intra = jnp.einsum('bhncs,bhnse->bhnce', a, vc)
    chunk_state = jnp.einsum('bhnsd,bhnse->bhnde', kc * jnp.exp(b_last - b), vc)
    chunk_decay = jnp.exp(b_last[:, :, :, 0, :])

    def step(state, inp):
        ds, dec = inp
        return state * dec[..., None] + ds, state

    _, prev = lax.scan(step, jnp.zeros((bsz, n_heads, d, d), jnp.float32),
                       (jnp.moveaxis(chunk_state, 2, 0), jnp.moveaxis(chunk_decay, 2, 0)))
    prev = jnp.moveaxis(prev, 0, 2)
    o_inter = jnp.einsum('bhncd,bhnde->bhnce', qc * jnp.exp(b), prev)
    o = (o_intra + o_inter).transpose(0, 2, 3, 1, 4).reshape(bsz, seq, n_heads, d)
    return o.astype(q.dtype)

def first_inputs(seed: int = 0) -> dict:
    key = jax.random.key(seed)
    ks = jax.random.split(key, 14)
    x = jax.random.normal(ks[0], (BATCH, SEQ, D_MODEL), jnp.float32)
    c = jax.random.normal(ks[1], (BATCH, D_MODEL), jnp.float32)
    offset = jax.random.randint(ks[2], (BATCH, 1), 0, 4096, dtype=jnp.int32)
    positions = (offset + jnp.arange(SEQ, dtype=jnp.int32)[None, :]).astype(jnp.int32)
    ada_w = jax.random.normal(ks[3], (DEPTH, D_MODEL, 3 * D_MODEL), jnp.float32) * (0.5 * D_MODEL ** -0.5)
    ada_b = 0.02 * jax.random.normal(ks[4], (DEPTH, 3 * D_MODEL), jnp.float32)
    norm_g = 1.0 + 0.02 * jax.random.normal(ks[5], (DEPTH, D_MODEL), jnp.float32)
    w_in = jax.random.normal(ks[6], (DEPTH, D_MODEL, N_IN), jnp.float32) * D_MODEL ** -0.5
    q_norm_g = 1.0 + 0.02 * jax.random.normal(ks[7], (DEPTH, HEAD_DIM), jnp.float32)
    k_norm_g = 1.0 + 0.02 * jax.random.normal(ks[8], (DEPTH, HEAD_DIM), jnp.float32)
    idx_k_norm_g = 1.0 + 0.02 * jax.random.normal(ks[9], (DEPTH, IDX_DIM), jnp.float32)
    hgrn_lb_logits = 0.1 * jax.random.normal(ks[10], (DEPTH + 1, B_WIDTH), jnp.float32)
    hgrn_norm_g = 1.0 + 0.02 * jax.random.normal(ks[11], (DEPTH, HEAD_DIM), jnp.float32)
    w_out = jax.random.normal(ks[12], (DEPTH, MIX_WIDTH, D_MODEL), jnp.float32) * MIX_WIDTH ** -0.5
    return {'x': x, 'c': c, 'positions': positions, 'ada_w': ada_w, 'ada_b': ada_b,
            'norm_g': norm_g, 'w_in': w_in, 'q_norm_g': q_norm_g, 'k_norm_g': k_norm_g,
            'idx_k_norm_g': idx_k_norm_g, 'hgrn_lb_logits': hgrn_lb_logits,
            'hgrn_norm_g': hgrn_norm_g, 'w_out': w_out}

def first_block(x, c, positions, ada_w, ada_b, norm_g, w_in, q_norm_g, k_norm_g, idx_k_norm_g,
              hgrn_lb_logits, hgrn_norm_g, w_out):
    bsz, seq, _ = x.shape
    lower_bounds = jnp.cumsum(jax.nn.softmax(hgrn_lb_logits.astype(jnp.float32), axis=0), axis=0)
    offsets = np.cumsum(SPLITS)[:-1].tolist()
    for layer in range(DEPTH):
        mod = jax.nn.silu(c) @ ada_w[layer] + ada_b[layer]
        shift, scale, gate = jnp.split(mod, 3, axis=-1)
        h = rms_norm(x, norm_g[layer]) * (1.0 + scale[:, None, :]) + shift[:, None, :]
        proj = h @ w_in[layer]
        a_q, a_k, a_v, a_g, i_q, i_k, i_w, r_q, r_f, r_i, r_g = jnp.split(proj, offsets, axis=-1)

        q = rope(rms_norm(a_q.reshape(bsz, seq, A_HEADS, HEAD_DIM), q_norm_g[layer]), positions)
        k = rope(rms_norm(a_k.reshape(bsz, seq, A_HEADS, HEAD_DIM), k_norm_g[layer]), positions)
        v = a_v.reshape(bsz, seq, A_HEADS, HEAD_DIM)
        qi = rope(i_q.reshape(bsz, seq, IDX_HEADS, IDX_DIM), positions)
        ki = rope(rms_norm(i_k, idx_k_norm_g[layer])[:, :, None, :], positions)[:, :, 0, :]
        wi = i_w * (IDX_HEADS ** -0.5)
        o_a = dsa_sparse_attention(q, k, v, qi, ki, wi).reshape(bsz, seq, A_WIDTH) * jax.nn.silu(a_g)

        lb = lower_bounds[layer].reshape(B_HEADS, HEAD_DIM)
        o_r = hgrn2_recurrence(r_q.reshape(bsz, seq, B_HEADS, HEAD_DIM),
                               r_f.reshape(bsz, seq, B_HEADS, HEAD_DIM),
                               r_i.reshape(bsz, seq, B_HEADS, HEAD_DIM), lb)
        o_r = rms_norm(o_r, hgrn_norm_g[layer]).reshape(bsz, seq, B_WIDTH) * jax.nn.silu(r_g)

        mix = jnp.concatenate([o_a, o_r], axis=-1) @ w_out[layer]
        x = x + gate[:, None, :] * mix
    return x


DEPTH_2 = 2

SB_HEADS = 8
SB_HEAD_DIM = 128
SB_WIDTH = SB_HEADS * SB_HEAD_DIM
POOL_WINDOWS = (2, 4, 8, 16)
POOL_GROUPS = len(POOL_WINDOWS)
POOL_WIDTH = D_MODEL - SB_WIDTH
POOL_GROUP_DIM = POOL_WIDTH // POOL_GROUPS
MIX_WIDTH_2 = SB_WIDTH + POOL_WIDTH
EVEN_IN = 4 * SB_WIDTH + 2 * POOL_WIDTH
BLOCK_Q = 128

RWKV_HEAD_DIM = 64
RWKV_HEADS = D_MODEL // RWKV_HEAD_DIM
DECAY_LORA = 96
ICLR_LORA = 96
GN_EPS = 64e-5
L2_EPS = 1e-12

LN_EPS = 1e-5
DEEPNORM_ALPHA = (2 * DEPTH_2) ** 0.25
DEEPNORM_BETA = (8 * DEPTH_2) ** -0.25
N_EVEN = (DEPTH_2 + 1) // 2
N_ODD = DEPTH_2 // 2


def layer_norm(x, g, b):
    xf = x.astype(jnp.float32)
    mean = jnp.mean(xf, axis=-1, keepdims=True)
    var = jnp.mean(jnp.square(xf - mean), axis=-1, keepdims=True)
    return ((xf - mean) * lax.rsqrt(var + LN_EPS) * g + b).astype(x.dtype)

def stick_breaking_attention(q, k, v):
    S = q.shape[2]
    scale = SB_HEAD_DIM ** -0.5
    outs = []
    for start in range(0, S, BLOCK_Q):
        end = start + BLOCK_Q
        qb = q[:, :, start:end].astype(jnp.float32)
        kb = k[:, :, :end].astype(jnp.float32)
        vb = v[:, :, :end]
        z = jnp.einsum('bhqd,bhkd->bhqk', qb, kb) * scale
        t_idx = start + jnp.arange(BLOCK_Q)[:, None]
        s_idx = jnp.arange(end)[None, :]
        causal = s_idx < t_idx
        log_keep = jnp.where(causal, jax.nn.log_sigmoid(-z), 0.0)
        later = lax.cumsum(log_keep, axis=3, reverse=True) - log_keep
        weights = jnp.where(causal, jnp.exp(jax.nn.log_sigmoid(z) + later), 0.0)
        outs.append(jnp.einsum('bhqk,bhkd->bhqd', weights.astype(vb.dtype), vb))
    return jnp.concatenate(outs, axis=2)

def multiscale_pool(u, w_pool, pool_scale):
    B_, S, _ = u.shape
    ug = u.reshape(B_, S, POOL_GROUPS, POOL_GROUP_DIM).astype(jnp.float32)
    c0 = jnp.concatenate([jnp.zeros_like(ug[:, :1]), jnp.cumsum(ug, axis=1)], axis=1)
    pos = jnp.arange(1, S + 1, dtype=jnp.float32)
    outs = []
    for g, w in enumerate(POOL_WINDOWS):
        cg = c0[:, :, g]
        lower = jnp.concatenate([jnp.zeros_like(cg[:, :w - 1]), cg[:, :S - w + 1]], axis=1)
        count = jnp.minimum(pos, float(w))[None, :, None]
        outs.append((cg[:, 1:] - lower) / count - ug[:, :, g])
    pooled = jnp.stack(outs, axis=2)
    mixed = jnp.einsum('bsgc,gcd->bsgd', pooled, w_pool.astype(jnp.float32))
    return (mixed.reshape(B_, S, POOL_WIDTH) * pool_scale).astype(u.dtype)

def even_layer(x, w_in, w_pool, pool_scale, w_out):
    B_, S, _ = x.shape
    h = x @ w_in
    q, k, v, g_a, u, g_b = jnp.split(
        h, [SB_WIDTH, 2 * SB_WIDTH, 3 * SB_WIDTH, 4 * SB_WIDTH, 4 * SB_WIDTH + POOL_WIDTH], axis=-1)

    def heads(t):
        return t.reshape(B_, S, SB_HEADS, SB_HEAD_DIM).transpose(0, 2, 1, 3)

    o_a = stick_breaking_attention(heads(q), heads(k), heads(v))
    o_a = o_a.transpose(0, 2, 1, 3).reshape(B_, S, SB_WIDTH)
    o_b = multiscale_pool(u, w_pool, pool_scale)
    mixed = jnp.concatenate([o_a * jax.nn.silu(g_a), o_b * jax.nn.silu(g_b)], axis=-1)
    return mixed @ w_out

def wkv7_scan(r, w, k, v, kk, a):
    B_, S, H, N = r.shape

    def step(state, inp):
        r_t, w_t, k_t, v_t, kk_t, a_t = inp
        sa = jnp.einsum('bhvk,bhk->bhv', state, -kk_t)
        state = (state * w_t[:, :, None, :]
                 + sa[..., None] * (kk_t * a_t)[:, :, None, :]
                 + v_t[..., None] * k_t[:, :, None, :])
        return state, jnp.einsum('bhvk,bhk->bhv', state, r_t)

    xs = (jnp.moveaxis(r, 1, 0), jnp.moveaxis(w, 1, 0), jnp.moveaxis(k, 1, 0),
          jnp.moveaxis(v, 1, 0), jnp.moveaxis(kk, 1, 0), jnp.moveaxis(a, 1, 0))
    state0 = jnp.zeros((B_, H, N, N), jnp.float32)
    _, out = lax.scan(step, state0, xs)
    return jnp.moveaxis(out, 0, 1)

def odd_layer(x, mu, w_r, w_k, w_v, w_g, w0, w1, w2, a0, a1, a2, k_k, k_a, r_k, gn_w, gn_b, w_o):
    B_, S, D = x.shape
    H, N = RWKV_HEADS, RWKV_HEAD_DIM
    f32 = jnp.float32
    x_prev = jnp.pad(x, ((0, 0), (1, 0), (0, 0)))[:, :S]
    xx = x_prev - x
    xr = x + xx * mu[0]
    xw = x + xx * mu[1]
    xk = x + xx * mu[2]
    xv = x + xx * mu[3]
    xa = x + xx * mu[4]
    xg = x + xx * mu[5]
    r = (xr @ w_r).astype(f32)
    k = (xk @ w_k).astype(f32)
    v = (xv @ w_v).astype(f32)
    g = (xg @ w_g).astype(f32)
    w_log = -jax.nn.softplus(-(w0 + jnp.tanh(xw @ w1) @ w2).astype(f32)) - 0.5
    decay = jnp.exp(-jnp.exp(w_log))
    a = jax.nn.sigmoid((a0 + (xa @ a1) @ a2).astype(f32))
    kk = (k * k_k).reshape(B_, S, H, N)
    kk = kk / jnp.maximum(jnp.sqrt(jnp.sum(kk * kk, axis=-1, keepdims=True)), L2_EPS)
    k = k * (1.0 + (a - 1.0) * k_a)
    r = r.reshape(B_, S, H, N)
    k = k.reshape(B_, S, H, N)
    v = v.reshape(B_, S, H, N)
    o = wkv7_scan(r, decay.reshape(B_, S, H, N), k, v, kk, a.reshape(B_, S, H, N))
    mean = jnp.mean(o, axis=-1, keepdims=True)
    var = jnp.mean(jnp.square(o - mean), axis=-1, keepdims=True)
    o = ((o - mean) * lax.rsqrt(var + GN_EPS)).reshape(B_, S, D) * gn_w + gn_b
    bonus = jnp.sum(r * k * r_k, axis=-1, keepdims=True) * v
    o = (o + bonus.reshape(B_, S, D)) * jax.nn.silu(g)
    return o.astype(x.dtype) @ w_o

def second_inputs(seed: int = 0) -> dict:
    key = jax.random.key(seed)
    ks = list(jax.random.split(key, 32))
    f32 = jnp.float32

    def nrm(i, shape, scale):
        return scale * jax.random.normal(ks[i], shape, f32)

    def unif(i, shape, lo, hi):
        return jax.random.uniform(ks[i], shape, f32, lo, hi)

    D = D_MODEL
    H, N = RWKV_HEADS, RWKV_HEAD_DIM
    return {
        'x': nrm(0, (BATCH, SEQ, D), 1.0),
        'ev_w_in': nrm(1, (N_EVEN, D, EVEN_IN), D ** -0.5),
        'ev_w_pool': nrm(2, (N_EVEN, POOL_GROUPS, POOL_GROUP_DIM, POOL_GROUP_DIM), POOL_GROUP_DIM ** -0.5),
        'ev_pool_scale': 1.0 + nrm(3, (N_EVEN, POOL_WIDTH), 0.1),
        'ev_w_out': nrm(4, (N_EVEN, MIX_WIDTH_2, D), DEEPNORM_BETA * MIX_WIDTH_2 ** -0.5),
        'od_mu': unif(5, (N_ODD, 6, D), 0.0, 1.0),
        'od_w_r': nrm(6, (N_ODD, D, D), D ** -0.5),
        'od_w_k': nrm(7, (N_ODD, D, D), D ** -0.5),
        'od_w_v': nrm(8, (N_ODD, D, D), D ** -0.5),
        'od_w_g': nrm(9, (N_ODD, D, D), D ** -0.5),
        'od_w0': unif(10, (N_ODD, D), -6.0, 1.0),
        'od_w1': nrm(11, (N_ODD, D, DECAY_LORA), D ** -0.5),
        'od_w2': nrm(12, (N_ODD, DECAY_LORA, D), 0.5 * DECAY_LORA ** -0.5),
        'od_a0': nrm(13, (N_ODD, D), 0.1),
        'od_a1': nrm(14, (N_ODD, D, ICLR_LORA), D ** -0.5),
        'od_a2': nrm(15, (N_ODD, ICLR_LORA, D), 0.5 * ICLR_LORA ** -0.5),
        'od_k_k': 0.85 + nrm(16, (N_ODD, D), 0.05),
        'od_k_a': 1.0 + nrm(17, (N_ODD, D), 0.05),
        'od_r_k': nrm(18, (N_ODD, H, N), 0.1),
        'od_gn_w': 1.0 + nrm(19, (N_ODD, D), 0.05),
        'od_gn_b': nrm(20, (N_ODD, D), 0.02),
        'od_w_o': nrm(21, (N_ODD, D, D), DEEPNORM_BETA * D ** -0.5),
        'ln_g': 1.0 + nrm(22, (DEPTH_2, D), 0.02),
        'ln_b': nrm(23, (DEPTH_2, D), 0.02),
    }

def second_block(x, ev_w_in, ev_w_pool, ev_pool_scale, ev_w_out,
              od_mu, od_w_r, od_w_k, od_w_v, od_w_g, od_w0, od_w1, od_w2,
              od_a0, od_a1, od_a2, od_k_k, od_k_a, od_r_k, od_gn_w, od_gn_b, od_w_o,
              ln_g, ln_b):
    for layer in range(DEPTH_2):
        j = layer // 2
        if layer % 2 == 0:
            y = even_layer(x, ev_w_in[j], ev_w_pool[j], ev_pool_scale[j], ev_w_out[j])
        else:
            y = odd_layer(x, od_mu[j], od_w_r[j], od_w_k[j], od_w_v[j], od_w_g[j],
                          od_w0[j], od_w1[j], od_w2[j], od_a0[j], od_a1[j], od_a2[j],
                          od_k_k[j], od_k_a[j], od_r_k[j], od_gn_w[j], od_gn_b[j], od_w_o[j])
        x = layer_norm(DEEPNORM_ALPHA * x + y, ln_g[layer], ln_b[layer])
    return x


def setup_inputs(seed=0):
    out = dict(first_inputs(seed))
    for name, value in second_inputs(seed + 1).items():
        if name != "x":
            out[name + "_2"] = value
    return out


def reference(
    x, c, positions, ada_w, ada_b, norm_g, w_in, q_norm_g, k_norm_g, idx_k_norm_g,
    hgrn_lb_logits, hgrn_norm_g, w_out, ev_w_in_2, ev_w_pool_2, ev_pool_scale_2, ev_w_out_2,
    od_mu_2, od_w_r_2, od_w_k_2, od_w_v_2, od_w_g_2, od_w0_2, od_w1_2, od_w2_2, od_a0_2,
    od_a1_2, od_a2_2, od_k_k_2, od_k_a_2, od_r_k_2, od_gn_w_2, od_gn_b_2, od_w_o_2, ln_g_2,
    ln_b_2,
):
    x = first_block(
        x, c, positions, ada_w, ada_b, norm_g, w_in, q_norm_g, k_norm_g, idx_k_norm_g,
        hgrn_lb_logits, hgrn_norm_g, w_out,
    )
    return second_block(
        x, ev_w_in_2, ev_w_pool_2, ev_pool_scale_2, ev_w_out_2, od_mu_2, od_w_r_2, od_w_k_2,
        od_w_v_2, od_w_g_2, od_w0_2, od_w1_2, od_w2_2, od_a0_2, od_a1_2, od_a2_2, od_k_k_2,
        od_k_a_2, od_r_k_2, od_gn_w_2, od_gn_b_2, od_w_o_2, ln_g_2, ln_b_2,
    )


_drawn_inputs = setup_inputs


def setup_inputs(seed=0):
    import zlib

    import numpy as np

    out = dict(_drawn_inputs(seed))
    spreads = {}
    factors = {'ada_b': 4.129,
     'norm_g': 8.0,
     'q_norm_g': 8.0,
     'k_norm_g': 8.0,
     'idx_k_norm_g': 8.0,
     'hgrn_lb_logits': 8.0,
     'hgrn_norm_g': 8.0,
     'ev_pool_scale_2': 4.14,
     'od_w1_2': 8.0,
     'od_w2_2': 8.0,
     'od_a0_2': 8.0,
     'od_k_k_2': 36.091,
     'od_k_a_2': 6.318,
     'od_gn_w_2': 6.85,
     'od_gn_b_2': 25.707}
    for name, (base, spread) in spreads.items():
        noise = np.random.default_rng([zlib.crc32(name.encode()), seed]).standard_normal(out[name].shape)
        drawn = base * np.exp(spread * noise) if base else spread * noise
        out[name] = jnp.asarray(drawn.astype(out[name].dtype))
    for name, factor in factors.items():
        out[name] = (out[name] * factor).astype(out[name].dtype)
    return out
```

```python
import math
from contextlib import ExitStack

import numpy as np

import concourse.bass as bass
from concourse import mybir

F32 = mybir.dt.float32
F32R = mybir.dt.float32r
I32 = mybir.dt.int32
ACT = mybir.ActivationFunctionType
ALU = mybir.AluOpType
AX = mybir.AxisListType

P = 128
SEQ = 512
D = 2048
KT = D // P
TB = SEQ // P
SLOTS = 4
SKT = KT // SLOTS
GC = 512
HEADS = 8
HD = 128
IDX_HEADS, IDX_DIM, N_SEL = 16, 64, 128
CH = 64
NCH = SEQ // CH
PAIRS = KT
ADA_GROUPS = 3 * D // GC
RMS_EPS, LN_EPS, GN_EPS, L2_EPS = 1e-6, 1e-5, 64e-5, 1e-12
ALPHA = 4.0 ** 0.25
ATT_SCALE = HD ** -0.5
IDX_SCALE = IDX_DIM ** -0.5
WI_SCALE = IDX_HEADS ** -0.5
NEG = -1e30
INADMISSIBLE = -3.0e38
TAKEN = -3.3e38

G_KW = 0
G_QI = 1
G_ATT = G_QI + 2
G_HG = G_ATT + HEADS
G_OUT1 = G_HG + HEADS
G_EVA = G_OUT1 + 4
G_POOL = G_EVA + HEADS
G_OUT2 = G_POOL + 4
G_LORA = G_OUT2 + 4
G_RW = G_LORA + 2
G_OUT3 = G_RW + 16
GROUPS = G_OUT3 + 4

COLS = {}
_at = 0
for _name, _n in (("c", 16), ("ada_b", 48), ("norm_g", 16), ("qg", 1), ("kg", 1), ("ikg", 1), ("lb0", 8),
                  ("lb1", 8), ("hg", 1), ("pscale", 8), ("mu", 96), ("w0", 16), ("a0", 16), ("k_k", 16),
                  ("k_a", 16), ("r_k", 16), ("gn_w", 16), ("gn_b", 16), ("ln_g", 32), ("ln_b", 32), ("freq", 2)):
    COLS[_name] = _at
    _at += _n
NCOLS = _at

MATS = ("ident", "mean128", "mean64", "swap128", "swap64", "neg_suffix", "neg_ones", "later_only", "later_neg",
        "mean2048", "ones64", "strict64", "incl_each", "lev1", "lev1t", "lev2t", "lev3t", "lev4t", "lev5t", "lev6t")
NMATS = len(MATS)
PI_IN = float(np.nextafter(np.float32(math.pi), np.float32(0)))


def _two_pi_parts():
    a = math.floor(2 * math.pi * 64) / 64
    b = math.floor((2 * math.pi - a) * 2 ** 17) / 2 ** 17
    return a, b, 2 * math.pi - a - b


TWO_PI = _two_pi_parts()
BAND_W = P + 16

ROW_W = [P * (b + 1) for b in range(TB)]
ROW_O = [sum(ROW_W[:b]) for b in range(TB)]
COL_W = [SEQ - P * b for b in range(TB)]
COL_O = [sum(COL_W[:b]) for b in range(TB)]
CAUSAL = sum(ROW_W)


def wait(eng, sem, value):
    if not isinstance(value, int) or value > 0:
        eng.wait_ge(sem, value)


def tile(buf, i):
    return buf[:, bass.ds(i * SEQ, SEQ)]


def build(nc, xT, positions, cols_d, mats_d, causal_i_d, rows_d, band_d, wpool_d, lora_d, ada_d, w_d, out):
    ctx = ExitStack()
    with ctx:
        def sb(name, shape, dt=F32):
            return ctx.enter_context(nc.sbuf_tensor(name, shape, dt))

        def sem(name):
            return ctx.enter_context(nc.semaphore(name))

        x1_d = nc.dram_tensor("x1_scratch", (KT, P, SEQ), F32).ap()
        rkvg_d = nc.dram_tensor("rkvg_scratch", (4, KT, P, SEQ), F32).ap()

        at = (nc.sbuf_base + 31) // 32 * 32
        WS = sb("WS", [P, (2 * KT + 4 * SKT) * SEQ])

        WS_AT = at

        def placed(name, shape, offset):
            return nc.alloc_sbuf_tensor_at(name, shape, F32R, offset=WS_AT + 4 * offset)

        XH = placed("XH", [P, KT * SEQ], 0)
        XL = placed("XL", [P, KT * SEQ], KT * SEQ)
        WH = [placed(f"WH{r}", [P, SKT, GC], (2 * KT + SKT * r) * SEQ) for r in range(2)]
        WL = [placed(f"WL{r}", [P, SKT, GC], (2 * KT + SKT * (2 + r)) * SEQ) for r in range(2)]
        X = sb("X", [P, KT * SEQ])
        RAW = [sb(f"RAW{r}", [P, SKT * GC]) for r in range(2)]
        NWK = 18
        WK = sb("WK", [P, NWK * SEQ])
        TBL = sb("TBL", [P, CAUSAL + 4 * SEQ])
        COL = sb("COL", [P, NCOLS])
        MOD = sb("MOD", [P, 48])
        LB = sb("LB", [P, 8])
        OMLB = sb("OMLB", [P, 8])
        MAT = sb("MAT", [P, NMATS * P])
        SMALL = sb("SMALL", [P, 128])
        CI = sb("CI", [P, 3 * P], I32)
        SC = sb("SC", [P, 8])

        PJ = ctx.enter_context(nc.psum_tensor("PJ", [P, 4, SEQ], F32))
        AB = ctx.enter_context(nc.psum_tensor("AB", [P, 4, SEQ], F32))

        def mat(name):
            i = MATS.index(name)
            return MAT[:, i * P:(i + 1) * P]

        def col(name, i=0):
            return COL[:, bass.ds(COLS[name] + i, 1)]

        def wk(i, n=1):
            return WK[:, i * SEQ:(i + n) * SEQ]

        MASK = TBL[:, 0:CAUSAL]
        COS = TBL[:, CAUSAL:CAUSAL + SEQ]
        SIN = TBL[:, CAUSAL + SEQ:CAUSAL + 2 * SEQ]
        COSI = TBL[:, CAUSAL + 2 * SEQ:CAUSAL + 3 * SEQ]
        SINI = TBL[:, CAUSAL + 3 * SEQ:CAUSAL + 4 * SEQ]
        RESET = COSI
        BAND = TBL[:, 0:8 * BAND_W]
        WP = TBL[:, 8 * BAND_W:8 * BAND_W + SEQ]

        consts_in = sem("consts_in")
        x_in = sem("x_in")
        ada_in = [sem(f"ada_in{r}") for r in range(4)]
        ada_used = sem("ada_used")
        silu_c = sem("silu_c")
        mod_done = sem("mod_done")
        pos_f = sem("pos_f")
        angles = sem("angles")
        x_sq = sem("x_sq")
        x_sq_used = sem("x_sq_used")
        x_ms = sem("x_ms")
        x_sd = sem("x_sd")
        raw_in = [sem(f"raw_in{r}") for r in range(2)]
        wh_ready = sem("wh_ready")
        wl_ready = sem("wl_ready")
        slot_done = sem("slot_done")
        evac_a = sem("evac_a")
        evac_d = sem("evac_d")
        src_ready = sem("src_ready")
        xh_ready = sem("xh_ready")
        xl_ready = sem("xl_ready")
        table_in = sem("table_in")
        band_in = sem("band_in")
        S = {}

        def s(name):
            if name not in S:
                S[name] = sem(name)
            return S[name]

        for name in ("sq", "stat", "sd", "qn", "swapped", "roped", "scores", "masked", "expd", "probs", "pt_t",
                     "pt_a", "pt_d", "pv", "mix_done", "gs"):
            s("at_" + name)
        block = ctx.enter_context(nc.Block())

        def pe_slot(pe, G, k, refill=None, tiles=4, bank=None):
            bank = PJ if bank is None else bank
            g = SLOTS * G + k
            if refill is not None:
                wait(pe, xl_ready, KT * refill + SKT * (k + 1))
            wait(pe, wl_ready, g + 1)
            for n in range(tiles):
                for j in range(SKT):
                    kt = SKT * k + j
                    hi = WH[k % 2][:, j, n * P:(n + 1) * P]
                    lo = WL[k % 2][:, j, n * P:(n + 1) * P]
                    xh, xl = tile(XH, kt), tile(XL, kt)
                    first, last = k == 0 and j == 0, k == SLOTS - 1 and j == SKT - 1
                    nc.tensor.matmul(bank[:, n, :], hi, xh, start=first, stop=False)
                    nc.tensor.matmul(bank[:, n, :], hi, xl, start=False, stop=False)
                    m = nc.tensor.matmul(bank[:, n, :], lo, xh, start=False, stop=last)
            m.then_inc(slot_done, 1)

        def pe_group(pe, G, steps=None, refill=None, tiles=4, bank=None, ago=0):
            wait(pe, evac_a, G - ago)
            wait(pe, evac_d, G - ago)
            for k in range(SLOTS):
                pe_slot(pe, G, k, refill, tiles, bank)
                if steps is not None:
                    steps(k)
            if steps is not None:
                steps(4)

        def act_split(act, G, k):
            g = SLOTS * G + k
            wait(act, raw_in[k % 2], 16 * (2 * G + k // 2 + 1))
            wait(act, slot_done, g - 1)
            nc.scalar.activation(WH[k % 2][:, :, :], RAW[k % 2][:, :].rearrange("p (j n) -> p j n", j=SKT),
                                 ACT.Copy).then_inc(wh_ready, 1)

        def dve_split(dve, G, k):
            g = SLOTS * G + k
            wait(dve, wh_ready, g + 1)
            nc.vector.tensor_tensor(WL[k % 2][:, :, :], RAW[k % 2][:, :].rearrange("p (j n) -> p j n", j=SKT),
                                    WH[k % 2][:, :, :].bitcast(F32), ALU.subtract).then_inc(wl_ready, 1)

        def act_group(act, G, evac, steps=None, pre=None, last=False):
            for k in range(SLOTS):
                if k < SLOTS - 1:
                    act_split(act, G, k + 1)
                elif not last:
                    act_split(act, G + 1, 0)
                if k < SLOTS - 1 and steps is not None:
                    steps(k)
            wait(act, slot_done, SLOTS * (G + 1))
            evac()
            if steps is not None:
                steps(3)
                steps(4)
            if pre is not None:
                pre()

        def dve_group(dve, G, evac, steps=None, pre=None, last=False):
            for k in range(SLOTS):
                if k < SLOTS - 1:
                    dve_split(dve, G, k + 1)
                elif not last:
                    dve_split(dve, G + 1, 0)
                if k < SLOTS - 1 and steps is not None:
                    steps(k)
            wait(dve, slot_done, SLOTS * (G + 1))
            evac()
            if steps is not None:
                steps(3)
                steps(4)
            if pre is not None:
                pre()

        def act_refill(act, e, src, G, tiles=range(KT)):
            for kt in tiles:
                wait(act, src_ready, KT * e + kt + 1)
                if kt % SKT == 0:
                    wait(act, slot_done, SLOTS * (G - 1) + kt // SKT + 1)
                nc.scalar.activation(tile(XH, kt), src(kt), ACT.Copy).then_inc(xh_ready, 1)

        def dve_refill(dve, e, src, tiles=range(KT)):
            for kt in tiles:
                wait(dve, xh_ready, KT * e + kt + 1)
                nc.vector.tensor_tensor(tile(XL, kt), src(kt), tile(XH, kt).bitcast(F32),
                                        ALU.subtract).then_inc(xl_ready, 1)

        def evac_act_plain(n0, n1, scale0=1.0):
            def f():
                if scale0 != 1.0:
                    nc.scalar.activation(wk(0), PJ[:, 0, :], ACT.Copy, scale=scale0)
                    nc.scalar.activation(wk(1), PJ[:, 1, :], ACT.Copy).then_inc(evac_a, 1)
                else:
                    nc.scalar.activation(WK[:, n0 * SEQ:n1 * SEQ].rearrange("p (b n) -> p b n", n=SEQ),
                                         PJ[:, n0:n1, :], ACT.Copy).then_inc(evac_a, 1)
            return f

        def evac_dve_plain(n0, n1):
            def f():
                nc.vector.tensor_copy(WK[:, n0 * SEQ:n1 * SEQ].rearrange("p (b n) -> p b n", n=SEQ),
                                      PJ[:, n0:n1, :]).then_inc(evac_d, 1)
            return f

        def transpose_blocks(dst, src, last_sem=None):
            for t in range(TB):
                m = nc.tensor.transpose(dst[:, t * P:(t + 1) * P], src[:, t * P:(t + 1) * P], mat("ident"))
            return m

        def att_pe(pe, h, k):
            if k == 0:
                wait(pe, s("at_sq"), h + 1)
                wait(pe, s("mix_done"), h)
                for j in range(2):
                    nc.tensor.matmul(AB[:, j, :], mat("mean128"), wk(4 + j), start=True, stop=True)
                transpose_blocks(AB[:, 2, :], wk(2)).then_inc(s("at_stat"), 1)
            elif k == 1:
                wait(pe, s("at_qn"), h + 1)
                for j in range(2):
                    m = nc.tensor.matmul(AB[:, j, :], mat("swap128"), wk(j), start=True, stop=True)
                m.then_inc(s("at_swapped"), 1)
            elif k == 2:
                wait(pe, s("at_roped"), h + 1)
                for b in range(TB):
                    m = nc.tensor.matmul(AB[:, b, 0:ROW_W[b]], wk(4)[:, b * P:(b + 1) * P], wk(5)[:, 0:ROW_W[b]],
                                         start=True, stop=True)
                m.then_inc(s("at_scores"), 1)
            elif k == 3:
                wait(pe, s("at_probs"), h + 1)
                for b in range(TB):
                    for kb in range(b + 1):
                        m = nc.tensor.transpose(AB[:, kb, b * P:(b + 1) * P],
                                                WK[:, 10 * SEQ + ROW_O[b] + kb * P:10 * SEQ + ROW_O[b] + (kb + 1) * P],
                                                mat("ident"))
                m.then_inc(s("at_pt_t"), 1)
            else:
                wait(pe, s("at_pt_a"), h + 1)
                wait(pe, s("at_pt_d"), h + 1)
                for kb in range(TB):
                    m = nc.tensor.matmul(AB[:, 0, kb * P:SEQ], wk(9)[:, kb * P:(kb + 1) * P],
                                         wk(13 + kb)[:, kb * P:SEQ], start=kb == 0, stop=kb == TB - 1)
                m.then_inc(s("at_pv"), 1)

        def att_act(act, h, k):
            if k == 0:
                wait(act, s("at_stat"), h + 1)
                nc.scalar.activation(wk(6, 2).rearrange("p (b n) -> p b n", n=SEQ), AB[:, 0:2, :], ACT.Sqrt,
                                     bias=SC[:, 0:1]).then_inc(s("at_sd"), 1)
            elif k == 2:
                wait(act, s("at_masked"), h + 1)
                for b in range(TB):
                    a = WK[:, 10 * SEQ + ROW_O[b]:10 * SEQ + ROW_O[b] + ROW_W[b]]
                    m = nc.scalar.activation(a, a, ACT.Exp, bias=SMALL[:, b:b + 1], scale=ATT_SCALE,
                                             accum_out=SMALL[:, 4 + b:5 + b])
                m.then_inc(s("at_expd"), 1)
            elif k == 3:
                wait(act, s("at_pt_t"), h + 1)
                nc.scalar.activation(wk(13), AB[:, 0, :], ACT.Copy)
                nc.scalar.activation(wk(14)[:, P:SEQ], AB[:, 1, P:SEQ], ACT.Copy).then_inc(s("at_pt_a"), 1)

        def att_act_pre(act, h, G):
            nc.scalar.drain()
            nc.scalar.activation(wk(4, 2), wk(0, 2), ACT.Square).then_inc(s("at_sq"), 1)
            wait(act, evac_d, G + 1)
            wait(act, s("mix_done"), h)
            nc.scalar.activation(wk(8), wk(3), ACT.Silu).then_inc(s("at_gs"), 1)

        def att_dve(dve, h, k):
            if k == 0:
                wait(dve, s("at_stat"), h + 1)
                nc.vector.tensor_copy(wk(9), AB[:, 2, :])
                wait(dve, s("at_sd"), h + 1)
                nc.vector.reciprocal(wk(6, 2), wk(6, 2))
                dve.drain()
                nc.vector.scalar_tensor_tensor(wk(0), wk(0), col("qg"), wk(6), ALU.mult, ALU.mult)
                nc.vector.scalar_tensor_tensor(wk(1), wk(1), col("kg"), wk(7), ALU.mult,
                                               ALU.mult).then_inc(s("at_qn"), 1)
            elif k == 1:
                wait(dve, s("at_swapped"), h + 1)
                for j in range(2):
                    nc.vector.tensor_tensor(wk(6 + j), AB[:, j, :], SIN, ALU.mult)
                    nc.vector.tensor_tensor(wk(j), wk(j), COS, ALU.mult)
                dve.drain()
                nc.vector.tensor_tensor(wk(4, 2), wk(0, 2), wk(6, 2), ALU.add).then_inc(s("at_roped"), 1)
            elif k == 2:
                wait(dve, s("at_scores"), h + 1)
                for b in range(TB):
                    nc.vector.tensor_tensor(WK[:, 10 * SEQ + ROW_O[b]:10 * SEQ + ROW_O[b] + ROW_W[b]],
                                            AB[:, b, 0:ROW_W[b]], MASK[:, ROW_O[b]:ROW_O[b] + ROW_W[b]], ALU.add)
                dve.drain()
                for b in range(TB):
                    nc.vector.reduce_max(SMALL[:, 8 + b:9 + b],
                                         WK[:, 10 * SEQ + ROW_O[b]:10 * SEQ + ROW_O[b] + ROW_W[b]], AX.X)
                dve.drain()
                nc.vector.tensor_scalar(SMALL[:, 0:4], SMALL[:, 8:12], -ATT_SCALE, None,
                                        ALU.mult).then_inc(s("at_masked"), 1)
                wait(dve, s("at_expd"), h + 1)
                nc.vector.reciprocal(SMALL[:, 12:16], SMALL[:, 4:8])
                dve.drain()
                for b in range(TB):
                    a = WK[:, 10 * SEQ + ROW_O[b]:10 * SEQ + ROW_O[b] + ROW_W[b]]
                    m = nc.vector.tensor_scalar(a, a, SMALL[:, 12 + b:13 + b], None, ALU.mult)
                m.then_inc(s("at_probs"), 1)
            elif k == 3:
                wait(dve, s("at_pt_t"), h + 1)
                nc.vector.tensor_copy(wk(15)[:, 2 * P:SEQ], AB[:, 2, 2 * P:SEQ])
                nc.vector.tensor_copy(wk(16)[:, 3 * P:SEQ], AB[:, 3, 3 * P:SEQ]).then_inc(s("at_pt_d"), 1)
            else:
                wait(dve, s("at_pv"), h + 1)
                wait(dve, s("at_gs"), h + 1)
                nc.vector.tensor_tensor(tile(X, h), AB[:, 0, :], wk(8), ALU.mult).then_inc(s("mix_done"), 1)

        ix = lambda n: s("ix_" + n)
        for name in ("sq", "stat", "sd", "qn", "swapped", "roped", "key", "logits", "relu", "acc", "sel"):
            ix(name)

        def kw_pe(pe, k):
            if k == 0:
                wait(pe, ix("sq"), 1)
                nc.tensor.matmul(AB[:, 0, :], mat("mean64"), wk(4), start=True, stop=True)
                transpose_blocks(AB[:, 1, :], wk(1)).then_inc(ix("stat"), 1)
            elif k == 1:
                wait(pe, ix("qn"), 1)
                nc.tensor.matmul(AB[:, 0, :], mat("swap64"), wk(0), start=True,
                                 stop=True).then_inc(ix("swapped"), 1)

        def kw_act(act, k):
            if k == 0:
                wait(act, ix("stat"), 1)
                nc.scalar.activation(wk(6), AB[:, 0, :], ACT.Sqrt, bias=SC[:, 0:1]).then_inc(ix("sd"), 1)

        def kw_act_pre(act):
            nc.scalar.drain()
            nc.scalar.activation(wk(4), wk(0), ACT.Square).then_inc(ix("sq"), 1)

        def kw_dve(dve, k):
            if k == 0:
                wait(dve, ix("stat"), 1)
                nc.vector.tensor_scalar(wk(17), AB[:, 1, :], WI_SCALE, None, ALU.mult)
                wait(dve, ix("sd"), 1)
                nc.vector.reciprocal(wk(6), wk(6))
                dve.drain()
                nc.vector.scalar_tensor_tensor(wk(0), wk(0), col("ikg"), wk(6), ALU.mult,
                                               ALU.mult).then_inc(ix("qn"), 1)
            elif k == 1:
                wait(dve, ix("swapped"), 1)
                nc.vector.tensor_tensor(wk(6), AB[:, 0, :], SINI, ALU.mult)
                nc.vector.tensor_tensor(wk(8), wk(0), COSI, ALU.mult)
                dve.drain()
                nc.vector.tensor_tensor(wk(9), wk(8), wk(6), ALU.add).then_inc(ix("key"), 1)

        def qi_pe(pe, u, k):
            if k == 0:
                wait(pe, evac_a, G_QI + u + 1)
                wait(pe, evac_d, G_QI + u + 1)
                wait(pe, ix("acc"), 32 * u)
                wait(pe, ix("key"), 1)
                for j in range(4):
                    m = nc.tensor.matmul(AB[:, j, :], mat("swap64"), wk(j), start=True, stop=True)
                m.then_inc(ix("swapped"), 1)
            elif k == 1:
                wait(pe, ix("roped"), u + 1)
                n = 0
                for hh in range(8):
                    lo = (hh % 2) * IDX_DIM
                    for b in range(TB):
                        if n >= 4:
                            wait(pe, ix("relu"), 32 * u + n - 3)
                        nc.tensor.matmul(AB[:, n % 4, 0:ROW_W[b]],
                                         WK[lo:lo + IDX_DIM, (hh // 2) * SEQ + b * P:(hh // 2) * SEQ + (b + 1) * P],
                                         WK[lo:lo + IDX_DIM, 9 * SEQ:9 * SEQ + ROW_W[b]],
                                         start=True, stop=True).then_inc(ix("logits"), 1)
                        n += 1

        def qi_act(act, u, k):
            if k == 1:
                for n in range(32):
                    b = n % 4
                    wait(act, ix("logits"), 32 * u + n + 1)
                    wait(act, ix("acc"), 32 * u + n - 1)
                    nc.scalar.activation(wk(13 + n % 2)[:, 0:ROW_W[b]], AB[:, n % 4, 0:ROW_W[b]], ACT.Relu,
                                         scale=IDX_SCALE).then_inc(ix("relu"), 1)

        def qi_dve(dve, u, k):
            if k == 0:
                wait(dve, ix("swapped"), u + 2)
                for j in range(4):
                    nc.vector.tensor_tensor(wk(4 + (j % 4)), AB[:, j, :], SINI, ALU.mult)
                    nc.vector.tensor_tensor(wk(j), wk(j), COSI, ALU.mult)
                dve.drain()
                nc.vector.tensor_tensor(wk(0, 4), wk(0, 4), wk(4, 4), ALU.add).then_inc(ix("roped"), 1)
            elif k == 1:
                for n in range(32):
                    b, hh = n % 4, n // 4
                    acc = WK[:, 10 * SEQ + ROW_O[b]:10 * SEQ + ROW_O[b] + ROW_W[b]]
                    w = wk(17)[:, b * P + 8 * u + hh:b * P + 8 * u + hh + 1]
                    wait(dve, ix("relu"), 32 * u + n + 1)
                    r = wk(13 + n % 2)[:, 0:ROW_W[b]]
                    if u == 0 and hh == 0:
                        nc.vector.tensor_scalar(acc, r, w, None, ALU.mult).then_inc(ix("acc"), 1)
                    else:
                        nc.vector.scalar_tensor_tensor(acc, r, w, acc, ALU.mult, ALU.add).then_inc(ix("acc"), 1)
                    if n % 4 == 3:
                        dve.drain()
            elif k == 2 and u == 1:
                for b in range(TB):
                    nc.vector.memset(WK[0:CH, 10 * SEQ + ROW_O[b] + ROW_W[b] - CH:10 * SEQ + ROW_O[b] + ROW_W[b]],
                                     INADMISSIBLE)
                dve.drain()
                a = WK[:, 10 * SEQ + ROW_O[0]:10 * SEQ + ROW_O[0] + ROW_W[0]]
                nc.vector.tensor_scalar(MASK[:, 0:ROW_W[0]], a, -3.2e38 * 0.9, NEG, ALU.is_lt, ALU.mult)
                for r in range(N_SEL // 8):
                    for b in range(1, TB):
                        a = WK[:, 10 * SEQ + ROW_O[b]:10 * SEQ + ROW_O[b] + ROW_W[b]]
                        nc.vector.max(SMALL[:, 16 + 8 * b:24 + 8 * b], a)
                    dve.drain()
                    for b in range(1, TB):
                        a = WK[:, 10 * SEQ + ROW_O[b]:10 * SEQ + ROW_O[b] + ROW_W[b]]
                        nc.vector.match_replace(a, SMALL[:, 16 + 8 * b:24 + 8 * b], a, TAKEN)
                    dve.drain()
                for b in range(1, TB):
                    a = WK[:, 10 * SEQ + ROW_O[b]:10 * SEQ + ROW_O[b] + ROW_W[b]]
                    nc.vector.tensor_scalar(MASK[:, ROW_O[b]:ROW_O[b] + ROW_W[b]], a, -3.15e38, NEG,
                                            ALU.is_gt, ALU.mult)
                dve.drain()

        hg = lambda n: s("hg_" + n)
        for name in ("sig", "forget", "logf", "sums", "exps", "scaled", "tok", "v", "kl", "prod", "state", "o",
                     "sq", "ms", "sd"):
            hg(name)
        chunked = lambda a: a.rearrange("p (c n) -> p c n", n=CH)
        halves = lambda a, w: a.rearrange("p (c n) -> p c n", n=w)

        def hg_act_pre(act, h, G):
            nc.scalar.drain()
            wait(act, evac_d, G + 1)
            wait(act, s("mix_done"), HEADS + h)
            nc.scalar.activation(wk(4), wk(0), ACT.Silu)
            nc.scalar.activation(wk(5), wk(3), ACT.Silu)
            nc.scalar.activation(wk(6), wk(1), ACT.Sigmoid).then_inc(hg("sig"), 1)
            wait(act, hg("forget"), h + 1)
            nc.scalar.activation(wk(7), wk(6), ACT.Ln).then_inc(hg("logf"), 1)
            wait(act, hg("sums"), h + 1)
            nc.scalar.activation(wk(12), wk(11), ACT.Exp, scale=-1.0)
            nc.scalar.activation(wk(11), wk(11), ACT.Exp)
            nc.scalar.activation(wk(9), wk(9), ACT.Exp)
            nc.scalar.activation(wk(14), wk(14), ACT.Exp)
            nc.scalar.activation(wk(10), wk(10), ACT.Exp)
            nc.scalar.activation(wk(13), wk(8), ACT.Exp)
            nc.scalar.activation(SMALL[:, 16:24], wk(8)[:, CH - 1:SEQ:CH], ACT.Exp).then_inc(hg("exps"), 1)

        def hg_dve_pre(dve, h):
            wait(dve, hg("sig"), h + 1)
            nc.vector.tensor_scalar(wk(6), wk(6), OMLB[:, bass.ds(h, 1)], LB[:, bass.ds(h, 1)], ALU.mult,
                                    ALU.add).then_inc(hg("forget"), 1)
            dve.drain()
            nc.vector.tensor_scalar(wk(1), wk(6), -1.0, 1.0, ALU.mult, ALU.add)
            wait(dve, hg("logf"), h + 1)
            wait(dve, table_in, 16)
            nc.vector.tensor_tensor_scan(wk(8), RESET, wk(7), 0.0, ALU.mult, ALU.add)
            dve.drain()
            b3 = chunked(wk(8))
            for w, t in ((CH, 9), (CH // 2, 14)):
                b4, t4 = halves(wk(8), w), halves(wk(t), w)
                mid = b4[:, :, w // 2 - 1:w // 2].to_broadcast([P, SEQ // w, w // 2])
                nc.vector.tensor_tensor(t4[:, :, 0:w // 2], mid, b4[:, :, 0:w // 2], ALU.subtract)
                nc.vector.tensor_tensor(t4[:, :, w // 2:w], b4[:, :, w // 2:w], mid, ALU.subtract)
            b4 = halves(wk(8), CH // 4)
            nc.vector.tensor_tensor(halves(wk(11), CH // 4), b4,
                                    b4[:, :, CH // 8 - 1:CH // 8].to_broadcast([P, 4 * NCH, CH // 4]), ALU.subtract)
            nc.vector.tensor_tensor(chunked(wk(10)), b3[:, :, CH - 1:CH].to_broadcast([P, NCH, CH]), b3,
                                    ALU.subtract).then_inc(hg("sums"), 1)
            wait(dve, hg("exps"), h + 1)
            nc.vector.tensor_tensor(wk(11), wk(4), wk(11), ALU.mult)
            nc.vector.tensor_tensor(wk(12), wk(1), wk(12), ALU.mult)
            nc.vector.tensor_tensor(wk(10), wk(1), wk(10), ALU.mult)
            for w, t in ((CH, 9), (CH // 2, 14)):
                t4, k4, q4 = halves(wk(t), w), halves(wk(1), w), halves(wk(4), w)
                nc.vector.tensor_tensor(t4[:, :, 0:w // 2], t4[:, :, 0:w // 2], k4[:, :, 0:w // 2], ALU.mult)
                nc.vector.tensor_tensor(t4[:, :, w // 2:w], t4[:, :, w // 2:w], q4[:, :, w // 2:w], ALU.mult)
            nc.vector.tensor_tensor(wk(13), wk(4), wk(13), ALU.mult).then_inc(hg("scaled"), 1)

        blocks = lambda a: a.rearrange("p (t n) -> p t n", n=P)
        level_mask = lambda l: CI[:, l * P:(l + 1) * P].unsqueeze(1).to_broadcast([P, TB, P])
        VP = lambda t: WK[:, 15 * SEQ + 2 * P * t:15 * SEQ + 2 * P * (t + 1)]
        ST = lambda c: WK[:, 6 * SEQ + c * P:6 * SEQ + (c + 1) * P]

        def hg_pe(pe, h, k):
            if k == 0:
                wait(pe, hg("scaled"), h + 1)
                wait(pe, s("mix_done"), HEADS + h)
                transpose_blocks(AB[:, 0, :], wk(2))
                transpose_blocks(AB[:, 1, :], wk(10))
                for bank, z in ((2, 9), (3, 14)):
                    for t in range(TB):
                        ts = slice(t * P, (t + 1) * P)
                        m = nc.tensor.matmul(AB[:, bank, ts], wk(z)[:, ts], wk(z)[:, ts], start=True, stop=True)
                m.then_inc(hg("tok"), 1)
            elif k == 1:
                wait(pe, hg("v"), h + 1)
                wait(pe, hg("kl"), h + 1)
                for t in range(TB):
                    ts = slice(t * P, (t + 1) * P)
                    nc.tensor.matmul(AB[:, 2, ts], wk(12)[:, ts], wk(11)[:, ts], start=True, stop=True)
                for t in range(TB):
                    m = nc.tensor.matmul(AB[:, t // 2, (t % 2) * 2 * P:(t % 2 + 1) * 2 * P],
                                         wk(8)[:, t * P:(t + 1) * P], VP(t), start=True, stop=True)
                m.then_inc(hg("prod"), 1)
            elif k == 2:
                wait(pe, hg("state"), h + 1)
                for t in range(TB):
                    ts = slice(t * P, (t + 1) * P)
                    nc.tensor.matmul(AB[:, 3, ts], wk(17)[:, ts], wk(9)[:, ts], start=True, stop=True)
                    for c in (2 * t, 2 * t + 1):
                        if c:
                            cs = slice(c * CH, (c + 1) * CH)
                            m = nc.tensor.matmul(AB[:, 3, cs], ST(c), wk(13)[:, cs], start=False,
                                                 stop=True, skip_group_check=True)
                m.then_inc(hg("o"), 1)
            elif k == 3:
                wait(pe, hg("sq"), h + 1)
                nc.tensor.matmul(AB[:, 0, :], mat("mean128"), wk(11), start=True, stop=True).then_inc(hg("ms"), 1)

        def hg_act(act, h, k):
            if k == 0:
                wait(act, hg("tok"), h + 1)
                nc.scalar.activation(wk(8), AB[:, 1, :], ACT.Copy).then_inc(hg("kl"), 1)
            elif k == 2:
                wait(act, hg("o"), h + 1)
                nc.scalar.activation(wk(10), AB[:, 3, :], ACT.Copy)
                nc.scalar.activation(wk(11), AB[:, 3, :], ACT.Square).then_inc(hg("sq"), 1)
            elif k == 3:
                wait(act, hg("ms"), h + 1)
                nc.scalar.activation(wk(12), AB[:, 0, :], ACT.Sqrt, bias=SC[:, 0:1]).then_inc(hg("sd"), 1)

        def hg_dve(dve, h, k):
            if k == 0:
                nc.vector.memset(wk(15, 2), 0.0)
                wait(dve, hg("tok"), h + 1)
                nc.vector.tensor_copy(wk(17), AB[:, 0, :])
                nc.vector.memset(wk(9), 0.0)
                dve.drain()
                for bank in (2, 3):
                    nc.vector.copy_predicated(blocks(wk(9)), level_mask(bank - 2), AB[:, bank, :].rearrange(
                        "p (t n) -> p t n", n=P))
                    dve.drain()
                for half in range(2):
                    rows = slice(half * CH, (half + 1) * CH)
                    m = nc.vector.tensor_copy(
                        WK[rows, 15 * SEQ:17 * SEQ].rearrange("p (t c n) -> p t c n", c=2, n=P)[:, :, half, :],
                        AB[rows, 0, :].rearrange("p (t n) -> p t n", n=P))
                m.then_inc(hg("v"), 1)
            elif k == 1:
                wait(dve, hg("prod"), h + 1)
                nc.vector.memset(ST(0), 0.0)
                dve.drain()
                nc.vector.copy_predicated(blocks(wk(9)), level_mask(2), AB[:, 2, :].rearrange(
                    "p (t n) -> p t n", n=P))
                for c in range(NCH - 1):
                    nc.vector.scalar_tensor_tensor(ST(c + 1), ST(c), SMALL[:, 16 + c:17 + c],
                                                   AB[:, c // 4, (c % 4) * P:(c % 4 + 1) * P], ALU.mult, ALU.add)
                    dve.drain()
                nc.vector.drain().then_inc(hg("state"), 1)
            elif k == 3:
                wait(dve, hg("sd"), h + 1)
                nc.vector.reciprocal(wk(12), wk(12))
                dve.drain()
                nc.vector.scalar_tensor_tensor(wk(10), wk(10), col("hg"), wk(12), ALU.mult, ALU.mult)
                dve.drain()
                nc.vector.tensor_tensor(tile(X, HEADS + h), wk(10), wk(5), ALU.mult).then_inc(s("mix_done"), 1)


        SUM, RSTD = TBL[:, 0:SEQ], TBL[:, SEQ:2 * SEQ]
        SQR = [TBL[:, (2 + i) * SEQ:(3 + i) * SEQ] for i in range(2)]
        for name in ("in", "added", "stored", "x1_stored"):
            s("res_" + name)

        def out_act(act, g, n, gate, bank):
            def f():
                wait(act, s("res_added"), g)
                for j in (2, 3):
                    scale = MOD[:, bass.ds(32 + n + j, 1)] if gate else 1.0
                    m = nc.scalar.activation(wk(14 + j), bank[:, j, :], ACT.Copy, scale=scale)
                m.then_inc(evac_a, 1)
            return f

        def out_dve(dve, g, n, kind, bank, G):
            def f():
                if kind != 3:
                    wait(dve, s("res_in"), 16 * g + 16)
                for j in range(4):
                    if j == 2:
                        wait(dve, evac_a, G + 1)
                    y = bank[:, j, :] if j < 2 else wk(14 + j)
                    x = tile(X, n + j)
                    if kind == 1:
                        if j < 2:
                            m = nc.vector.scalar_tensor_tensor(x, y, MOD[:, bass.ds(32 + n + j, 1)], wk(j), ALU.mult,
                                                               ALU.add)
                        else:
                            m = nc.vector.tensor_tensor(x, y, wk(j), ALU.add)
                    else:
                        m = nc.vector.scalar_tensor_tensor(x, x if kind == 3 else wk(j), ALPHA, y, ALU.mult, ALU.add)
                    if j == 1:
                        m.then_inc(evac_d, 1)
                if kind == 1:
                    dve.drain().then_inc(s("res_added"), 1)
                else:
                    dve.drain().then_inc(s("res_added"), 1)
                    for j in range(4):
                        nc.vector.tensor_tensor(SUM, SUM, tile(X, n + j), ALU.add)
                        dve.drain()
            return f

        for name in ("sum", "mean", "xc", "sq", "used", "var", "sd", "scaled", "out"):
            s("ln_" + name)

        def ln_pe(pe, l):
            wait(pe, s("ln_sum"), l + 1)
            nc.tensor.matmul(AB[:, 0, :], mat("mean2048"), SUM, start=True, stop=True).then_inc(s("ln_mean"), 1)
            for kt in range(KT):
                wait(pe, s("ln_sq"), KT * l + kt + 1)
                nc.tensor.matmul(AB[:, 1, :], mat("mean2048"), SQR[kt % 2], start=kt == 0,
                                 stop=kt == KT - 1).then_inc(s("ln_used"), 1)

        def ln_act(act, l):
            for kt in range(KT):
                wait(act, s("ln_xc"), KT * l + kt + 1)
                wait(act, s("ln_used"), KT * l + kt - 1)
                nc.scalar.activation(SQR[kt % 2], tile(X, kt), ACT.Square).then_inc(s("ln_sq"), 1)
            wait(act, s("ln_used"), KT * (l + 1))
            nc.scalar.activation(RSTD, AB[:, 1, :], ACT.Sqrt, bias=SC[:, 1:2]).then_inc(s("ln_sd"), 1)
            for kt in range(KT):
                wait(act, s("ln_scaled"), KT * l + kt + 1)
                nc.scalar.activation(tile(X, kt), tile(X, kt), ACT.Identity, scale=col("ln_g", KT * l + kt),
                                     bias=col("ln_b", KT * l + kt)).then_inc(s("ln_out"), 1)

        def ln_dve(dve, l):
            dve.drain().then_inc(s("ln_sum"), 1)
            wait(dve, s("ln_mean"), l + 1)
            for kt in range(KT):
                nc.vector.tensor_tensor(tile(X, kt), tile(X, kt), AB[:, 0, :],
                                        ALU.subtract).then_inc(s("ln_xc"), 1)
            wait(dve, s("ln_sd"), l + 1)
            nc.vector.reciprocal(RSTD, RSTD)
            dve.drain()
            for kt in range(KT):
                nc.vector.tensor_tensor(tile(X, kt), tile(X, kt), RSTD, ALU.mult).then_inc(s("ln_scaled"), 1)

        sk = lambda n: s("sb_" + n)
        for name in ("gs", "v_t", "v", "zt", "z", "abs", "log", "sp", "later", "arg", "w", "o"):
            sk(name)
        PK = lambda i, kb: WK[:, i * SEQ + COL_O[kb]:i * SEQ + COL_O[kb] + COL_W[kb]]
        BASE = 2 * HEADS

        def sb_act_pre(act, h, G):
            wait(act, evac_d, G + 1)
            wait(act, s("mix_done"), BASE + h)
            nc.scalar.activation(wk(16), wk(3), ACT.Silu).then_inc(sk("gs"), 1)

        def sb_pe(pe, h, k):
            if k == 0:
                wait(pe, s("mix_done"), BASE + h)
                transpose_blocks(AB[:, 0, :], wk(2)).then_inc(sk("v_t"), 1)
            elif k == 1:
                wait(pe, sk("v"), h + 1)
                for kb in range(TB):
                    m = nc.tensor.matmul(AB[:, kb, kb * P:SEQ], wk(1)[:, kb * P:(kb + 1) * P], wk(0)[:, kb * P:SEQ],
                                         start=True, stop=True)
                m.then_inc(sk("zt"), 1)
            elif k == 2:
                wait(pe, sk("sp"), h + 1)
                for kb in range(TB):
                    more = kb < TB - 1
                    m = nc.tensor.matmul(AB[:, kb, kb * P:SEQ], mat("neg_suffix"), PK(10, kb), start=True,
                                         stop=not more)
                    if more:
                        m = nc.tensor.matmul(AB[:, kb, (kb + 1) * P:SEQ], mat("neg_ones"), later_sum(kb),
                                             start=False, stop=True)
                m.then_inc(sk("later"), 1)
            elif k == 3:
                wait(pe, sk("w"), h + 1)
                for kb in range(TB):
                    m = nc.tensor.matmul(AB[:, 0, kb * P:SEQ], wk(15)[:, kb * P:(kb + 1) * P], PK(7, kb),
                                         start=kb == 0, stop=kb == TB - 1)
                m.then_inc(sk("o"), 1)

        def later_sum(kb):
            if kb == 2:
                return PK(10, 3)
            o = 13 * SEQ + (0 if kb == 0 else COL_W[1])
            return WK[:, o:o + COL_W[kb + 1]]

        def sb_act(act, h, k):
            if k == 1:
                wait(act, sk("zt"), h + 1)
                for kb in range(TB):
                    m = nc.scalar.activation(PK(4, kb), AB[:, kb, kb * P:SEQ], ACT.Copy)
                m.then_inc(sk("z"), 1)
                wait(act, sk("abs"), h + 1)
                a = WK[:, 7 * SEQ:7 * SEQ + CAUSAL]
                nc.scalar.activation(a, a, ACT.Exp, scale=-1.0)
                act.drain()
                nc.scalar.activation(a, a, ACT.Ln, bias=SC[:, 3:4]).then_inc(sk("log"), 1)
            elif k == 2:
                wait(act, sk("arg"), h + 1)
                nc.scalar.activation(WK[:, 7 * SEQ:7 * SEQ + CAUSAL], WK[:, 4 * SEQ:4 * SEQ + CAUSAL],
                                     ACT.Exp).then_inc(sk("w"), 1)

        def sb_dve(dve, h, k):
            if k == 0:
                wait(dve, sk("v_t"), h + 1)
                nc.vector.tensor_copy(wk(15), AB[:, 0, :]).then_inc(sk("v"), 1)
            elif k == 1:
                z, a, sp = (WK[:, i * SEQ:i * SEQ + CAUSAL] for i in (4, 7, 10))
                wait(dve, sk("z"), h + 1)
                nc.vector.scalar_tensor_tensor(a, z, -1.0, z, ALU.mult, ALU.max).then_inc(sk("abs"), 1)
                wait(dve, sk("log"), h + 1)
                nc.vector.scalar_tensor_tensor(sp, z, 0.0, a, ALU.max, ALU.add)
                dve.drain()
                for kb in range(TB):
                    d = PK(10, kb)[:, 0:P]
                    nc.vector.tensor_tensor(d, d, mat("later_only"), ALU.mult)
                dve.drain()
                nc.vector.tensor_tensor(later_sum(1)[:, P:2 * P], PK(10, 2)[:, P:2 * P], PK(10, 3), ALU.add)
                nc.vector.tensor_copy(later_sum(1)[:, 0:P], PK(10, 2)[:, 0:P])
                dve.drain()
                nc.vector.tensor_tensor(later_sum(0)[:, P:3 * P], PK(10, 1)[:, P:3 * P], later_sum(1), ALU.add)
                nc.vector.tensor_copy(later_sum(0)[:, 0:P], PK(10, 1)[:, 0:P])
                dve.drain().then_inc(sk("sp"), 1)
            elif k == 2:
                wait(dve, sk("later"), h + 1)
                for kb in range(TB):
                    nc.vector.tensor_tensor(PK(4, kb), PK(4, kb), AB[:, kb, kb * P:SEQ], ALU.add)
                dve.drain()
                for kb in range(TB):
                    d = PK(4, kb)[:, 0:P]
                    nc.vector.tensor_tensor(d, d, mat("later_neg"), ALU.add)
                dve.drain().then_inc(sk("arg"), 1)
            elif k == 3:
                wait(dve, sk("o"), h + 1)
                wait(dve, sk("gs"), h + 1)
                wait(dve, s("res_stored"), 64)
                nc.vector.tensor_tensor(tile(X, h), AB[:, 0, :], wk(16), ALU.mult).then_inc(s("mix_done"), 1)

        pk = lambda n: s("pool_" + n)
        for name in ("gs", "u_t", "u_a", "u_d", "pooled", "copied", "mixed", "w_in"):
            pk(name)
        PBASE = BASE + HEADS

        def pool_act_pre(act, g, G):
            wait(act, evac_d, G + 1)
            wait(act, s("mix_done"), PBASE + g)
            nc.scalar.activation(wk(14, 2), wk(2, 2), ACT.Silu).then_inc(pk("gs"), 1)

        def pool_pe(pe, g, k):
            if k == 0:
                wait(pe, evac_a, G_POOL + 1 + g)
                wait(pe, s("mix_done"), PBASE + g)
                for c in range(2):
                    m = transpose_blocks(AB[:, c, :], wk(c))
                m.then_inc(pk("u_t"), 1)
            elif k == 1:
                wait(pe, band_in, 16)
                wait(pe, pk("u_a"), g + 1)
                wait(pe, pk("u_d"), g + 1)
                for c in range(2):
                    for t in range(TB):
                        w = min(BAND_W, SEQ - t * P)
                        band = BAND[:, bass.ds(g * 2 * BAND_W + (t > 0) * BAND_W, w)]
                        m = nc.tensor.matmul(AB[:, 2 + c, t * P:t * P + w], wk(4 + c)[:, t * P:(t + 1) * P], band,
                                             start=t == 0, stop=True, skip_group_check=True)
                m.then_inc(pk("pooled"), 1)
            elif k == 2:
                wait(pe, pk("copied"), g + 1)
                wait(pe, pk("w_in"), 16 * g + 16)
                for d in range(2):
                    for c in range(2):
                        m = nc.tensor.matmul(AB[:, d, :], WP[:, c * 256 + d * P:c * 256 + (d + 1) * P], wk(6 + c),
                                             start=c == 0, stop=c == 1)
                m.then_inc(pk("mixed"), 1)

        def pool_act(act, g, k):
            if k == 0:
                wait(act, pk("u_t"), g + 1)
                nc.scalar.activation(wk(4), AB[:, 0, :], ACT.Copy).then_inc(pk("u_a"), 1)
            elif k == 1:
                wait(act, pk("pooled"), g + 1)
                nc.scalar.activation(blocks4(wk(6, 2)), AB[:, 2:4, :], ACT.Copy).then_inc(pk("copied"), 1)

        blocks4 = lambda a: a.rearrange("p (b n) -> p b n", n=SEQ)

        def pool_dve(dve, g, k):
            if k == 0:
                wait(dve, pk("u_t"), g + 1)
                nc.vector.tensor_copy(wk(5), AB[:, 1, :]).then_inc(pk("u_d"), 1)
            elif k == 2:
                wait(dve, pk("mixed"), g + 1)
                wait(dve, pk("gs"), g + 1)
                for d in range(2):
                    nc.vector.scalar_tensor_tensor(tile(X, HEADS + 2 * g + d), AB[:, d, :], col("pscale", 2 * g + d),
                                                   wk(14 + d), ALU.mult, ALU.mult)
                dve.drain().then_inc(s("mix_done"), 1)

        def mix_act(act, e, k, G):
            act_refill(act, e, lambda kt: wk(8 + kt % 4), G, range(SKT * k, SKT * (k + 1)))

        def mix_dve(dve, e, k):
            for kt in range(SKT * k, SKT * (k + 1)):
                x, d = tile(X, kt), wk(4 + kt % 4)
                nc.vector.tensor_tensor(d[:, 1:SEQ], x[:, 0:SEQ - 1], x[:, 1:SEQ], ALU.subtract)
                nc.vector.tensor_scalar(d[:, 0:1], x[:, 0:1], -1.0, None, ALU.mult)
                dve.drain()
                nc.vector.scalar_tensor_tensor(wk(8 + kt % 4), d, col("mu", KT * (e - 4) + kt), x, ALU.mult,
                                               ALU.add).then_inc(src_ready, 1)
            dve_refill(dve, e, lambda kt: wk(8 + kt % 4), range(SKT * k, SKT * (k + 1)))

        TW, TA = TBL[:, 4 * SEQ:5 * SEQ], TBL[:, 5 * SEQ:6 * SEQ]
        LORA = 96
        s("rk_stored")

        def rw_act(act, n, bank):
            def f():
                wait(act, s("rk_stored"), 16 * n)
                nc.scalar.activation(blocks4(wk(0, 2)), bank[:, 0:2, :], ACT.Copy).then_inc(evac_a, 1)
            return f

        def rw_dve(dve, n, bank):
            def f():
                wait(dve, s("rk_stored"), 16 * n)
                nc.vector.tensor_copy(blocks4(wk(2, 2)), bank[:, 2:4, :]).then_inc(evac_d, 1)
            return f

        ws = lambda i, n=1: WS[:, i * SEQ:(i + n) * SEQ]
        wc = lambda i, c: WS[:, i * SEQ + c * P:i * SEQ + (c + 1) * P]
        wh = lambda i, f: WS[:, (i + f) * SEQ:(i + f + 1) * SEQ]
        bank = lambda i: PJ[:, i, :] if i < 4 else AB[:, i - 4, :]
        banks = lambda i: PJ[:, i:i + 2, :] if i < 4 else AB[:, i - 4:i - 2, :]
        bc = lambda i, c: bank(i + c // 4)[:, (c % 4) * P:(c % 4 + 1) * P]
        two = lambda a: a.rearrange("p (b n) -> p b n", n=SEQ)
        mats8 = lambda name: mat(name).unsqueeze(1).to_broadcast([P, NCH, P])
        mats4 = lambda name: mat(name).unsqueeze(1).to_broadcast([P, NCH // 2, P])
        by_mat = lambda a: a.rearrange("p (c n) -> p c n", n=P)
        (T_R, T_KEY, T_V, T_G, T_LOGW, T_A, T_B, T_BP, T_EB, T_EBP, T_EN, T_KK, T_NORM, T_K2, T_BONUS, T_RR,
         T_AKK) = range(17)
        T_GS = 19
        T_K, T_D, T_E, T_VT = 20, 22, 24, 26
        T_KT, T_DT, T_ET, T_VV = 28, 30, 32, 34
        T_N, T_L, T_X, T_Y, T_W = 36, (38, 40), 42, 44, 46
        T_KE, T_RD, T_RE, T_REFF, T_R1 = 4, 6, 7, 8, 16
        T_P, T_Q, T_F, T_GG, T_S = 40, 42, 46, 20, 22
        DEC = SMALL[:, 80:88]
        LW2 = TBL[0:LORA, SEQ:SEQ + 2 * P]
        LEVELS = 5
        wv = lambda n: s("wv_" + n)
        for name in ("in", "lora_in", "lora", "sig", "kk", "kksq", "ss", "ssm", "sd", "sums", "exps", "bonus_in",
                     "bonus", "expanded", "silu", "free", "tok", "tok_a", "tok_d", "nt", "am", "bt", "gh", "nt_sb",
                     "lmask", "xy", "bt_sb", "wm", "w_sb", "xym", "r1m", "r1", "pq", "p_sb", "q_sb", "fg", "fgr",
                     "hop", "st", "om", "o", "omean", "oc", "osq", "ovar", "osd", "done", "zero"):
            wv(name)

        def wv_pool(pool, p):
            pool.wait_ge(wv("nt_sb"), p + 1)
            for i in range(LEVELS):
                if i == 0:
                    pool.wait_ge(wv("xy"), 12 * p + 2)
                if i >= 2:
                    pool.wait_ge(wv("wm"), 10 * p + 2 * i - 2)
                nc.gpsimd.tensor_tensor(by_mat(ws(T_L[i % 2], 2)), by_mat(ws(T_N, 2)), mats8(f"lev{i + 2}t"),
                                        ALU.mult).then_inc(wv("lmask"), 1)

        def wv_load(pool, p):
            for m in range(4):
                pool.dma_start(ws(m), rkvg_d[m, bass.ds(p, 1), :, :].rearrange("a p n -> (a p) n")
                               ).then_inc(wv("in"), 16)
            pool.dma_start(LW2.rearrange("p (j n) -> p j n", j=2),
                           lora_d.rearrange("p (j n) -> p j n", j=2)[:, :, bass.ds(p * P, P)]
                           ).then_inc(wv("in"), 16)

        def wv_pe(pe, p):
            pe.wait_ge(wv("in"), 80 * p + 80)
            wait(pe, wv("done"), p)
            nc.tensor.matmul(bank(4), LW2[:, 0:P], TW[0:LORA, :], start=True, stop=True)
            nc.tensor.matmul(bank(5), LW2[:, P:2 * P], TA[0:LORA, :], start=True, stop=True).then_inc(wv("lora"), 1)
            pe.wait_ge(wv("kksq"), p + 1)
            nc.tensor.matmul(bank(6), mat("ones64"), ws(T_NORM), start=True, stop=True).then_inc(wv("ss"), 1)
            pe.wait_ge(wv("bonus_in"), p + 1)
            nc.tensor.matmul(bank(7), mat("ones64"), ws(T_BONUS), start=True, stop=True).then_inc(wv("bonus"), 1)
            pe.wait_ge(wv("expanded"), p + 1)
            for n, (src, b) in enumerate(((T_K, 0), (T_D, 2), (T_VT, 4), (T_E, 6))):
                if b == 6:
                    pe.wait_ge(wv("free"), p + 1)
                for c in range(NCH):
                    m = nc.tensor.transpose(bc(b, c), wc(src, c), mat("ident"))
                m.then_inc(wv("tok"), 1)

            def products(b, lhs, rhs, done, width=P):
                for c in range(NCH):
                    o = bc(b, c) if width == P else bank(b)[:, c * width:(c + 1) * width]
                    m = nc.tensor.matmul(o, lhs(c), rhs(c), start=True, stop=True)
                m.then_inc(done, 1)

            pe.wait_ge(wv("tok_a"), 2 * p + 1)
            products(0, lambda c: wc(T_D, c), lambda c: wc(T_K, c), wv("nt"))
            pe.wait_ge(wv("tok_d"), 2 * p + 1)
            products(2, lambda c: wc(T_K, c), lambda c: wc(T_D, c), wv("am"))
            pe.wait_ge(wv("tok_a"), 2 * p + 2)
            products(4, lambda c: wc(T_E, c), lambda c: wc(T_K, c), wv("bt"))
            pe.wait_ge(wv("tok_d"), 2 * p + 2)
            rr = lambda c: ws(T_RR)[:, c * CH:(c + 1) * CH]
            products(6, lambda c: wc(T_D, c), rr, wv("gh"), CH)
            products(7, lambda c: wc(T_E, c), rr, wv("gh"), CH)
            for i in range(LEVELS):
                lvl = T_L[i % 2]
                pe.wait_ge(wv("lmask"), LEVELS * p + i + 1)
                for f in range(2):
                    pe.wait_ge(wv("xy"), 12 * p + 2 + (2 * (i - 1) + f + 1 if i else 0))
                    for c in range(4 * f, 4 * f + 4):
                        m = nc.tensor.matmul(bc(0, c), wc(lvl, c), wc(T_X, c), start=True, stop=True)
                    m.then_inc(wv("wm"), 1)
                if i == 0:
                    pe.wait_ge(wv("bt_sb"), p + 1)
                    products(6, lambda c: wc(T_KE, c), lambda c: wc(T_VV, c), wv("r1m"))
                for f in range(2):
                    pe.wait_ge(wv("w_sb"), 10 * p + 2 * i + f + 1)
                    for c in range(4 * f, 4 * f + 4):
                        if i < LEVELS - 1:
                            nc.tensor.matmul(bc(2, c), wc(T_Y, c), wc(T_W, c), start=True, stop=True)
                        m = nc.tensor.matmul(bc(4, c), wc(T_W, c), wc(T_Y, c), start=True, stop=True)
                    m.then_inc(wv("xym"), 1)
            pe.wait_ge(wv("xy"), 12 * p + 12)
            pe.wait_ge(wv("r1"), p + 1)
            products(2, lambda c: wc(T_Y, c), lambda c: wc(T_KT, c), wv("pq"))
            products(4, lambda c: wc(T_Y, c), lambda c: wc(T_R1, c), wv("pq"))
            pe.wait_ge(wv("p_sb"), p + 1)
            products(0, lambda c: wc(T_P, c), lambda c: wc(T_DT, c), wv("fg"))
            products(2, lambda c: wc(T_P, c), lambda c: ws(T_RD)[:, c * CH:(c + 1) * CH], wv("fg"), CH)
            pe.wait_ge(wv("q_sb"), p + 1)
            for c in range(NCH):
                nc.tensor.matmul(bc(6, c), wc(T_ET, c), wc(T_VV, c), start=True, stop=False)
                m = nc.tensor.matmul(bc(6, c), wc(T_DT, c), wc(T_Q, c), start=False, stop=True)
            m.then_inc(wv("fg"), 1)
            O = lambda c: bank(3)[:, c * CH:(c + 1) * CH]
            for c in range(NCH):
                cs = slice(c * CH, (c + 1) * CH)
                nc.tensor.matmul(O(c), wc(T_Q, c), ws(T_RD)[:, cs], start=c == 0, stop=True, skip_group_check=True)
                nc.tensor.matmul(O(c), wc(T_VV, c), ws(T_RE)[:, cs], start=False, stop=True, skip_group_check=True)
            pe.wait_ge(wv("fgr"), p + 1)
            for c in range(1, NCH):
                if c > 1:
                    pe.wait_ge(wv("st"), 6 * p + c - 1)
                if c < NCH - 1:
                    nc.tensor.matmul(bank(c % 2)[:, 0:P], wc(T_F, c), state(c), start=True,
                                     stop=True).then_inc(wv("hop"), 1)
                m = nc.tensor.matmul(O(c), state(c), ws(T_REFF)[:, c * CH:(c + 1) * CH], start=False, stop=True,
                                     skip_group_check=True)
            m.then_inc(wv("om"), 1)
            pe.wait_ge(wv("o"), p + 1)
            nc.tensor.matmul(bank(4), mat("mean64"), ws(T_EBP), start=True, stop=True).then_inc(wv("omean"), 1)
            pe.wait_ge(wv("osq"), p + 1)
            nc.tensor.matmul(bank(5), mat("mean64"), ws(T_EN), start=True, stop=True).then_inc(wv("ovar"), 1)

        def state(c):
            return wc(T_GG, 0) if c == 1 else wc(T_S, c)

        def wv_act(act, p):
            act.wait_ge(wv("kk"), p + 1)
            nc.scalar.activation(ws(T_NORM), ws(T_KK), ACT.Square).then_inc(wv("kksq"), 1)
            nc.scalar.activation(ws(T_GS), ws(T_G), ACT.Silu).then_inc(wv("silu"), 1)
            act.wait_ge(wv("lora"), p + 1)
            nc.scalar.activation(ws(T_LOGW), bank(4), ACT.Sigmoid, bias=col("w0", p))
            nc.scalar.activation(ws(T_A), bank(5), ACT.Sigmoid, bias=col("a0", p)).then_inc(wv("sig"), 1)
            act.wait_ge(wv("ssm"), p + 1)
            nc.scalar.activation(ws(T_NORM), ws(T_NORM), ACT.Sqrt).then_inc(wv("sd"), 1)
            act.wait_ge(wv("sums"), p + 1)
            nc.scalar.activation(ws(T_EB), ws(T_B), ACT.Exp)
            nc.scalar.activation(ws(T_EBP), ws(T_BP), ACT.Exp)
            nc.scalar.activation(ws(T_EN), ws(T_B), ACT.Exp, scale=-1.0)
            nc.scalar.activation(DEC, ws(T_B)[:, CH - 1:SEQ:CH], ACT.Exp).then_inc(wv("exps"), 1)
            act.wait_ge(wv("tok"), 4 * p + 1)
            nc.scalar.activation(two(ws(T_KT, 2)), banks(0), ACT.Copy).then_inc(wv("tok_a"), 1)
            act.wait_ge(wv("tok"), 4 * p + 3)
            nc.scalar.activation(two(ws(T_VV, 2)), banks(4), ACT.Copy).then_inc(wv("tok_a"), 1)
            act.wait_ge(wv("nt"), p + 1)
            nc.scalar.activation(two(ws(T_N, 2)), banks(0), ACT.Copy).then_inc(wv("nt_sb"), 1)
            for i in range(LEVELS):
                for f in range(2):
                    act.wait_ge(wv("wm"), 10 * p + 2 * i + f + 1)
                    nc.scalar.activation(wh(T_W, f), bank(f), ACT.Copy).then_inc(wv("w_sb"), 1)
                if i == 0:
                    act.wait_ge(wv("r1m"), p + 1)
                    nc.scalar.activation(two(ws(T_R1, 2)), banks(6), ACT.Copy).then_inc(wv("r1"), 1)
            act.wait_ge(wv("pq"), 2 * p + 1)
            nc.scalar.activation(two(ws(T_P, 2)), banks(2), ACT.Copy).then_inc(wv("p_sb"), 1)
            act.wait_ge(wv("om"), p + 1)
            nc.scalar.activation(ws(T_EBP), bank(3), ACT.Copy).then_inc(wv("o"), 1)
            act.wait_ge(wv("oc"), p + 1)
            nc.scalar.activation(ws(T_EN), ws(T_EBP), ACT.Square).then_inc(wv("osq"), 1)
            act.wait_ge(wv("ovar"), p + 1)
            nc.scalar.activation(ws(T_NORM), bank(5), ACT.Sqrt, bias=SC[:, 2:3]).then_inc(wv("osd"), 1)

        def wv_dve(dve, p):
            V, STT = nc.vector.tensor_tensor, nc.vector.scalar_tensor_tensor
            dve.wait_ge(wv("in"), 80 * p + 80)
            nc.vector.tensor_scalar(ws(T_KK), ws(T_KEY), col("k_k", p), None, ALU.mult).then_inc(wv("kk"), 1)
            dve.wait_ge(wv("sig"), p + 1)
            nc.vector.tensor_scalar(ws(T_LOGW), ws(T_LOGW), -math.exp(-0.5), None, ALU.mult)
            nc.vector.tensor_scalar(ws(T_K2), ws(T_A), 1.0, col("k_a", p), ALU.subtract, ALU.mult)
            dve.drain()
            nc.vector.tensor_tensor_scan(ws(T_B), RSET, ws(T_LOGW), 0.0, ALU.mult, ALU.add)
            STT(ws(T_K2), ws(T_K2), 1.0, ws(T_KEY), ALU.add, ALU.mult)
            dve.drain()
            V(ws(T_BP), ws(T_B), ws(T_LOGW), ALU.subtract).then_inc(wv("sums"), 1)
            STT(ws(T_BONUS), ws(T_R), col("r_k", p), ws(T_K2), ALU.mult, ALU.mult).then_inc(wv("bonus_in"), 1)
            dve.wait_ge(wv("ss"), p + 1)
            nc.vector.tensor_scalar(ws(T_NORM), bank(6), L2_EPS ** 2, None, ALU.max).then_inc(wv("ssm"), 1)
            dve.wait_ge(wv("sd"), p + 1)
            nc.vector.reciprocal(ws(T_NORM), ws(T_NORM))
            dve.drain()
            V(ws(T_KK), ws(T_KK), ws(T_NORM), ALU.mult)
            dve.drain()
            V(ws(T_AKK), ws(T_KK), ws(T_A), ALU.mult)
            dve.wait_ge(wv("exps"), p + 1)
            V(ws(T_RR), ws(T_R), ws(T_EB), ALU.mult)
            dve.drain()
            for f in range(2):
                rows = slice(f * CH, (f + 1) * CH)
                h = lambda i: WS[rows, i * SEQ:(i + 1) * SEQ].rearrange("p (c n) -> p c n", n=CH)
                d = lambda i: WS[rows, i * SEQ:(i + 2) * SEQ].rearrange("p (c n) -> p c n", n=P)[
                    :, :, f * CH:(f + 1) * CH]
                V(d(T_K), h(T_KK), h(T_EBP), ALU.mult)
                V(d(T_D), h(T_AKK), h(T_EN), ALU.mult)
                V(d(T_E), h(T_K2), h(T_EN), ALU.mult)
                m = nc.vector.tensor_copy(d(T_VT), h(T_V))
            m.then_inc(wv("expanded"), 1)
            dve.wait_ge(wv("bonus"), p + 1)
            V(ws(T_BONUS), bank(7), ws(T_V), ALU.mult).then_inc(wv("free"), 1)
            dve.wait_ge(wv("tok"), 4 * p + 2)
            nc.vector.tensor_copy(two(ws(T_DT, 2)), banks(2)).then_inc(wv("tok_d"), 1)
            dve.wait_ge(wv("tok"), 4 * p + 4)
            nc.vector.tensor_copy(two(ws(T_ET, 2)), banks(6)).then_inc(wv("tok_d"), 1)
            bm = lambda i: banks(i).rearrange("p b (c n) -> p (b c) n", n=P)
            dve.wait_ge(wv("am"), p + 1)
            V(by_mat(ws(T_W, 2)), bm(2), mats8("lev1"), ALU.mult)
            dve.drain()
            V(by_mat(ws(T_X, 2)), mats8("ident"), by_mat(ws(T_W, 2)), ALU.subtract)
            dve.wait_ge(wv("nt_sb"), p + 1)
            V(by_mat(ws(T_Y, 2)), by_mat(ws(T_N, 2)), mats8("lev1t"), ALU.mult)
            dve.drain()
            V(by_mat(ws(T_Y, 2)), mats8("ident"), by_mat(ws(T_Y, 2)), ALU.subtract).then_inc(wv("xy"), 2)
            dve.wait_ge(wv("bt"), p + 1)
            V(by_mat(ws(T_KE, 2)), bm(4), mats8("strict64"), ALU.mult)
            dve.wait_ge(wv("gh"), 2 * p + 2)
            incl = mat("incl_each")[:, 0:CH].unsqueeze(1).to_broadcast([P, NCH, CH])
            V(chunked(ws(T_RD)), chunked(bank(6)), incl, ALU.mult)
            V(chunked(ws(T_RE)), chunked(bank(7)), incl, ALU.mult)
            dve.drain().then_inc(wv("bt_sb"), 1)
            for i in range(LEVELS):
                for f in range(2):
                    dve.wait_ge(wv("xym"), 10 * p + 2 * i + f + 1)
                    if i < LEVELS - 1:
                        V(wh(T_X, f), wh(T_X, f), bank(2 + f), ALU.subtract)
                    V(wh(T_Y, f), wh(T_Y, f), bank(4 + f), ALU.subtract).then_inc(wv("xy"), 1)
            dve.wait_ge(wv("pq"), 2 * p + 2)
            nc.vector.tensor_scalar(two(ws(T_Q, 2)), banks(4), -1.0, None, ALU.mult).then_inc(wv("q_sb"), 1)
            dve.wait_ge(wv("fg"), 3 * p + 1)
            V(by_mat(ws(T_F, 2)), mats8("ident"), bm(0), ALU.subtract)
            dve.wait_ge(wv("fg"), 3 * p + 2)
            V(ws(T_REFF), ws(T_RR), bank(2), ALU.subtract)
            dve.wait_ge(wv("fg"), 3 * p + 3)
            V(by_mat(ws(T_GG, 2)), bm(6), DEC.unsqueeze(2).to_broadcast([P, NCH, P]), ALU.mult)
            dve.drain().then_inc(wv("fgr"), 1)
            for c in range(1, NCH - 1):
                dve.wait_ge(wv("hop"), 6 * p + c)
                STT(wc(T_S, c + 1), bank(c % 2)[:, 0:P], DEC[:, c:c + 1], wc(T_GG, c), ALU.mult,
                    ALU.add).then_inc(wv("st"), 1)
            dve.wait_ge(wv("omean"), p + 1)
            V(ws(T_EBP), ws(T_EBP), bank(4), ALU.subtract).then_inc(wv("oc"), 1)
            dve.wait_ge(wv("osd"), p + 1)
            nc.vector.reciprocal(ws(T_NORM), ws(T_NORM))
            dve.drain()
            STT(ws(T_EBP), ws(T_EBP), col("gn_w", p), ws(T_NORM), ALU.mult, ALU.mult)
            dve.drain()
            STT(ws(T_EBP), ws(T_EBP), col("gn_b", p), ws(T_BONUS), ALU.add, ALU.add)
            dve.drain()
            V(tile(WK, p), ws(T_EBP), ws(T_GS), ALU.mult).then_inc(wv("done"), 1)

        RSET = TBL[:, 0:SEQ]
        s("reset_in")
        s("out_stored")

        @block.sync
        def _(sp):
            sp.dma_start(COL[:, :], cols_d).then_inc(consts_in, 16)
            sp.dma_start(MAT[:, :], mats_d).then_inc(consts_in, 16)
            sp.dma_start(CI[:, :], causal_i_d).then_inc(consts_in, 16)
            sp.dma_start(MASK.bitcast(I32)[:, 0:SEQ], positions).then_inc(consts_in, 16)
            for q in range(4):
                sp.dma_start(X[:, q * 4 * SEQ:(q + 1) * 4 * SEQ].rearrange("p (k n) -> p k n", n=SEQ),
                             xT.rearrange("(k p) n -> p k n", p=P)[:, q * 4:(q + 1) * 4, :]).then_inc(x_in, 16)

            def ada_load(cg, k):
                wait(sp, ada_used, SLOTS * (cg - 1) + k + 1)
                sp.dma_start(WK[:, k * 4 * SEQ:(k + 1) * 4 * SEQ], ada_d[cg, k]).then_inc(ada_in[k], 16)

            for k in range(SLOTS):
                sp.dma_start(WK[:, k * 4 * SEQ:(k + 1) * 4 * SEQ], ada_d[0, k]).then_inc(ada_in[k], 16)
            with sp.Fori(1, ADA_GROUPS) as cg:
                for k in range(SLOTS):
                    ada_load(cg, k)

            for k in range(SLOTS):
                wait(sp, wl_ready, k - 1)
                sp.dma_start(RAW[k % 2][:, :], w_d[0, k]).then_inc(raw_in[k % 2], 16)
            with sp.Fori(1, GROUPS) as G:
                for k in range(SLOTS):
                    sp.wait_ge(wl_ready, SLOTS * G + (k - 1))
                    sp.dma_start(RAW[k % 2][:, :], w_d[bass.ds(G, 1), k, :, :].rearrange("a p n -> (a p) n")
                                 ).then_inc(raw_in[k % 2], 16)
            for kt in range(KT):
                sp.wait_ge(s("ln_out"), KT + kt + 1)
                sp.dma_start(out[kt], tile(X, kt)).then_inc(s("out_stored"), 16)
            sp.wait_ge(s("out_stored"), 16 * KT)

        @block.gpsimd
        def _(pool):
            pool.wait_ge(ix("roped"), 2)
            pool.dma_start(RESET, rows_d[:, 0:SEQ]).then_inc(table_in, 16)
            pool.wait_ge(s("mix_done"), HEADS)
            pool.dma_start(BAND, band_d).then_inc(band_in, 16)
            pool.wait_ge(s("mix_done"), 2 * HEADS)
            for g in range(4):
                wait(pool, s("res_added"), g)
                src = xT.rearrange("(k p) n -> p k n", p=P)
                pool.dma_start(blocks4(wk(0, 4)), src[:, 4 * g:4 * g + 4, :]).then_inc(s("res_in"), 16)
                pool.wait_ge(s("res_added"), g + 1)
                pool.dma_start(x1_d[4 * g:4 * g + 4].rearrange("k p n -> p k n"),
                               blocks4(X[:, 4 * g * SEQ:4 * (g + 1) * SEQ])).then_inc(s("res_stored"), 16)
            for g in range(4):
                pool.wait_ge(s("mix_done"), PBASE if g == 0 else PBASE + g)
                pool.dma_start(WP, wpool_d[g]).then_inc(pk("w_in"), 16)
            pool.wait_ge(s("mix_done"), PBASE + 4)
            pool.wait_ge(s("res_stored"), 64)
            for g in range(4):
                wait(pool, s("res_added"), 4 + g)
                pool.dma_start(blocks4(wk(0, 4)), x1_d[4 * g:4 * g + 4].rearrange("k p n -> p k n")
                               ).then_inc(s("res_in"), 16)
            for n in range(16):
                m, g = n // 4, n % 4
                pool.wait_ge(evac_a, G_RW + n + 1)
                pool.wait_ge(evac_d, G_RW + n + 1)
                pool.dma_start(rkvg_d[m, 4 * g:4 * g + 4].rearrange("k p n -> p k n"),
                               blocks4(wk(0, 4))).then_inc(s("rk_stored"), 16)
            pool.wait_ge(s("rk_stored"), 256)
            pool.wait_ge(wl_ready, SLOTS * G_OUT3)
            pool.wait_ge(slot_done, SLOTS * G_OUT3)
            pool.dma_start(RSET, rows_d[:, 0:SEQ]).then_inc(s("reset_in"), 16)
            wv_load(pool, 0)
            nc.gpsimd.memset(ws(T_K, 8), 0.0).then_inc(wv("zero"), 1)
            with pool.Fori(0, PAIRS - 1) as p:
                pool.wait_ge(wv("free"), p + 1)
                pool.wait_ge(wv("silu"), p + 1)
                pool.wait_ge(wv("lora"), p + 1)
                wv_load(pool, p + 1)
                wv_pool(pool, p)
            wv_pool(pool, PAIRS - 1)

        @block.tensor
        def _(pe):
            pe.wait_ge(consts_in, 64)
            for kt in range(KT):
                pe.wait_ge(x_sq, kt + 1)
                m = nc.tensor.matmul(AB[:, 0, :], mat("mean2048"), wk(16 + kt % 2), start=kt == 0,
                                     stop=kt == KT - 1)
                m.then_inc(x_sq_used, 1)
            pe.wait_ge(silu_c, 1)
            with pe.Fori(0, ADA_GROUPS) as cg:
                for k in range(SLOTS):
                    pe.wait_ge(ada_in[k], 16 * cg + 16)
                    for n in range(4):
                        for j in range(SKT):
                            at = k * 4 * SEQ + j * GC + n * P
                            m = nc.tensor.matmul(AB[:, 1, bass.ds(4 * cg + n, 1)], WK[:, at:at + P],
                                                 SMALL[:, 32 + SKT * k + j:33 + SKT * k + j],
                                                 start=k == 0 and j == 0 and n == 0, stop=k == 3 and j == 3,
                                                 skip_group_check=True)
                    m.then_inc(ada_used, 1)

            pe_group(pe, G_KW, refill=0, tiles=2)
            pe_group(pe, G_QI, steps=lambda k: kw_pe(pe, k))
            pe_group(pe, G_QI + 1, steps=lambda k: qi_pe(pe, 0, k))
            pe_group(pe, G_ATT, steps=lambda k: qi_pe(pe, 1, k))
            with pe.Fori(1, HEADS) as h:
                pe_group(pe, G_ATT + h, steps=lambda k: att_pe(pe, h - 1, k))
            pe_group(pe, G_HG, steps=lambda k: att_pe(pe, HEADS - 1, k))
            with pe.Fori(1, HEADS) as h:
                pe_group(pe, G_HG + h, steps=lambda k: hg_pe(pe, h - 1, k))
            for k in range(5):
                hg_pe(pe, HEADS - 1, k)

            def pe_out(G0, refill):
                pe_group(pe, G0, refill=refill, bank=PJ, ago=1)
                pe_group(pe, G0 + 1, bank=AB, ago=1)
                with pe.Fori(1, 2) as i:
                    pe_group(pe, G0 + 2 * i, bank=PJ, ago=1)
                    pe_group(pe, G0 + 2 * i + 1, bank=AB, ago=1)

            pe_out(G_OUT1, 1)
            pe_group(pe, G_EVA, refill=2)
            with pe.Fori(1, HEADS) as h:
                pe_group(pe, G_EVA + h, steps=lambda k: sb_pe(pe, h - 1, k))
            pe_group(pe, G_POOL, steps=lambda k: sb_pe(pe, HEADS - 1, k))
            with pe.Fori(1, 4) as g:
                pe_group(pe, G_POOL + g, steps=lambda k: pool_pe(pe, g - 1, k))
            for k in range(5):
                pool_pe(pe, 3, k)
            pe_out(G_OUT2, 3)
            ln_pe(pe, 0)
            pe_group(pe, G_LORA, refill=4, tiles=1)
            pe_group(pe, G_LORA + 1, refill=5, tiles=1, bank=AB, ago=1)
            with pe.Fori(0, 4) as m:
                for g in range(4):
                    pe_group(pe, G_RW + 4 * m + g, refill=6 + m if g == 0 else None, bank=(PJ, AB)[g % 2], ago=1)
            pe.wait_ge(evac_a, G_OUT3)
            pe.wait_ge(evac_d, G_OUT3)
            with pe.Fori(0, PAIRS) as p:
                wv_pe(pe, p)
            pe_out(G_OUT3, 10)
            ln_pe(pe, 1)

        @block.scalar
        def _(act):
            act.wait_ge(consts_in, 64)
            nc.scalar.activation(SMALL[:, 32:48], COL[:, COLS["c"]:COLS["c"] + KT], ACT.Silu).then_inc(silu_c, 1)
            for kt in range(KT):
                if kt % 4 == 0:
                    act.wait_ge(x_in, 64)
                wait(act, x_sq_used, kt - 1)
                nc.scalar.activation(wk(16 + kt % 2), tile(X, kt), ACT.Square).then_inc(x_sq, 1)
            act.wait_ge(angles, 1)
            for j, t in enumerate((COS, SIN, COSI, SINI)):
                nc.scalar.activation(t, t, ACT.Sin)
            nc.scalar.drain().then_inc(angles, 1)
            act.wait_ge(x_sq_used, KT)
            nc.scalar.activation(wk(16), AB[:, 0, :], ACT.Sqrt, bias=SC[:, 0:1]).then_inc(x_sd, 1)
            nc.scalar.activation(SMALL[:, 64:80], COL[:, COLS["lb0"]:COLS["lb0"] + 16], ACT.Exp)
            nc.scalar.drain().then_inc(mod_done, 1)
            act_split(act, 0, 0)
            act_refill(act, 0, lambda kt: tile(X, kt), 0)
            act_group(act, G_KW, evac_act_plain(0, 1), pre=lambda: kw_act_pre(act))
            act_group(act, G_QI, evac_act_plain(0, 2), steps=lambda k: kw_act(act, k))
            act_group(act, G_QI + 1, evac_act_plain(0, 2), steps=lambda k: qi_act(act, 0, k))
            act_group(act, G_ATT, evac_act_plain(0, 2), steps=lambda k: qi_act(act, 1, k),
                      pre=lambda: att_act_pre(act, 0, G_ATT))
            with act.Fori(1, HEADS) as h:
                act_group(act, G_ATT + h, evac_act_plain(0, 2), steps=lambda k: att_act(act, h - 1, k),
                          pre=lambda: att_act_pre(act, h, G_ATT + h))
            act_group(act, G_HG, evac_act_plain(0, 2), steps=lambda k: att_act(act, HEADS - 1, k),
                      pre=lambda: hg_act_pre(act, 0, G_HG))
            with act.Fori(1, HEADS) as h:
                act_group(act, G_HG + h, evac_act_plain(0, 2), steps=lambda k: hg_act(act, h - 1, k),
                          pre=lambda: hg_act_pre(act, h, G_HG + h))
            for k in range(5):
                hg_act(act, HEADS - 1, k)

            def act_out(G0, done, gate):
                with act.Fori(0, 2) as i:
                    for j, bank in enumerate((PJ, AB)):
                        act_group(act, G0 + 2 * i + j, out_act(act, done + 2 * i + j, 8 * i + 4 * j, gate, bank))

            act_refill(act, 1, lambda kt: tile(X, kt), G_OUT1)
            act_out(G_OUT1, 0, True)
            act_refill(act, 2, lambda kt: tile(X, kt), G_EVA)
            act_group(act, G_EVA, evac_act_plain(0, 2, ATT_SCALE), pre=lambda: sb_act_pre(act, 0, G_EVA))
            with act.Fori(1, HEADS) as h:
                act_group(act, G_EVA + h, evac_act_plain(0, 2, ATT_SCALE), steps=lambda k: sb_act(act, h - 1, k),
                          pre=lambda: sb_act_pre(act, h, G_EVA + h))
            act_group(act, G_POOL, evac_act_plain(0, 2), steps=lambda k: sb_act(act, HEADS - 1, k),
                      pre=lambda: pool_act_pre(act, 0, G_POOL))
            with act.Fori(1, 4) as g:
                act_group(act, G_POOL + g, evac_act_plain(0, 2), steps=lambda k: pool_act(act, g - 1, k),
                          pre=lambda: pool_act_pre(act, g, G_POOL + g))
            for k in range(5):
                pool_act(act, 3, k)
            act_refill(act, 3, lambda kt: tile(X, kt), G_OUT2)
            act_out(G_OUT2, 4, False)
            ln_act(act, 0)
            for k in range(SLOTS):
                mix_act(act, 4, k, G_LORA)
            act_group(act, G_LORA, lambda: nc.scalar.activation(TW, PJ[:, 0, :], ACT.Tanh).then_inc(evac_a, 1),
                      steps=lambda k: k < SLOTS and mix_act(act, 5, k, G_LORA + 1))
            act_group(act, G_LORA + 1, lambda: nc.scalar.drain().then_inc(evac_a, 1),
                      steps=lambda k: k < SLOTS and mix_act(act, 6, k, G_RW))
            with act.Fori(0, 3) as m:
                for g in range(4):
                    act_group(act, G_RW + 4 * m + g, rw_act(act, 4 * m + g, (PJ, AB)[g % 2]),
                              steps=(lambda k: k < SLOTS and mix_act(act, 7 + m, k, G_RW + 4 * m + 4)) if g == 3
                              else None)
            for g in range(4):
                act_group(act, G_RW + 12 + g, rw_act(act, 12 + g, (PJ, AB)[g % 2]), last=g == 3)
            with act.Fori(0, PAIRS) as p:
                wv_act(act, p)
            act.wait_ge(wv("done"), PAIRS)
            act_split(act, G_OUT3, 0)
            act_refill(act, 10, lambda kt: wk(kt), G_OUT3)
            with act.Fori(0, 1) as i:
                for j, b in enumerate((PJ, AB)):
                    act_group(act, G_OUT3 + 2 * i + j, out_act(act, 8 + 2 * i + j, 8 * i + 4 * j, False, b))
            for j, b in enumerate((PJ, AB)):
                act_group(act, G_OUT3 + 2 + j, out_act(act, 10 + j, 8 + 4 * j, False, b), last=j == 1)
            ln_act(act, 1)

        @block.vector
        def _(dve):
            nc.vector.memset(SC[:, 0:1], RMS_EPS)
            nc.vector.memset(SC[:, 1:2], LN_EPS)
            nc.vector.memset(SC[:, 2:3], GN_EPS)
            nc.vector.memset(SC[:, 3:4], 1.0)
            dve.wait_ge(consts_in, 64)
            nc.vector.tensor_copy(MASK[:, SEQ:2 * SEQ], MASK.bitcast(I32)[:, 0:SEQ])
            dve.drain()
            pos, turns = MASK[:, SEQ:2 * SEQ], MASK[:, 0:SEQ]
            for t, f, quarter in ((COS, 0, 0.25), (SIN, 0, 0.0), (COSI, 1, 0.25), (SINI, 1, 0.0)):
                nc.vector.tensor_scalar(t, pos, col("freq", f), None, ALU.mult)
                dve.drain()
                nc.vector.tensor_scalar(turns, t, 1.0 / (2 * math.pi), quarter, ALU.mult, ALU.add)
                dve.drain()
                nc.vector.tensor_scalar(turns, turns, 12582912.0, None, ALU.add)
                dve.drain()
                nc.vector.tensor_scalar(turns, turns, 12582912.0, None, ALU.subtract)
                dve.drain()
                for part in TWO_PI:
                    nc.vector.scalar_tensor_tensor(t, turns, -part, t, ALU.mult, ALU.add)
                    dve.drain()
                if quarter:
                    nc.vector.tensor_scalar(t, t, math.pi / 2, None, ALU.add)
                    dve.drain()
                nc.vector.tensor_scalar(t, t, PI_IN, -PI_IN, ALU.min, ALU.max)
            nc.vector.drain().then_inc(angles, 1)
            dve.wait_ge(x_sd, 1)
            nc.vector.reciprocal(wk(16), wk(16))
            dve.drain()
            for kt in range(KT):
                nc.vector.tensor_tensor(tile(X, kt), tile(X, kt), wk(16), ALU.mult)
            nc.vector.drain().then_inc(x_sd, 1)
            dve.wait_ge(mod_done, 1)
            nc.vector.tensor_tensor(LB[:, :], SMALL[:, 64:72], SMALL[:, 72:80], ALU.add)
            dve.drain()
            nc.vector.reciprocal(LB[:, :], LB[:, :])
            dve.drain()
            nc.vector.tensor_tensor(LB[:, :], LB[:, :], SMALL[:, 64:72], ALU.mult)
            dve.drain()
            nc.vector.tensor_scalar(OMLB[:, :], LB[:, :], -1.0, 1.0, ALU.mult, ALU.add)
            dve.wait_ge(ada_used, SLOTS * ADA_GROUPS)
            nc.vector.tensor_tensor(MOD[:, :], AB[:, 1, 0:48], COL[:, COLS["ada_b"]:COLS["ada_b"] + 48], ALU.add)
            dve.drain()
            nc.vector.scalar_tensor_tensor(MOD[:, 16:32], MOD[:, 16:32], 1.0,
                                           COL[:, COLS["norm_g"]:COLS["norm_g"] + 16], ALU.add, ALU.mult)
            dve.drain()
            for kt in range(KT):
                nc.vector.tensor_scalar(tile(X, kt), tile(X, kt), MOD[:, 16 + kt:17 + kt], MOD[:, kt:kt + 1],
                                        ALU.mult, ALU.add).then_inc(src_ready, 1)
            dve_split(dve, 0, 0)
            dve_refill(dve, 0, lambda kt: tile(X, kt))
            dve_group(dve, G_KW, evac_dve_plain(1, 2))
            dve_group(dve, G_QI, evac_dve_plain(2, 4), steps=lambda k: kw_dve(dve, k))
            dve_group(dve, G_QI + 1, evac_dve_plain(2, 4), steps=lambda k: qi_dve(dve, 0, k))
            dve_group(dve, G_ATT, evac_dve_plain(2, 4), steps=lambda k: qi_dve(dve, 1, k))
            with dve.Fori(1, HEADS) as h:
                dve_group(dve, G_ATT + h, evac_dve_plain(2, 4), steps=lambda k: att_dve(dve, h - 1, k))
            dve_group(dve, G_HG, evac_dve_plain(2, 4), steps=lambda k: att_dve(dve, HEADS - 1, k),
                      pre=lambda: hg_dve_pre(dve, 0))
            with dve.Fori(1, HEADS) as h:
                dve_group(dve, G_HG + h, evac_dve_plain(2, 4), steps=lambda k: hg_dve(dve, h - 1, k),
                          pre=lambda: hg_dve_pre(dve, h))
            for k in range(5):
                hg_dve(dve, HEADS - 1, k)

            def dve_out(G0, done, kind):
                with dve.Fori(0, 2) as i:
                    for j, bank in enumerate((PJ, AB)):
                        G = G0 + 2 * i + j
                        dve_group(dve, G, out_dve(dve, done + 2 * i + j, 8 * i + 4 * j, kind, bank, G))

            dve.drain().then_inc(src_ready, KT)
            dve_refill(dve, 1, lambda kt: tile(X, kt))
            dve_out(G_OUT1, 0, 1)
            dve.drain().then_inc(src_ready, KT)
            dve_refill(dve, 2, lambda kt: tile(X, kt))
            dve_group(dve, G_EVA, evac_dve_plain(2, 4))
            with dve.Fori(1, HEADS) as h:
                dve_group(dve, G_EVA + h, evac_dve_plain(2, 4), steps=lambda k: sb_dve(dve, h - 1, k))
            dve_group(dve, G_POOL, evac_dve_plain(2, 4), steps=lambda k: sb_dve(dve, HEADS - 1, k))
            with dve.Fori(1, 4) as g:
                dve_group(dve, G_POOL + g, evac_dve_plain(2, 4), steps=lambda k: pool_dve(dve, g - 1, k))
            for k in range(5):
                pool_dve(dve, 3, k)
            dve.drain().then_inc(src_ready, KT)
            dve_refill(dve, 3, lambda kt: tile(X, kt))
            nc.vector.memset(SUM, 0.0)
            dve.drain()
            dve_out(G_OUT2, 4, 2)
            ln_dve(dve, 0)
            dve.wait_ge(s("ln_out"), KT)
            for k in range(SLOTS):
                mix_dve(dve, 4, k)
            dve_group(dve, G_LORA, lambda: dve.drain().then_inc(evac_d, 1),
                      steps=lambda k: k < SLOTS and mix_dve(dve, 5, k))
            dve_group(dve, G_LORA + 1, lambda: nc.vector.tensor_copy(TA, AB[:, 0, :]).then_inc(evac_d, 1),
                      steps=lambda k: k < SLOTS and mix_dve(dve, 6, k))
            with dve.Fori(0, 3) as m:
                for g in range(4):
                    dve_group(dve, G_RW + 4 * m + g, rw_dve(dve, 4 * m + g, (PJ, AB)[g % 2]),
                              steps=(lambda k: k < SLOTS and mix_dve(dve, 7 + m, k)) if g == 3 else None)
            for g in range(4):
                dve_group(dve, G_RW + 12 + g, rw_dve(dve, 12 + g, (PJ, AB)[g % 2]), last=g == 3)
            dve.wait_ge(s("reset_in"), 16)
            dve.wait_ge(wv("zero"), 1)
            with dve.Fori(0, PAIRS) as p:
                wv_dve(dve, p)
            nc.vector.memset(SUM, 0.0)
            dve.drain().then_inc(src_ready, KT)
            dve_split(dve, G_OUT3, 0)
            dve_refill(dve, 10, lambda kt: wk(kt))
            with dve.Fori(0, 1) as i:
                for j, b in enumerate((PJ, AB)):
                    G = G_OUT3 + 2 * i + j
                    dve_group(dve, G, out_dve(dve, 8 + 2 * i + j, 8 * i + 4 * j, 3, b, G))
            for j, b in enumerate((PJ, AB)):
                G = G_OUT3 + 2 + j
                dve_group(dve, G, out_dve(dve, 10 + j, 8 + 4 * j, 3, b, G), last=j == 1)
            ln_dve(dve, 1)


def constants():
    i = np.arange(P)
    k, m = i[:, None], i[None, :]
    same64 = (k // 64 == m // 64)
    f = {
        "ident": k == m, "mean128": np.full((P, P), 1 / 128), "mean64": same64 / 64, "ones64": same64 * 1.0,
        "mean2048": np.full((P, P), 1 / D),
        "swap128": np.where(k == m - 64, 1.0, 0) - np.where(k == m + 64, 1.0, 0),
        "swap64": same64 * (np.where(k == m - 32, 1.0, 0) - np.where(k == m + 32, 1.0, 0)),
        "neg_suffix": (k >= m) * -1.0, "neg_ones": -np.ones((P, P)),
        "later_only": (k < m) * 1.0, "later_neg": np.where(k < m, 0.0, NEG),
        "strict64": same64 & (k < m), "incl_each": k % 64 <= m % 64,
    }
    for l in range(1, 7):
        low = (k >> l == m >> l) & ((k >> (l - 1)) % 2 == 1) & ((m >> (l - 1)) % 2 == 0)
        f[f"lev{l}"], f[f"lev{l}t"] = low, low.T
    mats = np.concatenate([f[n].astype(np.float32) for n in MATS], axis=1)
    level = [(k // w == m // w) & (k % w < w // 2) & (m % w >= w // 2) for w in (CH, CH // 2)]
    level.append((k // (CH // 4) == m // (CH // 4)) & (k <= m))
    causal = np.concatenate(level, axis=1).astype(np.int32)
    t = np.arange(SEQ)
    reset = np.broadcast_to((t % CH != 0).astype(np.float32), (P, SEQ))
    band = np.zeros((P, 4, 2, BAND_W), np.float32)
    for g, w in enumerate((2, 4, 8, 16)):
        for first in range(2):
            q = np.arange(BAND_W)[None, :]
            inside = (q >= k) & (q - k < w)
            count = np.minimum(q + 1, w) if first == 0 else w
            band[:, g, first] = inside / count - (q == k)
    freq = np.zeros((P, 2), np.float32)
    for j, half in enumerate((64, 32)):
        inv = (10000.0 ** (-np.arange(half, dtype=np.float32) / np.float32(half)).astype(np.float64)).astype(np.float32)
        freq[:, j] = inv[i % half]
    return mats, causal, np.ascontiguousarray(reset), band.reshape(P, -1), freq


def by_channel(v):
    return np.ascontiguousarray(np.asarray(v).reshape(-1, P).T)


def pack_group(w):
    return w.reshape(SLOTS, SKT, P, GC).transpose(0, 2, 1, 3).reshape(SLOTS, P, SKT * GC)


def pack(x, c, positions, ada_w, ada_b, norm_g, w_in, q_norm_g, k_norm_g, idx_k_norm_g, hgrn_lb_logits,
         hgrn_norm_g, w_out, ev_w_in_2, ev_w_pool_2, ev_pool_scale_2, ev_w_out_2, od_mu_2, od_w_r_2, od_w_k_2,
         od_w_v_2, od_w_g_2, od_w0_2, od_w1_2, od_w2_2, od_a0_2, od_a1_2, od_a2_2, od_k_k_2, od_k_a_2,
         od_r_k_2, od_gn_w_2, od_gn_b_2, od_w_o_2, ln_g_2, ln_b_2):
    mats, causal, reset, band, freq = constants()
    cols = np.concatenate(
        [by_channel(c), by_channel(ada_b), by_channel(norm_g), by_channel(q_norm_g), by_channel(k_norm_g),
         by_channel(np.tile(np.asarray(idx_k_norm_g).reshape(-1), 2)), by_channel(hgrn_lb_logits),
         by_channel(hgrn_norm_g), by_channel(ev_pool_scale_2),
         by_channel(np.asarray(od_mu_2)[0][[1, 4, 0, 2, 3, 5]]), by_channel(od_w0_2),
         by_channel(od_a0_2), by_channel(od_k_k_2), by_channel(od_k_a_2), by_channel(od_r_k_2),
         by_channel(od_gn_w_2), by_channel(od_gn_b_2), by_channel(ln_g_2), by_channel(ln_b_2), freq], axis=1)
    w = np.empty((GROUPS, SLOTS, P, SKT * GC), np.float32)
    w_in, ev, at = np.asarray(w_in)[0], np.asarray(ev_w_in_2)[0], 0

    def put(columns):
        nonlocal at
        w[at] = pack_group(columns)
        at += 1

    def padded(*parts):
        z = np.zeros((D, GC), np.float32)
        for first, a in parts:
            z[:, first:first + a.shape[1]] = a
        return z

    iq = 4 * 1024
    ik, iw, rq = iq + 1024, iq + 1088, iq + 1104
    put(padded((0, w_in[:, ik:iw]), (64, w_in[:, ik:iw]), (128, w_in[:, iw:rq])))
    for g in range(2):
        put(w_in[:, iq + GC * g:iq + GC * (g + 1)])
    for base in (0, rq):
        for h in range(HEADS):
            put(np.concatenate([w_in[:, base + 1024 * i + P * h:base + 1024 * i + P * (h + 1)] for i in range(4)],
                               axis=1))
    for g in range(4):
        put(np.asarray(w_out)[0][:, GC * g:GC * (g + 1)])
    for h in range(HEADS):
        put(np.concatenate([ev[:, 1024 * i + P * h:1024 * i + P * (h + 1)] for i in range(4)], axis=1))
    for g in range(4):
        put(np.concatenate([ev[:, b + 256 * g:b + 256 * (g + 1)] for b in (4096, 5120)], axis=1))
    for g in range(4):
        put(np.asarray(ev_w_out_2)[0][:, GC * g:GC * (g + 1)])
    for m in (od_w1_2, od_a1_2):
        put(padded((0, np.asarray(m)[0])))
    for m in (od_w_r_2, od_w_k_2, od_w_v_2, od_w_g_2, od_w_o_2):
        for g in range(4):
            put(np.asarray(m)[0][:, GC * g:GC * (g + 1)])
    assert at == GROUPS
    ada = np.stack([pack_group(np.asarray(ada_w)[0][:, GC * g:GC * (g + 1)]) for g in range(ADA_GROUPS)])
    lora = np.concatenate([np.asarray(od_w2_2)[0], np.asarray(od_a2_2)[0]], axis=1)
    wpool = np.asarray(ev_w_pool_2)[0].reshape(4, 2, P, 256).transpose(0, 2, 1, 3).reshape(4, P, SEQ)
    return {
        "xT": np.ascontiguousarray(np.asarray(x)[0].T),
        "positions": np.ascontiguousarray(np.broadcast_to(np.asarray(positions), (P, SEQ))),
        "cols": np.ascontiguousarray(cols), "mats": mats, "causal": causal, "rows": reset, "band": band,
        "wpool": np.ascontiguousarray(wpool), "lora": np.ascontiguousarray(lora), "ada": ada, "w": w,
    }


def kernel(**inputs):
    import concourse.bacc as _bacc
    from concourse.bass_utils import run_bass_kernel_spmd as _run

    nc = _bacc.Bacc("TRN2", target_bir_lowering=False, num_devices=1)
    arrays = pack(**{k: np.asarray(v) for k, v in inputs.items()})
    args = [nc.dram_tensor(n, a.shape, mybir.dt.from_np(a.dtype), kind="ExternalInput").ap()
            for n, a in arrays.items()]
    out = nc.dram_tensor("out", (KT, P, SEQ), F32, kind="ExternalOutput").ap()
    build(nc, *args, out)
    r = _run(nc, [arrays], core_ids=[0])
    return np.ascontiguousarray(r.results[0]["out"].reshape(D, SEQ).T)[None]
```

```python
import math
from contextlib import ExitStack

import numpy as np

import concourse.bass as bass
from concourse import mybir

F32 = mybir.dt.float32
F32R = mybir.dt.float32r
I32 = mybir.dt.int32
ACT = mybir.ActivationFunctionType
ALU = mybir.AluOpType
AX = mybir.AxisListType

P = 128
SEQ = 512
D = 2048
KT = D // P
TB = SEQ // P
SLOTS = 4
SKT = KT // SLOTS
GC = 512
HEADS = 8
HD = 128
IDX_HEADS, IDX_DIM, N_SEL = 16, 64, 128
CH = 64
NCH = SEQ // CH
PAIRS = KT
ADA_GROUPS = 3 * D // GC
RMS_EPS, LN_EPS, GN_EPS, L2_EPS = 1e-6, 1e-5, 64e-5, 1e-12
ALPHA = 4.0 ** 0.25
ATT_SCALE = HD ** -0.5
IDX_SCALE = IDX_DIM ** -0.5
WI_SCALE = IDX_HEADS ** -0.5
NEG = -1e30
INADMISSIBLE = -3.0e38
TAKEN = -3.3e38

G_KW = 0
G_QI = 1
G_ATT = G_QI + 2
G_HG = G_ATT + HEADS
G_OUT1 = G_HG + HEADS
G_EVA = G_OUT1 + 4
G_POOL = G_EVA + HEADS
G_OUT2 = G_POOL + 4
G_LORA = G_OUT2 + 4
G_RW = G_LORA + 2
G_OUT3 = G_RW + 16
GROUPS = G_OUT3 + 4

COLS = {}
_at = 0
for _name, _n in (("c", 16), ("ada_b", 48), ("norm_g", 16), ("qg", 1), ("kg", 1), ("ikg", 1), ("lb0", 8),
                  ("lb1", 8), ("hg", 1), ("pscale", 8), ("mu", 96), ("w0", 16), ("a0", 16), ("k_k", 16),
                  ("k_a", 16), ("r_k", 16), ("gn_w", 16), ("gn_b", 16), ("ln_g", 32), ("ln_b", 32), ("freq", 2)):
    COLS[_name] = _at
    _at += _n
NCOLS = _at

MATS = ("ident", "mean128", "mean64", "swap128", "swap64", "neg_suffix", "neg_ones", "later_only", "later_neg",
        "mean2048", "ones64", "strict64", "incl_each", "lev1", "lev1t", "lev2t", "lev3t", "lev4t", "lev5t", "lev6t")
NMATS = len(MATS)
PI_IN = float(np.nextafter(np.float32(math.pi), np.float32(0)))


def _two_pi_parts():
    a = math.floor(2 * math.pi * 64) / 64
    b = math.floor((2 * math.pi - a) * 2 ** 17) / 2 ** 17
    return a, b, 2 * math.pi - a - b


TWO_PI = _two_pi_parts()
BAND_W = P + 16

ROW_W = [P * (b + 1) for b in range(TB)]
ROW_O = [sum(ROW_W[:b]) for b in range(TB)]
COL_W = [SEQ - P * b for b in range(TB)]
COL_O = [sum(COL_W[:b]) for b in range(TB)]
CAUSAL = sum(ROW_W)


def wait(eng, sem, value):
    if not isinstance(value, int) or value > 0:
        eng.wait_ge(sem, value)


def tile(buf, i):
    return buf[:, bass.ds(i * SEQ, SEQ)]


def build(nc, xT, positions, cols_d, mats_d, causal_i_d, rows_d, band_d, wpool_d, lora_d, ada_d, w_d, out):
    ctx = ExitStack()
    with ctx:
        def sb(name, shape, dt=F32):
            return ctx.enter_context(nc.sbuf_tensor(name, shape, dt))

        def sem(name):
            return ctx.enter_context(nc.semaphore(name))

        x1_d = nc.dram_tensor("x1_scratch", (KT, P, SEQ), F32).ap()
        rkvg_d = nc.dram_tensor("rkvg_scratch", (4, KT, P, SEQ), F32).ap()

        at = (nc.sbuf_base + 31) // 32 * 32
        WS = sb("WS", [P, (2 * KT + 4 * SKT) * SEQ])

        WS_AT = at

        def placed(name, shape, offset):
            return nc.alloc_sbuf_tensor_at(name, shape, F32R, offset=WS_AT + 4 * offset)

        XH = placed("XH", [P, KT * SEQ], 0)
        XL = placed("XL", [P, KT * SEQ], KT * SEQ)
        WH = [placed(f"WH{r}", [P, SKT, GC], (2 * KT + SKT * r) * SEQ) for r in range(2)]
        WL = [placed(f"WL{r}", [P, SKT, GC], (2 * KT + SKT * (2 + r)) * SEQ) for r in range(2)]
        X = sb("X", [P, KT * SEQ])
        RAW = [sb(f"RAW{r}", [P, SKT * GC]) for r in range(2)]
        NWK = 18
        WK = sb("WK", [P, NWK * SEQ])
        TBL = sb("TBL", [P, CAUSAL + 4 * SEQ])
        COL = sb("COL", [P, NCOLS])
        MOD = sb("MOD", [P, 48])
        LB = sb("LB", [P, 8])
        OMLB = sb("OMLB", [P, 8])
        MAT = sb("MAT", [P, NMATS * P])
        SMALL = sb("SMALL", [P, 128])
        CI = sb("CI", [P, 3 * P], I32)
        SC = sb("SC", [P, 8])
        OMU = sb("OMU", [P, 6 * KT])

        PJ = ctx.enter_context(nc.psum_tensor("PJ", [P, 4, SEQ], F32))
        AB = ctx.enter_context(nc.psum_tensor("AB", [P, 4, SEQ], F32))

        def mat(name):
            i = MATS.index(name)
            return MAT[:, i * P:(i + 1) * P]

        def col(name, i=0):
            return COL[:, bass.ds(COLS[name] + i, 1)]

        def wk(i, n=1):
            return WK[:, i * SEQ:(i + n) * SEQ]

        MASK = TBL[:, 0:CAUSAL]
        COS = TBL[:, CAUSAL:CAUSAL + SEQ]
        SIN = TBL[:, CAUSAL + SEQ:CAUSAL + 2 * SEQ]
        COSI = TBL[:, CAUSAL + 2 * SEQ:CAUSAL + 3 * SEQ]
        SINI = TBL[:, CAUSAL + 3 * SEQ:CAUSAL + 4 * SEQ]
        RESET = COSI
        BAND = TBL[:, 0:8 * BAND_W]
        WP = TBL[:, 8 * BAND_W:8 * BAND_W + SEQ]

        consts_in = sem("consts_in")
        x_in = sem("x_in")
        ada_in = [sem(f"ada_in{r}") for r in range(4)]
        cols_in = sem("cols_in")
        ada_used = sem("ada_used")
        ada_added = sem("ada_added")
        ones_set = sem("ones_set")
        row_sum = sem("row_sum")
        row_out = sem("row_out")
        row_used = sem("row_used")
        silu_c = sem("silu_c")
        mod_done = sem("mod_done")
        angles = sem("angles")
        x_sq = sem("x_sq")
        x_sq_used = sem("x_sq_used")
        x_sd = sem("x_sd")
        raw_in = [sem(f"raw_in{r}") for r in range(2)]
        wh_ready = sem("wh_ready")
        wl_ready = sem("wl_ready")
        slot_done = sem("slot_done")
        evac_a = sem("evac_a")
        evac_d = sem("evac_d")
        src_ready = sem("src_ready")
        xh_ready = sem("xh_ready")
        xl_ready = sem("xl_ready")
        table_in = sem("table_in")
        band_in = sem("band_in")
        S = {}

        def s(name):
            if name not in S:
                S[name] = sem(name)
            return S[name]

        for name in ("sq", "stat", "sd", "qn", "swapped", "roped", "scores", "masked", "expd", "probs", "pt_t",
                     "pt_a", "pt_d", "pv", "gs"):
            s("at_" + name)
        block = ctx.enter_context(nc.Block())

        ada_sum = lambda b: WS[:, b * SEQ:(b + 1) * SEQ]
        ada_row = lambda b: WS[0:1, (2 + b) * SEQ:(3 + b) * SEQ]
        SILU = SMALL[:, 32:48]
        ADA_PE = SKT - 1

        def ada_pe(pe, cg, b, squares=False):
            wait(pe, row_out, cg - 1)
            for k in range(SLOTS):
                pe.wait_ge(ada_in[k], 16 * cg + 16)
                for j in range(ADA_PE):
                    at = (k * SKT + j) * SEQ
                    m = nc.tensor.matmul(AB[0:1, 2 + b, :], SILU[:, SKT * k + j:SKT * k + j + 1], WK[:, at:at + SEQ],
                                         start=k == 0 and j == 0, stop=False)
                m.then_inc(ada_used, 1)
                if squares:
                    kt = SKT * (cg - 1) + k
                    pe.wait_ge(x_sq, kt + 1)
                    nc.tensor.matmul(AB[:, 0, :], mat("mean2048"), wk(16 + kt % 2), start=kt == 0,
                                     stop=kt == KT - 1).then_inc(x_sq_used, 1)
                if k == 0 and not (isinstance(cg, int) and cg == 0):
                    ada_columns(pe, cg - 1, 1 - b)
            pe.wait_ge(ada_added, SLOTS * cg + SLOTS)
            nc.tensor.matmul(AB[0:1, 2 + b, :], SC[:, 3:4], ada_sum(b), start=False, stop=True).then_inc(row_sum, 1)

        def ada_columns(pe, cg, b):
            pe.wait_ge(row_out, cg + 1)
            for n in range(4):
                m = nc.tensor.matmul(AB[:, 1, bass.ds(4 * cg + n, 1)], ada_row(b)[:, n * P:(n + 1) * P],
                                     mat("ident")[0:1, 0:1], start=True, stop=True)
            m.then_inc(row_used, 1)

        def ada_act(act, cg, b):
            act.wait_ge(row_sum, cg + 1)
            wait(act, row_used, cg - 1)
            nc.scalar.activation(ada_row(b), AB[0:1, 2 + b, :], ACT.Copy).then_inc(row_out, 1)

        def ada_dve(dve, cg, b):
            wait(dve, row_sum, cg - 1)
            for k in range(SLOTS):
                if k:
                    dve.drain()
                dve.wait_ge(ada_in[k], 16 * cg + 16)
                w, c = WK[:, (SKT * k + ADA_PE) * SEQ:SKT * (k + 1) * SEQ], SILU[:, SKT * k + ADA_PE:SKT * (k + 1)]
                if k == 0:
                    nc.vector.tensor_scalar(ada_sum(b), w, c, None, ALU.mult).then_inc(ada_added, 1)
                else:
                    nc.vector.scalar_tensor_tensor(ada_sum(b), w, c, ada_sum(b), ALU.mult,
                                                   ALU.add).then_inc(ada_added, 1)

        def pe_slot(pe, G, k, refill=None, tiles=4, bank=None):
            bank = PJ if bank is None else bank
            g = SLOTS * G + k
            if refill is not None:
                wait(pe, xl_ready, KT * refill + SKT * (k + 1))
            wait(pe, wl_ready, g + 1)
            for n in range(tiles):
                for j in range(SKT):
                    kt = SKT * k + j
                    hi = WH[k % 2][:, j, n * P:(n + 1) * P]
                    lo = WL[k % 2][:, j, n * P:(n + 1) * P]
                    xh, xl = tile(XH, kt), tile(XL, kt)
                    first, last = k == 0 and j == 0, k == SLOTS - 1 and j == SKT - 1
                    nc.tensor.matmul(bank[:, n, :], hi, xh, start=first, stop=False)
                    nc.tensor.matmul(bank[:, n, :], hi, xl, start=False, stop=False)
                    m = nc.tensor.matmul(bank[:, n, :], lo, xh, start=False, stop=last)
            m.then_inc(slot_done, 1)

        def pe_group(pe, G, steps=None, refill=None, tiles=4, bank=None, ago=0):
            wait(pe, evac_a, G - ago)
            wait(pe, evac_d, G - ago)
            for k in range(SLOTS):
                pe_slot(pe, G, k, refill, tiles, bank)
                if steps is not None:
                    steps(k)
            if steps is not None:
                steps(4)

        def act_split(act, G, k):
            g = SLOTS * G + k
            wait(act, raw_in[k % 2], 16 * (2 * G + k // 2 + 1))
            wait(act, slot_done, g - 1)
            nc.scalar.activation(WH[k % 2][:, :, :], RAW[k % 2][:, :].rearrange("p (j n) -> p j n", j=SKT),
                                 ACT.Copy).then_inc(wh_ready, 1)

        def dve_split(dve, G, k):
            g = SLOTS * G + k
            wait(dve, wh_ready, g + 1)
            nc.vector.tensor_tensor(WL[k % 2][:, :, :], RAW[k % 2][:, :].rearrange("p (j n) -> p j n", j=SKT),
                                    WH[k % 2][:, :, :].bitcast(F32), ALU.subtract).then_inc(wl_ready, 1)

        def act_group(act, G, evac, steps=None, pre=None, last=False):
            for k in range(SLOTS):
                if 0 < k < SLOTS - 1:
                    act_split(act, G, k + 1)
                elif k and not last:
                    act_split(act, G + 1, 0)
                if k < SLOTS - 1 and steps is not None:
                    steps(k)
            wait(act, slot_done, SLOTS * (G + 1))
            evac()
            if steps is not None:
                steps(3)
                steps(4)
            if not last:
                act_split(act, G + 1, 1)
            if pre is not None:
                pre()

        def dve_group(dve, G, evac, steps=None, pre=None, last=False):
            for k in range(SLOTS):
                if 0 < k < SLOTS - 1:
                    dve_split(dve, G, k + 1)
                elif k and not last:
                    dve_split(dve, G + 1, 0)
                if k < SLOTS - 1 and steps is not None:
                    steps(k)
            wait(dve, slot_done, SLOTS * (G + 1))
            evac()
            if steps is not None:
                steps(3)
                steps(4)
            if not last:
                dve_split(dve, G + 1, 1)
            if pre is not None:
                pre()

        def act_refill(act, e, src, G, tiles=range(KT)):
            for kt in tiles:
                wait(act, src_ready, KT * e + kt + 1)
                if kt % SKT == 0:
                    wait(act, slot_done, SLOTS * (G - 1) + kt // SKT + 1)
                nc.scalar.activation(tile(XH, kt), src(kt), ACT.Copy).then_inc(xh_ready, 1)

        def dve_refill(dve, e, src, tiles=range(KT)):
            for kt in tiles:
                wait(dve, xh_ready, KT * e + kt + 1)
                nc.vector.tensor_tensor(tile(XL, kt), src(kt), tile(XH, kt).bitcast(F32),
                                        ALU.subtract).then_inc(xl_ready, 1)

        def evac_act_plain(n0, n1, scale0=1.0):
            def f():
                if scale0 != 1.0:
                    nc.scalar.activation(wk(0), PJ[:, 0, :], ACT.Copy, scale=scale0)
                    nc.scalar.activation(wk(1), PJ[:, 1, :], ACT.Copy).then_inc(evac_a, 1)
                else:
                    nc.scalar.activation(WK[:, n0 * SEQ:n1 * SEQ].rearrange("p (b n) -> p b n", n=SEQ),
                                         PJ[:, n0:n1, :], ACT.Copy).then_inc(evac_a, 1)
            return f

        def evac_dve_plain(n0, n1):
            def f():
                nc.vector.tensor_copy(WK[:, n0 * SEQ:n1 * SEQ].rearrange("p (b n) -> p b n", n=SEQ),
                                      PJ[:, n0:n1, :]).then_inc(evac_d, 1)
            return f

        def transpose_blocks(dst, src):
            for t in range(TB):
                m = nc.tensor.transpose(dst[:, t * P:(t + 1) * P], src[:, t * P:(t + 1) * P], mat("ident"))
            return m

        def att_pe(pe, h, k):
            if k == 0:
                wait(pe, s("at_sq"), h + 1)
                wait(pe, s("mix_done"), h)
                for j in range(2):
                    nc.tensor.matmul(AB[:, j, :], mat("mean128"), wk(4 + j), start=True, stop=True)
                transpose_blocks(AB[:, 2, :], wk(2)).then_inc(s("at_stat"), 1)
            elif k == 1:
                wait(pe, s("at_qn"), h + 1)
                for j in range(2):
                    m = nc.tensor.matmul(AB[:, j, :], mat("swap128"), wk(j), start=True, stop=True)
                m.then_inc(s("at_swapped"), 1)
            elif k == 2:
                wait(pe, s("at_roped"), h + 1)
                for b in range(TB):
                    m = nc.tensor.matmul(AB[:, b, 0:ROW_W[b]], wk(4)[:, b * P:(b + 1) * P], wk(5)[:, 0:ROW_W[b]],
                                         start=True, stop=True)
                m.then_inc(s("at_scores"), 1)
            elif k == 3:
                wait(pe, s("at_probs"), h + 1)
                for b in range(TB):
                    for kb in range(b + 1):
                        m = nc.tensor.transpose(AB[:, kb, b * P:(b + 1) * P],
                                                WK[:, 10 * SEQ + ROW_O[b] + kb * P:10 * SEQ + ROW_O[b] + (kb + 1) * P],
                                                mat("ident"))
                m.then_inc(s("at_pt_t"), 1)
            else:
                wait(pe, s("at_pt_a"), h + 1)
                wait(pe, s("at_pt_d"), h + 1)
                for kb in range(TB):
                    m = nc.tensor.matmul(AB[:, 0, kb * P:SEQ], wk(9)[:, kb * P:(kb + 1) * P],
                                         wk(13 + kb)[:, kb * P:SEQ], start=kb == 0, stop=kb == TB - 1)
                m.then_inc(s("at_pv"), 1)

        def att_act(act, h, k):
            if k == 0:
                wait(act, s("at_stat"), h + 1)
                nc.scalar.activation(wk(6, 2).rearrange("p (b n) -> p b n", n=SEQ), AB[:, 0:2, :], ACT.Sqrt,
                                     bias=SC[:, 0:1]).then_inc(s("at_sd"), 1)
            elif k == 2:
                wait(act, s("at_masked"), h + 1)
                for b in range(TB):
                    a = WK[:, 10 * SEQ + ROW_O[b]:10 * SEQ + ROW_O[b] + ROW_W[b]]
                    m = nc.scalar.activation(a, a, ACT.Exp, bias=SMALL[:, b:b + 1], scale=ATT_SCALE,
                                             accum_out=SMALL[:, 4 + b:5 + b])
                m.then_inc(s("at_expd"), 1)
            elif k == 3:
                wait(act, s("at_pt_t"), h + 1)
                nc.scalar.activation(wk(13), AB[:, 0, :], ACT.Copy)
                nc.scalar.activation(wk(14)[:, P:SEQ], AB[:, 1, P:SEQ], ACT.Copy).then_inc(s("at_pt_a"), 1)

        def att_act_pre(act, h, G):
            nc.scalar.drain()
            nc.scalar.activation(wk(4, 2), wk(0, 2), ACT.Square).then_inc(s("at_sq"), 1)
            wait(act, evac_d, G + 1)
            wait(act, s("mix_done"), h)
            nc.scalar.activation(wk(8), wk(3), ACT.Silu).then_inc(s("at_gs"), 1)

        def att_dve(dve, h, k):
            if k == 0:
                wait(dve, s("at_stat"), h + 1)
                nc.vector.tensor_copy(wk(9), AB[:, 2, :])
                wait(dve, s("at_sd"), h + 1)
                nc.vector.reciprocal(wk(6, 2), wk(6, 2))
                dve.drain()
                nc.vector.scalar_tensor_tensor(wk(0), wk(0), col("qg"), wk(6), ALU.mult, ALU.mult)
                nc.vector.scalar_tensor_tensor(wk(1), wk(1), col("kg"), wk(7), ALU.mult,
                                               ALU.mult).then_inc(s("at_qn"), 1)
            elif k == 1:
                wait(dve, s("at_swapped"), h + 1)
                for j in range(2):
                    nc.vector.tensor_tensor(wk(6 + j), AB[:, j, :], SIN, ALU.mult)
                    nc.vector.tensor_tensor(wk(j), wk(j), COS, ALU.mult)
                dve.drain()
                nc.vector.tensor_tensor(wk(4, 2), wk(0, 2), wk(6, 2), ALU.add).then_inc(s("at_roped"), 1)
            elif k == 2:
                wait(dve, s("at_scores"), h + 1)
                for b in range(TB):
                    nc.vector.tensor_tensor(WK[:, 10 * SEQ + ROW_O[b]:10 * SEQ + ROW_O[b] + ROW_W[b]],
                                            AB[:, b, 0:ROW_W[b]], MASK[:, ROW_O[b]:ROW_O[b] + ROW_W[b]], ALU.add)
                dve.drain()
                for b in range(TB):
                    nc.vector.reduce_max(SMALL[:, 8 + b:9 + b],
                                         WK[:, 10 * SEQ + ROW_O[b]:10 * SEQ + ROW_O[b] + ROW_W[b]], AX.X)
                dve.drain()
                nc.vector.tensor_scalar(SMALL[:, 0:4], SMALL[:, 8:12], -ATT_SCALE, None,
                                        ALU.mult).then_inc(s("at_masked"), 1)
                wait(dve, s("at_expd"), h + 1)
                nc.vector.reciprocal(SMALL[:, 12:16], SMALL[:, 4:8])
                dve.drain()
                for b in range(TB):
                    a = WK[:, 10 * SEQ + ROW_O[b]:10 * SEQ + ROW_O[b] + ROW_W[b]]
                    m = nc.vector.tensor_scalar(a, a, SMALL[:, 12 + b:13 + b], None, ALU.mult)
                m.then_inc(s("at_probs"), 1)
            elif k == 3:
                wait(dve, s("at_pt_t"), h + 1)
                nc.vector.tensor_copy(wk(15)[:, 2 * P:SEQ], AB[:, 2, 2 * P:SEQ])
                nc.vector.tensor_copy(wk(16)[:, 3 * P:SEQ], AB[:, 3, 3 * P:SEQ]).then_inc(s("at_pt_d"), 1)
            else:
                wait(dve, s("at_pv"), h + 1)
                wait(dve, s("at_gs"), h + 1)
                nc.vector.tensor_tensor(tile(X, h), AB[:, 0, :], wk(8), ALU.mult).then_inc(s("mix_done"), 1)

        ix = lambda n: s("ix_" + n)
        for name in ("sq", "stat", "sd", "qn", "swapped", "roped", "key", "logits", "relu", "acc"):
            ix(name)

        def kw_pe(pe, k):
            if k == 0:
                wait(pe, ix("sq"), 1)
                nc.tensor.matmul(AB[:, 0, :], mat("mean64"), wk(4), start=True, stop=True)
                transpose_blocks(AB[:, 1, :], wk(1)).then_inc(ix("stat"), 1)
            elif k == 1:
                wait(pe, ix("qn"), 1)
                nc.tensor.matmul(AB[:, 0, :], mat("swap64"), wk(0), start=True,
                                 stop=True).then_inc(ix("swapped"), 1)

        def kw_act(act, k):
            if k == 0:
                wait(act, ix("stat"), 1)
                nc.scalar.activation(wk(6), AB[:, 0, :], ACT.Sqrt, bias=SC[:, 0:1]).then_inc(ix("sd"), 1)

        def kw_act_pre(act):
            nc.scalar.drain()
            nc.scalar.activation(wk(4), wk(0), ACT.Square).then_inc(ix("sq"), 1)

        def kw_dve(dve, k):
            if k == 0:
                wait(dve, ix("stat"), 1)
                nc.vector.tensor_scalar(wk(17), AB[:, 1, :], WI_SCALE, None, ALU.mult)
                wait(dve, ix("sd"), 1)
                nc.vector.reciprocal(wk(6), wk(6))
                dve.drain()
                nc.vector.scalar_tensor_tensor(wk(0), wk(0), col("ikg"), wk(6), ALU.mult,
                                               ALU.mult).then_inc(ix("qn"), 1)
            elif k == 1:
                wait(dve, ix("swapped"), 1)
                nc.vector.tensor_tensor(wk(6), AB[:, 0, :], SINI, ALU.mult)
                nc.vector.tensor_tensor(wk(8), wk(0), COSI, ALU.mult)
                dve.drain()
                nc.vector.tensor_tensor(wk(9), wk(8), wk(6), ALU.add).then_inc(ix("key"), 1)

        def qi_pe(pe, u, k):
            if k == 0:
                wait(pe, evac_a, G_QI + u + 1)
                wait(pe, evac_d, G_QI + u + 1)
                wait(pe, ix("acc"), 32 * u)
                wait(pe, ix("key"), 1)
                for j in range(4):
                    m = nc.tensor.matmul(AB[:, j, :], mat("swap64"), wk(j), start=True, stop=True)
                m.then_inc(ix("swapped"), 1)
            elif k == 1:
                wait(pe, ix("roped"), u + 1)
                n = 0
                for hh in range(8):
                    lo = (hh % 2) * IDX_DIM
                    for b in range(TB):
                        if n >= 4:
                            wait(pe, ix("relu"), 32 * u + n - 3)
                        nc.tensor.matmul(AB[:, n % 4, 0:ROW_W[b]],
                                         WK[lo:lo + IDX_DIM, (hh // 2) * SEQ + b * P:(hh // 2) * SEQ + (b + 1) * P],
                                         WK[lo:lo + IDX_DIM, 9 * SEQ:9 * SEQ + ROW_W[b]],
                                         start=True, stop=True).then_inc(ix("logits"), 1)
                        n += 1

        def qi_act(act, u, k):
            if k == 1:
                for n in range(32):
                    b = n % 4
                    wait(act, ix("logits"), 32 * u + n + 1)
                    wait(act, ix("acc"), 32 * u + n - 1)
                    nc.scalar.activation(wk(13 + n % 2)[:, 0:ROW_W[b]], AB[:, n % 4, 0:ROW_W[b]], ACT.Relu,
                                         scale=IDX_SCALE).then_inc(ix("relu"), 1)

        def qi_dve(dve, u, k):
            if k == 0:
                wait(dve, ix("swapped"), u + 2)
                for j in range(4):
                    nc.vector.tensor_tensor(wk(4 + (j % 4)), AB[:, j, :], SINI, ALU.mult)
                    nc.vector.tensor_tensor(wk(j), wk(j), COSI, ALU.mult)
                dve.drain()
                nc.vector.tensor_tensor(wk(0, 4), wk(0, 4), wk(4, 4), ALU.add).then_inc(ix("roped"), 1)
            elif k == 1:
                for n in range(32):
                    b, hh = n % 4, n // 4
                    acc = WK[:, 10 * SEQ + ROW_O[b]:10 * SEQ + ROW_O[b] + ROW_W[b]]
                    w = wk(17)[:, b * P + 8 * u + hh:b * P + 8 * u + hh + 1]
                    wait(dve, ix("relu"), 32 * u + n + 1)
                    r = wk(13 + n % 2)[:, 0:ROW_W[b]]
                    if u == 0 and hh == 0:
                        nc.vector.tensor_scalar(acc, r, w, None, ALU.mult).then_inc(ix("acc"), 1)
                    else:
                        nc.vector.scalar_tensor_tensor(acc, r, w, acc, ALU.mult, ALU.add).then_inc(ix("acc"), 1)
                    if n % 4 == 3:
                        dve.drain()
            elif k == 2 and u == 1:
                for b in range(TB):
                    nc.vector.memset(WK[0:CH, 10 * SEQ + ROW_O[b] + ROW_W[b] - CH:10 * SEQ + ROW_O[b] + ROW_W[b]],
                                     INADMISSIBLE)
                dve.drain()
                a = WK[:, 10 * SEQ + ROW_O[0]:10 * SEQ + ROW_O[0] + ROW_W[0]]
                nc.vector.tensor_scalar(MASK[:, 0:ROW_W[0]], a, -3.2e38 * 0.9, NEG, ALU.is_lt, ALU.mult)

        def select_rounds(dve, n):
            for r in range(n):
                for b in range(1, TB):
                    a = WK[:, 10 * SEQ + ROW_O[b]:10 * SEQ + ROW_O[b] + ROW_W[b]]
                    nc.vector.max(SMALL[:, 16 + 8 * b:24 + 8 * b], a)
                dve.drain()
                for b in range(1, TB):
                    a = WK[:, 10 * SEQ + ROW_O[b]:10 * SEQ + ROW_O[b] + ROW_W[b]]
                    nc.vector.match_replace(a, SMALL[:, 16 + 8 * b:24 + 8 * b], a, TAKEN)
                dve.drain()

        def select_dve(dve):
            quarter = N_SEL // 8 // 4
            select_rounds(dve, quarter)
            dve_split(dve, G_ATT + 1, 0)
            select_rounds(dve, quarter)
            wait(dve, slot_done, SLOTS * (G_ATT + 1))
            evac_dve_plain(2, 4)()
            dve_split(dve, G_ATT + 1, 1)
            select_rounds(dve, quarter)
            att_dve(dve, 0, 0)
            select_rounds(dve, N_SEL // 8 - 3 * quarter)
            for b in range(1, TB):
                a = WK[:, 10 * SEQ + ROW_O[b]:10 * SEQ + ROW_O[b] + ROW_W[b]]
                nc.vector.tensor_scalar(MASK[:, ROW_O[b]:ROW_O[b] + ROW_W[b]], a, -3.15e38, NEG, ALU.is_gt, ALU.mult)
            dve.drain()

        hg = lambda n: s("hg_" + n)
        for name in ("sig", "forget", "logf", "sums", "exps", "scaled", "tok", "v", "kl", "prod", "state", "o",
                     "sq", "ms", "sd"):
            hg(name)
        chunked = lambda a: a.rearrange("p (c n) -> p c n", n=CH)
        halves = lambda a, w: a.rearrange("p (c n) -> p c n", n=w)

        def hg_act_pre(act, h, G):
            nc.scalar.drain()
            wait(act, evac_d, G + 1)
            wait(act, s("mix_done"), HEADS + h)
            nc.scalar.activation(wk(4), wk(0), ACT.Silu)
            nc.scalar.activation(wk(5), wk(3), ACT.Silu)
            nc.scalar.activation(wk(6), wk(1), ACT.Sigmoid).then_inc(hg("sig"), 1)
            wait(act, hg("forget"), h + 1)
            nc.scalar.activation(wk(7), wk(6), ACT.Ln).then_inc(hg("logf"), 1)

        def hg_act_decays(act, h):
            wait(act, hg("sums"), h + 1)
            nc.scalar.activation(wk(12), wk(11), ACT.Exp, scale=-1.0)
            nc.scalar.activation(wk(11), wk(11), ACT.Exp)
            nc.scalar.activation(wk(9), wk(9), ACT.Exp)
            nc.scalar.activation(wk(14), wk(14), ACT.Exp)
            nc.scalar.activation(wk(10), wk(10), ACT.Exp)
            nc.scalar.activation(wk(13), wk(8), ACT.Exp)
            nc.scalar.activation(SMALL[:, 16:24], wk(8)[:, CH - 1:SEQ:CH], ACT.Exp).then_inc(hg("exps"), 1)

        def hg_dve_pre(dve, h):
            wait(dve, hg("sig"), h + 1)
            nc.vector.tensor_scalar(wk(6), wk(6), OMLB[:, bass.ds(h, 1)], LB[:, bass.ds(h, 1)], ALU.mult,
                                    ALU.add).then_inc(hg("forget"), 1)
            dve.drain()
            nc.vector.tensor_scalar(wk(1), wk(6), -1.0, 1.0, ALU.mult, ALU.add)

        def hg_dve_decays(dve, h):
            wait(dve, hg("logf"), h + 1)
            wait(dve, table_in, 16)
            nc.vector.tensor_tensor_scan(wk(8), RESET, wk(7), 0.0, ALU.mult, ALU.add)
            dve.drain()
            b3 = chunked(wk(8))
            for w, t in ((CH, 9), (CH // 2, 14)):
                b4, t4 = halves(wk(8), w), halves(wk(t), w)
                mid = b4[:, :, w // 2 - 1:w // 2].to_broadcast([P, SEQ // w, w // 2])
                nc.vector.tensor_tensor(t4[:, :, 0:w // 2], mid, b4[:, :, 0:w // 2], ALU.subtract)
                nc.vector.tensor_tensor(t4[:, :, w // 2:w], b4[:, :, w // 2:w], mid, ALU.subtract)
            b4 = halves(wk(8), CH // 4)
            nc.vector.tensor_tensor(halves(wk(11), CH // 4), b4,
                                    b4[:, :, CH // 8 - 1:CH // 8].to_broadcast([P, 4 * NCH, CH // 4]), ALU.subtract)
            nc.vector.tensor_tensor(chunked(wk(10)), b3[:, :, CH - 1:CH].to_broadcast([P, NCH, CH]), b3,
                                    ALU.subtract).then_inc(hg("sums"), 1)
            wait(dve, hg("exps"), h + 1)
            nc.vector.tensor_tensor(wk(11), wk(4), wk(11), ALU.mult)
            nc.vector.tensor_tensor(wk(12), wk(1), wk(12), ALU.mult)
            nc.vector.tensor_tensor(wk(10), wk(1), wk(10), ALU.mult)
            for w, t in ((CH, 9), (CH // 2, 14)):
                t4, k4, q4 = halves(wk(t), w), halves(wk(1), w), halves(wk(4), w)
                nc.vector.tensor_tensor(t4[:, :, 0:w // 2], t4[:, :, 0:w // 2], k4[:, :, 0:w // 2], ALU.mult)
                nc.vector.tensor_tensor(t4[:, :, w // 2:w], t4[:, :, w // 2:w], q4[:, :, w // 2:w], ALU.mult)
            nc.vector.tensor_tensor(wk(13), wk(4), wk(13), ALU.mult).then_inc(hg("scaled"), 1)

        blocks = lambda a: a.rearrange("p (t n) -> p t n", n=P)
        level_mask = lambda l: CI[:, l * P:(l + 1) * P].unsqueeze(1).to_broadcast([P, TB, P])
        VP = lambda t: WK[:, 15 * SEQ + 2 * P * t:15 * SEQ + 2 * P * (t + 1)]
        ST = lambda c: WK[:, 6 * SEQ + c * P:6 * SEQ + (c + 1) * P]

        def hg_pe(pe, h, k):
            if k == 1:
                wait(pe, hg("scaled"), h + 1)
                wait(pe, s("mix_done"), HEADS + h)
                transpose_blocks(AB[:, 0, :], wk(2))
                transpose_blocks(AB[:, 1, :], wk(10))
                for bank, z in ((2, 9), (3, 14)):
                    for t in range(TB):
                        ts = slice(t * P, (t + 1) * P)
                        m = nc.tensor.matmul(AB[:, bank, ts], wk(z)[:, ts], wk(z)[:, ts], start=True, stop=True)
                m.then_inc(hg("tok"), 1)
            elif k == 2:
                wait(pe, hg("v"), h + 1)
                wait(pe, hg("kl"), h + 1)
                for t in range(TB):
                    ts = slice(t * P, (t + 1) * P)
                    nc.tensor.matmul(AB[:, 2, ts], wk(12)[:, ts], wk(11)[:, ts], start=True, stop=True)
                for t in range(TB):
                    m = nc.tensor.matmul(AB[:, t // 2, (t % 2) * 2 * P:(t % 2 + 1) * 2 * P],
                                         wk(8)[:, t * P:(t + 1) * P], VP(t), start=True, stop=True)
                m.then_inc(hg("prod"), 1)
            elif k == 3:
                wait(pe, hg("state"), h + 1)
                for t in range(TB):
                    ts = slice(t * P, (t + 1) * P)
                    nc.tensor.matmul(AB[:, 3, ts], wk(17)[:, ts], wk(9)[:, ts], start=True, stop=True)
                    for c in (2 * t, 2 * t + 1):
                        if c:
                            cs = slice(c * CH, (c + 1) * CH)
                            m = nc.tensor.matmul(AB[:, 3, cs], ST(c), wk(13)[:, cs], start=False,
                                                 stop=True, skip_group_check=True)
                m.then_inc(hg("o"), 1)
            elif k == 4:
                wait(pe, hg("sq"), h + 1)
                nc.tensor.matmul(AB[:, 0, :], mat("mean128"), wk(11), start=True, stop=True).then_inc(hg("ms"), 1)

        def hg_act(act, h, k):
            if k == 0:
                hg_act_decays(act, h)
            elif k == 1:
                wait(act, hg("tok"), h + 1)
                nc.scalar.activation(wk(8), AB[:, 1, :], ACT.Copy).then_inc(hg("kl"), 1)
            elif k == 3:
                wait(act, hg("o"), h + 1)
                nc.scalar.activation(wk(10), AB[:, 3, :], ACT.Copy)
                nc.scalar.activation(wk(11), AB[:, 3, :], ACT.Square).then_inc(hg("sq"), 1)
            elif k == 4:
                wait(act, hg("ms"), h + 1)
                nc.scalar.activation(wk(12), AB[:, 0, :], ACT.Sqrt, bias=SC[:, 0:1]).then_inc(hg("sd"), 1)

        def hg_dve(dve, h, k):
            if k == 0:
                hg_dve_decays(dve, h)
            elif k == 1:
                nc.vector.memset(wk(15, 2), 0.0)
                wait(dve, hg("tok"), h + 1)
                nc.vector.tensor_copy(wk(17), AB[:, 0, :])
                nc.vector.memset(wk(9), 0.0)
                dve.drain()
                for bank in (2, 3):
                    nc.vector.copy_predicated(blocks(wk(9)), level_mask(bank - 2), AB[:, bank, :].rearrange(
                        "p (t n) -> p t n", n=P))
                    dve.drain()
                for half in range(2):
                    rows = slice(half * CH, (half + 1) * CH)
                    m = nc.vector.tensor_copy(
                        WK[rows, 15 * SEQ:17 * SEQ].rearrange("p (t c n) -> p t c n", c=2, n=P)[:, :, half, :],
                        AB[rows, 0, :].rearrange("p (t n) -> p t n", n=P))
                m.then_inc(hg("v"), 1)
            elif k == 2:
                wait(dve, hg("prod"), h + 1)
                nc.vector.memset(ST(0), 0.0)
                dve.drain()
                nc.vector.copy_predicated(blocks(wk(9)), level_mask(2), AB[:, 2, :].rearrange(
                    "p (t n) -> p t n", n=P))
                for c in range(NCH - 1):
                    nc.vector.scalar_tensor_tensor(ST(c + 1), ST(c), SMALL[:, 16 + c:17 + c],
                                                   AB[:, c // 4, (c % 4) * P:(c % 4 + 1) * P], ALU.mult, ALU.add)
                    dve.drain()
                nc.vector.drain().then_inc(hg("state"), 1)
            elif k == 4:
                wait(dve, hg("sd"), h + 1)
                nc.vector.reciprocal(wk(12), wk(12))
                dve.drain()
                nc.vector.scalar_tensor_tensor(wk(10), wk(10), col("hg"), wk(12), ALU.mult, ALU.mult)
                dve.drain()
                nc.vector.tensor_tensor(tile(X, HEADS + h), wk(10), wk(5), ALU.mult).then_inc(s("mix_done"), 1)


        SUM, RSTD = TBL[:, 0:SEQ], TBL[:, SEQ:2 * SEQ]
        SQR = [TBL[:, (2 + i) * SEQ:(3 + i) * SEQ] for i in range(2)]
        for name in ("in", "added", "stored"):
            s("res_" + name)

        def out_act(act, g, n, gate, bank):
            def f():
                wait(act, s("res_added"), g)
                for j in (2, 3):
                    scale = MOD[:, bass.ds(32 + n + j, 1)] if gate else 1.0
                    m = nc.scalar.activation(wk(14 + j), bank[:, j, :], ACT.Copy, scale=scale)
                m.then_inc(evac_a, 1)
            return f

        def out_dve(dve, g, n, kind, bank, G):
            def f():
                if kind != 3:
                    wait(dve, s("res_in"), 16 * g + 16)
                for j in range(4):
                    if j == 2:
                        wait(dve, evac_a, G + 1)
                    y = bank[:, j, :] if j < 2 else wk(14 + j)
                    x = tile(X, n + j)
                    if kind == 1:
                        if j < 2:
                            m = nc.vector.scalar_tensor_tensor(x, y, MOD[:, bass.ds(32 + n + j, 1)], wk(j), ALU.mult,
                                                               ALU.add)
                        else:
                            m = nc.vector.tensor_tensor(x, y, wk(j), ALU.add)
                    else:
                        m = nc.vector.scalar_tensor_tensor(x, x if kind == 3 else wk(j), ALPHA, y, ALU.mult, ALU.add)
                    if j == 1:
                        m.then_inc(evac_d, 1)
                if kind == 1:
                    dve.drain().then_inc(s("res_added"), 1)
                else:
                    dve.drain().then_inc(s("res_added"), 1)
                    for j in range(4):
                        nc.vector.tensor_tensor(SUM, SUM, tile(X, n + j), ALU.add)
                        dve.drain()
            return f

        for name in ("sum", "mean", "xc", "sq", "used", "sd", "scaled", "out"):
            s("ln_" + name)

        def ln_pe(pe, l):
            wait(pe, s("ln_sum"), l + 1)
            nc.tensor.matmul(AB[:, 0, :], mat("mean2048"), SUM, start=True, stop=True).then_inc(s("ln_mean"), 1)
            for kt in range(KT):
                wait(pe, s("ln_sq"), KT * l + kt + 1)
                nc.tensor.matmul(AB[:, 1, :], mat("mean2048"), SQR[kt % 2], start=kt == 0,
                                 stop=kt == KT - 1).then_inc(s("ln_used"), 1)

        def ln_act(act, l):
            for kt in range(KT):
                wait(act, s("ln_xc"), KT * l + kt + 1)
                wait(act, s("ln_used"), KT * l + kt - 1)
                nc.scalar.activation(SQR[kt % 2], tile(X, kt), ACT.Square).then_inc(s("ln_sq"), 1)
            wait(act, s("ln_used"), KT * (l + 1))
            nc.scalar.activation(RSTD, AB[:, 1, :], ACT.Sqrt, bias=SC[:, 1:2]).then_inc(s("ln_sd"), 1)
            for kt in range(KT):
                wait(act, s("ln_scaled"), KT * l + kt + 1)
                nc.scalar.activation(tile(X, kt), tile(X, kt), ACT.Identity, scale=col("ln_g", KT * l + kt),
                                     bias=col("ln_b", KT * l + kt)).then_inc(s("ln_out"), 1)

        def ln_dve(dve, l):
            dve.drain().then_inc(s("ln_sum"), 1)
            wait(dve, s("ln_mean"), l + 1)
            for kt in range(KT):
                nc.vector.tensor_tensor(tile(X, kt), tile(X, kt), AB[:, 0, :],
                                        ALU.subtract).then_inc(s("ln_xc"), 1)
            wait(dve, s("ln_sd"), l + 1)
            nc.vector.reciprocal(RSTD, RSTD)
            dve.drain()
            for kt in range(KT):
                nc.vector.tensor_tensor(tile(X, kt), tile(X, kt), RSTD, ALU.mult).then_inc(s("ln_scaled"), 1)

        sk = lambda n: s("sb_" + n)
        for name in ("gs", "v_t", "v", "zt", "z", "abs", "log", "sp", "later", "arg", "w", "o"):
            sk(name)
        PK = lambda i, kb: WK[:, i * SEQ + COL_O[kb]:i * SEQ + COL_O[kb] + COL_W[kb]]
        BASE = 2 * HEADS

        def sb_act_pre(act, h, G):
            wait(act, evac_d, G + 1)
            wait(act, s("mix_done"), BASE + h)
            nc.scalar.activation(wk(16), wk(3), ACT.Silu).then_inc(sk("gs"), 1)

        def sb_pe(pe, h, k):
            if k == 0:
                wait(pe, s("mix_done"), BASE + h)
                transpose_blocks(AB[:, 0, :], wk(2)).then_inc(sk("v_t"), 1)
            elif k == 1:
                wait(pe, sk("v"), h + 1)
                for kb in range(TB):
                    m = nc.tensor.matmul(AB[:, kb, kb * P:SEQ], wk(1)[:, kb * P:(kb + 1) * P], wk(0)[:, kb * P:SEQ],
                                         start=True, stop=True)
                m.then_inc(sk("zt"), 1)
            elif k == 2:
                wait(pe, sk("sp"), h + 1)
                for kb in range(TB):
                    more = kb < TB - 1
                    m = nc.tensor.matmul(AB[:, kb, kb * P:SEQ], mat("neg_suffix"), PK(10, kb), start=True,
                                         stop=not more)
                    if more:
                        m = nc.tensor.matmul(AB[:, kb, (kb + 1) * P:SEQ], mat("neg_ones"), later_sum(kb),
                                             start=False, stop=True)
                m.then_inc(sk("later"), 1)
            elif k == 3:
                wait(pe, sk("w"), h + 1)
                for kb in range(TB):
                    m = nc.tensor.matmul(AB[:, 0, kb * P:SEQ], wk(15)[:, kb * P:(kb + 1) * P], PK(7, kb),
                                         start=kb == 0, stop=kb == TB - 1)
                m.then_inc(sk("o"), 1)

        def later_sum(kb):
            if kb == 2:
                return PK(10, 3)
            o = 13 * SEQ + (0 if kb == 0 else COL_W[1])
            return WK[:, o:o + COL_W[kb + 1]]

        def sb_act(act, h, k):
            if k == 1:
                wait(act, sk("zt"), h + 1)
                for kb in range(TB):
                    m = nc.scalar.activation(PK(4, kb), AB[:, kb, kb * P:SEQ], ACT.Copy)
                m.then_inc(sk("z"), 1)
                wait(act, sk("abs"), h + 1)
                a = WK[:, 7 * SEQ:7 * SEQ + CAUSAL]
                nc.scalar.activation(a, a, ACT.Exp, scale=-1.0)
                act.drain()
                nc.scalar.activation(a, a, ACT.Ln, bias=SC[:, 3:4]).then_inc(sk("log"), 1)
            elif k == 2:
                wait(act, sk("arg"), h + 1)
                nc.scalar.activation(WK[:, 7 * SEQ:7 * SEQ + CAUSAL], WK[:, 4 * SEQ:4 * SEQ + CAUSAL],
                                     ACT.Exp).then_inc(sk("w"), 1)

        def sb_dve(dve, h, k):
            if k == 0:
                wait(dve, sk("v_t"), h + 1)
                nc.vector.tensor_copy(wk(15), AB[:, 0, :]).then_inc(sk("v"), 1)
            elif k == 1:
                z, a, sp = (WK[:, i * SEQ:i * SEQ + CAUSAL] for i in (4, 7, 10))
                wait(dve, sk("z"), h + 1)
                nc.vector.scalar_tensor_tensor(a, z, -1.0, z, ALU.mult, ALU.max).then_inc(sk("abs"), 1)
                wait(dve, sk("log"), h + 1)
                nc.vector.scalar_tensor_tensor(sp, z, 0.0, a, ALU.max, ALU.add)
                dve.drain()
                for kb in range(TB):
                    d = PK(10, kb)[:, 0:P]
                    nc.vector.tensor_tensor(d, d, mat("later_only"), ALU.mult)
                dve.drain()
                nc.vector.tensor_tensor(later_sum(1)[:, P:2 * P], PK(10, 2)[:, P:2 * P], PK(10, 3), ALU.add)
                nc.vector.tensor_copy(later_sum(1)[:, 0:P], PK(10, 2)[:, 0:P])
                dve.drain()
                nc.vector.tensor_tensor(later_sum(0)[:, P:3 * P], PK(10, 1)[:, P:3 * P], later_sum(1), ALU.add)
                nc.vector.tensor_copy(later_sum(0)[:, 0:P], PK(10, 1)[:, 0:P])
                dve.drain().then_inc(sk("sp"), 1)
            elif k == 2:
                wait(dve, sk("later"), h + 1)
                for kb in range(TB):
                    nc.vector.tensor_tensor(PK(4, kb), PK(4, kb), AB[:, kb, kb * P:SEQ], ALU.add)
                dve.drain()
                for kb in range(TB):
                    d = PK(4, kb)[:, 0:P]
                    nc.vector.tensor_tensor(d, d, mat("later_neg"), ALU.add)
                dve.drain().then_inc(sk("arg"), 1)
            elif k == 3:
                wait(dve, sk("o"), h + 1)
                wait(dve, sk("gs"), h + 1)
                wait(dve, s("res_stored"), 64)
                nc.vector.tensor_tensor(tile(X, h), AB[:, 0, :], wk(16), ALU.mult).then_inc(s("mix_done"), 1)

        pk = lambda n: s("pool_" + n)
        for name in ("gs", "u_t", "u_a", "u_d", "pooled", "copied", "mixed", "w_in"):
            pk(name)
        PBASE = BASE + HEADS

        def pool_act_pre(act, g, G):
            wait(act, evac_d, G + 1)
            wait(act, s("mix_done"), PBASE + g)
            nc.scalar.activation(wk(14, 2), wk(2, 2), ACT.Silu).then_inc(pk("gs"), 1)

        def pool_pe(pe, g, k):
            if k == 0:
                wait(pe, evac_a, G_POOL + 1 + g)
                wait(pe, s("mix_done"), PBASE + g)
                for c in range(2):
                    m = transpose_blocks(AB[:, c, :], wk(c))
                m.then_inc(pk("u_t"), 1)
            elif k == 1:
                wait(pe, band_in, 16)
                wait(pe, pk("u_a"), g + 1)
                wait(pe, pk("u_d"), g + 1)
                for c in range(2):
                    for t in range(TB):
                        w = min(BAND_W, SEQ - t * P)
                        band = BAND[:, bass.ds(g * 2 * BAND_W + (t > 0) * BAND_W, w)]
                        m = nc.tensor.matmul(AB[:, 2 + c, t * P:t * P + w], wk(4 + c)[:, t * P:(t + 1) * P], band,
                                             start=t == 0, stop=True, skip_group_check=True)
                m.then_inc(pk("pooled"), 1)
            elif k == 2:
                wait(pe, pk("copied"), g + 1)
                wait(pe, pk("w_in"), 16 * g + 16)
                for d in range(2):
                    for c in range(2):
                        m = nc.tensor.matmul(AB[:, d, :], WP[:, c * 256 + d * P:c * 256 + (d + 1) * P], wk(6 + c),
                                             start=c == 0, stop=c == 1)
                m.then_inc(pk("mixed"), 1)

        def pool_act(act, g, k):
            if k == 0:
                wait(act, pk("u_t"), g + 1)
                nc.scalar.activation(wk(4), AB[:, 0, :], ACT.Copy).then_inc(pk("u_a"), 1)
            elif k == 1:
                wait(act, pk("pooled"), g + 1)
                nc.scalar.activation(blocks4(wk(6, 2)), AB[:, 2:4, :], ACT.Copy).then_inc(pk("copied"), 1)

        blocks4 = lambda a: a.rearrange("p (b n) -> p b n", n=SEQ)

        def pool_dve(dve, g, k):
            if k == 0:
                wait(dve, pk("u_t"), g + 1)
                nc.vector.tensor_copy(wk(5), AB[:, 1, :]).then_inc(pk("u_d"), 1)
            elif k == 2:
                wait(dve, pk("mixed"), g + 1)
                wait(dve, pk("gs"), g + 1)
                for d in range(2):
                    nc.vector.scalar_tensor_tensor(tile(X, HEADS + 2 * g + d), AB[:, d, :], col("pscale", 2 * g + d),
                                                   wk(14 + d), ALU.mult, ALU.mult)
                dve.drain().then_inc(s("mix_done"), 1)

        s("mix_scaled")
        ZERO = SC[:, 5:6]
        def mix_act(act, e, k, G):
            for kt in range(SKT * k, SKT * (k + 1)):
                wait(act, xl_ready, KT * e + kt - 7)
                nc.scalar.activation(wk(4 + kt % 8), tile(X, kt), ACT.Identity, bias=ZERO,
                                     scale=OMU[:, bass.ds(KT * (e - 4) + kt, 1)]).then_inc(s("mix_scaled"), 1)
            act_refill(act, e, lambda kt: wk(4 + kt % 8), G, range(SKT * k, SKT * (k + 1)))

        def mix_dve(dve, e, k):
            for kt in range(SKT * k, SKT * (k + 1)):
                mixed = wk(4 + kt % 8)[:, 1:SEQ]
                wait(dve, s("mix_scaled"), KT * (e - 4) + kt + 1)
                nc.vector.scalar_tensor_tensor(mixed, tile(X, kt)[:, 0:SEQ - 1], col("mu", KT * (e - 4) + kt),
                                               mixed, ALU.mult, ALU.add).then_inc(src_ready, 1)
            dve_refill(dve, e, lambda kt: wk(4 + kt % 8), range(SKT * k, SKT * (k + 1)))

        TW, TA = TBL[:, 4 * SEQ:5 * SEQ], TBL[:, 5 * SEQ:6 * SEQ]
        LORA = 96
        s("rk_stored")

        def rw_act(act, n, bank):
            def f():
                wait(act, s("rk_stored"), 16 * n)
                nc.scalar.activation(blocks4(wk(0, 2)), bank[:, 0:2, :], ACT.Copy).then_inc(evac_a, 1)
            return f

        def rw_dve(dve, n, bank):
            def f():
                wait(dve, s("rk_stored"), 16 * n)
                nc.vector.tensor_copy(blocks4(wk(2, 2)), bank[:, 2:4, :]).then_inc(evac_d, 1)
            return f

        def ws(i, n=1):
            buf, first = ((WS, 0) if i < 48 else (RAW[0], 48) if i < 52 else (RAW[1], 52) if i < 56 else
                          (TBL, 54) if i < 58 else (WK, 42))
            return buf[:, (i - first) * SEQ:(i - first + n) * SEQ]

        wc = lambda i, c: ws(i, 2)[:, c * P:(c + 1) * P]
        wx = lambda i, c: ws(i)[:, c * CH:(c + 1) * CH]
        wh = lambda i, f: ws(i, 2)[:, f * SEQ:(f + 1) * SEQ]
        xh_ = lambda i, f: ws(i)[:, f * SEQ // 2:(f + 1) * SEQ // 2]
        bank = lambda i: PJ[:, i, :] if i < 4 else AB[:, i - 4, :]
        banks = lambda i: PJ[:, i:i + 2, :] if i < 4 else AB[:, i - 4:i - 2, :]
        bc = lambda i, c: bank(i + c // 4)[:, (c % 4) * P:(c % 4 + 1) * P]
        two = lambda a: a.rearrange("p (b n) -> p b n", n=SEQ)
        mats8 = lambda name: mat(name).unsqueeze(1).to_broadcast([P, NCH, P])
        by_mat = lambda a: a.rearrange("p (c n) -> p c n", n=P)
        bm = lambda i: banks(i).rearrange("p b (c n) -> p (b c) n", n=P)
        rows = lambda f: slice(f * CH, (f + 1) * CH)
        own = lambda a, f: a[rows(f), :].rearrange("p (c n) -> p c n", n=CH)
        diag = lambda a, f: a[rows(f)].rearrange("p (c n) -> p c n", n=P)[:, :, f * CH:(f + 1) * CH]
        (T_R, T_KEY, T_V, T_G, T_LOGW, T_A, T_B, T_BP, T_EB, T_EBP, T_EN, T_KK, T_NORM, T_K2, T_BONUS, T_RR,
         T_AKK, T_SG, T_WX, T_GS) = range(20)
        T_K, T_D, T_E, T_VT = 20, 22, 24, 26
        T_KT, T_DT, T_ET, T_VV = 28, 30, 32, 34
        T_N, T_L, T_X, T_Y, T_W = 36, (38, 40), 42, 44, 46
        T_P, T_Q, T_F = 40, 42, 46
        T_KE, T_R1, T_GG, T_S, T_RE, T_REFF, T_BV, T_RD = 48, 50, 52, 54, 56, 57, 58, 59
        T_O, T_O2 = T_EBP, T_EN
        DEC, DECN = SMALL[:, 80:88], SMALL[:, 88:96]
        LW2 = TBL[0:LORA, SEQ:SEQ + 2 * P]
        LEVELS = 5
        L2_SHIFT = 20
        wv = lambda n: s("wv_" + n)
        for name in ("in", "lw_in", "bv", "lora", "sig", "kk", "kksq", "ss", "ssm", "rnorm", "sums", "exps", 
                     "bonus", "expanded", "free", "tok", "tok_sb", "nt", "am", "am_sb", "bt", "gh", "nt_sb",
                     "lmask", "xy", "bt_sb", "wm", "w_sb", "ym", "r1m", "r1", "pq", "p_sb",
                     "q_sb", "fg", "fgr", "rr", "hop", "st", "om", "o", "omean", "oc", "osq", "ovar", "ors", "done",
                     "zero"):
            wv(name)

        def wv_pool(pool, p):
            pool.wait_ge(wv("nt_sb"), p + 1)
            for i in range(LEVELS):
                if i == 1:
                    pool.wait_ge(wv("xy"), 11 * p + 2)
                if i >= 2:
                    pool.wait_ge(wv("wm"), 10 * p + 2 * i - 2)
                nc.gpsimd.tensor_tensor(by_mat(ws(T_L[i % 2], 2)), by_mat(ws(T_N, 2)), mats8(f"lev{i + 2}t"),
                                        ALU.mult).then_inc(wv("lmask"), 1)

        def wv_load(sp, p):
            for m in range(4):
                sp.dma_start(ws(m), rkvg_d[m, bass.ds(p, 1), :, :].rearrange("a p n -> (a p) n")
                             ).then_inc(wv("in"), 16)

        def wv_load_lora(sp, p):
            sp.dma_start(LW2.rearrange("p (j n) -> p j n", j=2),
                         lora_d.rearrange("p (j n) -> p j n", j=2)[:, :, bass.ds(p * P, P)]
                         ).then_inc(wv("lw_in"), 16)

        def pe_inputs(pe, q, part):
            if part == 1:
                pe.wait_ge(wv("lw_in"), 16 * q + 16)
                nc.tensor.matmul(bank(6), LW2[:, 0:P], TW[0:LORA, :], start=True, stop=True)
                nc.tensor.matmul(bank(7), LW2[:, P:2 * P], TA[0:LORA, :], start=True,
                                 stop=True).then_inc(wv("lora"), 1)
            elif part == 2:
                pe.wait_ge(wv("kksq"), q + 1)
                pe.wait_ge(wv("sig"), q + 1)
                nc.tensor.matmul(bank(6), mat("ones64"), ws(T_NORM), start=True, stop=True).then_inc(wv("ss"), 1)

        def act_inputs(act, q, part):
            if part == 1:
                act.wait_ge(wv("kk"), q + 1)
                nc.scalar.activation(ws(T_NORM), ws(T_KK), ACT.Square).then_inc(wv("kksq"), 1)
                act.wait_ge(wv("lora"), q + 1)
                nc.scalar.activation(ws(T_LOGW), bank(6), ACT.Sigmoid, bias=col("w0", q))
                nc.scalar.activation(ws(T_A), bank(7), ACT.Sigmoid, bias=col("a0", q))
                nc.scalar.activation(ws(T_SG), ws(T_G), ACT.Sigmoid).then_inc(wv("sig"), 1)
            elif part == 3:
                act.wait_ge(wv("ssm"), q + 1)
                nc.scalar.activation(ws(T_NORM), ws(T_NORM), ACT.Ln, scale=2.0 ** L2_SHIFT)
                act.drain()
                nc.scalar.activation(ws(T_NORM), ws(T_NORM), ACT.Exp, scale=-0.5,
                                     bias=SC[:, 4:5]).then_inc(wv("rnorm"), 1)
            elif part == 4:
                act.wait_ge(wv("sums"), q + 1)
                nc.scalar.activation(ws(T_EBP), ws(T_BP), ACT.Exp)
                nc.scalar.activation(ws(T_EN), ws(T_B), ACT.Exp, scale=-1.0)
                nc.scalar.activation(ws(T_EB), ws(T_B), ACT.Exp)
                nc.scalar.activation(DECN, ws(T_B)[:, CH - 1:SEQ:CH], ACT.Exp).then_inc(wv("exps"), 1)

        def dve_inputs(dve, q, part):
            V, STT, TS = nc.vector.tensor_tensor, nc.vector.scalar_tensor_tensor, nc.vector.tensor_scalar
            if part == 0:
                dve.wait_ge(wv("in"), 64 * q + 64)
                TS(ws(T_KK), ws(T_KEY), col("k_k", q), None, ALU.mult).then_inc(wv("kk"), 1)
            elif part == 2:
                dve.wait_ge(wv("sig"), q + 1)
                TS(ws(T_LOGW), ws(T_LOGW), -math.exp(-0.5), None, ALU.mult)
                TS(ws(T_K2), ws(T_A), 1.0, col("k_a", q), ALU.subtract, ALU.mult)
                dve.drain()
                nc.vector.tensor_tensor_scan(ws(T_B), RSET, ws(T_LOGW), 0.0, ALU.mult, ALU.add)
                STT(ws(T_K2), ws(T_K2), 1.0, ws(T_KEY), ALU.add, ALU.mult)
                dve.drain()
                V(ws(T_BP), ws(T_B), ws(T_LOGW), ALU.subtract).then_inc(wv("sums"), 1)
                dve.wait_ge(wv("ss"), q + 1)
                TS(ws(T_NORM), bank(6), L2_EPS ** 2, None, ALU.max).then_inc(wv("ssm"), 1)
            elif part == 3:
                STT(ws(T_BONUS), ws(T_R), col("r_k", q), ws(T_K2), ALU.mult, ALU.mult)
                dve.wait_ge(wv("rnorm"), q + 1)
                V(ws(T_KK), ws(T_KK), ws(T_NORM), ALU.mult)
                dve.drain()
                V(ws(T_AKK), ws(T_KK), ws(T_A), ALU.mult)
            elif part == 4:
                dve.drain()
                dve.wait_ge(wv("exps"), q + 1)
                for f in range(2):
                    V(diag(ws(T_K, 2), f), own(ws(T_KK), f), own(ws(T_EBP), f), ALU.mult)
                    V(diag(ws(T_D, 2), f), own(ws(T_AKK), f), own(ws(T_EN), f), ALU.mult)
            elif part == 5:
                for f in range(2):
                    V(diag(ws(T_E, 2), f), own(ws(T_K2), f), own(ws(T_EN), f), ALU.mult)
                    m = nc.vector.tensor_copy(diag(ws(T_VT, 2), f), own(ws(T_V), f))
                m.then_inc(wv("expanded"), 1)

        def products(b, lhs, rhs, done, width=P):
            for c in range(NCH):
                o = bc(b, c) if width == P else bank(b)[:, c * width:(c + 1) * width]
                m = nc.tensor.matmul(o, lhs(c), rhs(c), start=True, stop=True)
            m.then_inc(done, 1)

        def pe_matrices(pe, q, piece):
            if piece < 4:
                src, b = ((T_K, 4), (T_D, 6), (T_VT, 4), (T_E, 6))[piece]
                if piece == 0:
                    pe.wait_ge(wv("expanded"), q + 1)
                else:
                    wait(pe, wv("fgr"), q) if piece == 1 else pe.wait_ge(wv("tok_sb"), 4 * q + piece - 1)
                for c in range(NCH):
                    m = nc.tensor.transpose(bc(b, c), wc(src, c), mat("ident"))
                m.then_inc(wv("tok"), 1)
            elif piece == 4:
                pe.wait_ge(wv("tok_sb"), 4 * q + 3)
                products(4, lambda c: wc(T_D, c), lambda c: wc(T_K, c), wv("nt"))
            elif piece == 5:
                pe.wait_ge(wv("tok_sb"), 4 * q + 4)
                products(6, lambda c: wc(T_K, c), lambda c: wc(T_D, c), wv("am"))
            elif piece == 6:
                pe.wait_ge(wv("nt_sb"), q + 1)
                products(4, lambda c: wc(T_E, c), lambda c: wc(T_K, c), wv("bt"))
            elif piece == 7:
                pe.wait_ge(wv("am_sb"), q + 1)
                pe.wait_ge(wv("rr"), q + 1)
                products(6, lambda c: wc(T_D, c), lambda c: wx(T_RR, c), wv("gh"), CH)
                products(7, lambda c: wc(T_E, c), lambda c: wx(T_RR, c), wv("gh"), CH)
            elif piece == 8:
                nc.tensor.matmul(bank(3), mat("ones64"), ws(T_BONUS), start=True, stop=True).then_inc(wv("bonus"), 1)

        def act_matrices(act, q):
            for i, (dst, b) in enumerate(((T_KT, 4), (T_DT, 6), (T_VV, 4), (T_ET, 6))):
                act.wait_ge(wv("tok"), 4 * q + i + 1)
                nc.scalar.activation(two(ws(dst, 2)), banks(b), ACT.Copy).then_inc(wv("tok_sb"), 1)
            act.wait_ge(wv("nt"), q + 1)
            nc.scalar.activation(two(ws(T_N, 2)), banks(4), ACT.Copy).then_inc(wv("nt_sb"), 1)

        def dve_rr(dve, q):
            nc.vector.tensor_tensor(ws(T_RR), ws(T_R), ws(T_EB), ALU.mult).then_inc(wv("rr"), 1)

        def dve_first_blocks(dve, q):
            V = nc.vector.tensor_tensor
            each = lambda name, f: mat(name)[rows(f), rows(f)].unsqueeze(1).to_broadcast([CH, NCH, CH])
            dve.wait_ge(wv("am"), q + 1)
            for f in range(2):
                m = V(own(ws(T_X), f), diag(banks(6).rearrange("p b n -> p (b n)"), f), each("lev1", f), ALU.mult)
            m.then_inc(wv("am_sb"), 1)
            dve.wait_ge(wv("nt_sb"), q + 1)
            V(by_mat(ws(T_Y, 2)), by_mat(ws(T_N, 2)), mats8("lev1t"), ALU.mult)
            dve.drain()
            for f in range(2):
                V(own(ws(T_X), f), each("ident", f), own(ws(T_X), f), ALU.subtract)
            V(by_mat(ws(T_Y, 2)), mats8("ident"), by_mat(ws(T_Y, 2)), ALU.subtract).then_inc(wv("xy"), 2)

        def dve_masks(dve, q):
            V = nc.vector.tensor_tensor
            dve.wait_ge(wv("bt"), q + 1)
            V(by_mat(ws(T_KE, 2)), bm(4), mats8("strict64"), ALU.mult)
            dve.wait_ge(wv("gh"), 2 * q + 2)
            incl = mat("incl_each")[:, 0:CH].unsqueeze(1).to_broadcast([P, NCH, CH])
            V(chunked(ws(T_RD)), chunked(bank(6)), incl, ALU.mult)
            V(chunked(ws(T_RE)), chunked(bank(7)), incl, ALU.mult)
            dve.drain().then_inc(wv("bt_sb"), 1)

        def dve_last_inputs(dve, q):
            V = nc.vector.tensor_tensor
            dve.wait_ge(wv("bonus"), q + 1)
            V(ws(T_BV), bank(3), ws(T_V), ALU.mult).then_inc(wv("bv"), 1)
            nc.vector.tensor_copy(DEC, DECN)
            V(ws(T_GS), ws(T_G), ws(T_SG), ALU.mult)
            dve.drain().then_inc(wv("free"), 1)

        def wv_pe(pe, p, more):
            for i in range(LEVELS):
                lvl = T_L[i % 2]
                pe.wait_ge(wv("lmask"), LEVELS * p + i + 1)
                for f in range(2):
                    pe.wait_ge(wv("xy"), 11 * p + 2 + (2 * (i - 1) + f + 1 if i else 0))
                    for c in range(4 * f, 4 * f + 4):
                        m = nc.tensor.matmul(bank(f)[:, (c % 4) * CH:(c % 4 + 1) * CH], wc(lvl, c), wx(T_X, c),
                                             start=True, stop=True)
                    m.then_inc(wv("wm"), 1)
                if i == 0:
                    pe.wait_ge(wv("bt_sb"), p + 1)
                    products(6, lambda c: wc(T_KE, c), lambda c: wc(T_VV, c), wv("r1m"))
                elif more:
                    if i == 1:
                        pe.wait_ge(wv("r1"), p + 1)
                    pe_inputs(pe, p + 1, i)
                for f in range(2):
                    pe.wait_ge(wv("w_sb"), 10 * p + 2 * i + f + 1)
                    if i == 0 and f == 0:
                        pe.wait_ge(wv("ors"), p)
                    elif i == 0:
                        pe.wait_ge(wv("bv"), p + 1)
                    for c in range(4 * f, 4 * f + 4):
                        if i < LEVELS - 1:
                            nc.tensor.matmul(bank(2 + f)[:, (c % 4) * CH:(c % 4 + 1) * CH], wc(T_Y, c), wx(T_WX, c),
                                             start=True, stop=True)
                        m = nc.tensor.matmul(bc(4, c), wc(T_W, c), wc(T_Y, c), start=True, stop=True)
                    m.then_inc(wv("ym"), 1)
            pe.wait_ge(wv("xy"), 11 * p + 11)
            products(2, lambda c: wc(T_Y, c), lambda c: wc(T_KT, c), wv("pq"))
            products(4, lambda c: wc(T_Y, c), lambda c: wc(T_R1, c), wv("pq"))
            pe.wait_ge(wv("p_sb"), p + 1)
            products(0, lambda c: wc(T_P, c), lambda c: wc(T_DT, c), wv("fg"))
            products(2, lambda c: wc(T_P, c), lambda c: wx(T_RD, c), wv("fg"), CH)
            pe.wait_ge(wv("q_sb"), p + 1)
            for c in range(NCH):
                nc.tensor.matmul(bc(6, c), wc(T_ET, c), wc(T_VV, c), start=True, stop=False)
                m = nc.tensor.matmul(bc(6, c), wc(T_DT, c), wc(T_Q, c), start=False, stop=True)
            m.then_inc(wv("fg"), 1)
            O = lambda c: bank(3)[:, c * CH:(c + 1) * CH]
            for c in range(NCH):
                nc.tensor.matmul(O(c), wc(T_Q, c), wx(T_RD, c), start=c == 0, stop=True, skip_group_check=True)
                nc.tensor.matmul(O(c), wc(T_VV, c), wx(T_RE, c), start=False, stop=True, skip_group_check=True)
            pe.wait_ge(wv("fgr"), p + 1)
            for c in range(1, NCH):
                if c > 1:
                    pe.wait_ge(wv("st"), 6 * p + c - 1)
                if c < NCH - 1:
                    nc.tensor.matmul(bank(c % 2)[:, 0:P], wc(T_F, c), state(c), start=True,
                                     stop=True).then_inc(wv("hop"), 1)
                m = nc.tensor.matmul(O(c), state(c), wx(T_REFF, c), start=False, stop=True, skip_group_check=True)
                if c == NCH - 1:
                    m.then_inc(wv("om"), 1)
                if more and c < 7:
                    pe_matrices(pe, p + 1, c - 1)
            if more:
                pe_matrices(pe, p + 1, 6)
            pe.wait_ge(wv("o"), p + 1)
            nc.tensor.matmul(bank(2), mat("mean64"), ws(T_O), start=True, stop=True).then_inc(wv("omean"), 1)
            if more:
                pe_matrices(pe, p + 1, 7)
            pe.wait_ge(wv("osq"), p + 1)
            nc.tensor.matmul(bank(2), mat("mean64"), ws(T_O2), start=True, stop=True).then_inc(wv("ovar"), 1)
            if more:
                pe_matrices(pe, p + 1, 8)

        def state(c):
            return wc(T_GG, 0) if c == 1 else wc(T_S, c)

        def wv_act(act, p, more):
            for i in range(LEVELS):
                for f in range(2):
                    act.wait_ge(wv("wm"), 10 * p + 2 * i + f + 1)
                    nc.scalar.activation(xh_(T_WX, f), bank(f)[:, 0:SEQ // 2], ACT.Copy)
                    for g in range(2):
                        m = nc.scalar.activation(diag(wh(T_W, f), g),
                                                 bank(f)[rows(g), 0:SEQ // 2].rearrange("p (c n) -> p c n", n=CH),
                                                 ACT.Copy)
                    m.then_inc(wv("w_sb"), 1)
                if i == 0:
                    act.wait_ge(wv("r1m"), p + 1)
                    nc.scalar.activation(two(ws(T_R1, 2)), banks(6), ACT.Copy).then_inc(wv("r1"), 1)
                if more:
                    act_inputs(act, p + 1, i)
            act.wait_ge(wv("pq"), 2 * p + 1)
            nc.scalar.activation(two(ws(T_P, 2)), banks(2), ACT.Copy).then_inc(wv("p_sb"), 1)
            if more:
                act_matrices(act, p + 1)
            act.wait_ge(wv("om"), p + 1)
            nc.scalar.activation(ws(T_O), bank(3), ACT.Copy).then_inc(wv("o"), 1)
            act.wait_ge(wv("oc"), p + 1)
            nc.scalar.activation(ws(T_O2), ws(T_O), ACT.Square).then_inc(wv("osq"), 1)
            act.wait_ge(wv("ovar"), p + 1)
            nc.scalar.activation(ws(T_O2), bank(2), ACT.Ln, bias=SC[:, 2:3])
            act.drain()
            nc.scalar.activation(ws(T_O2), ws(T_O2), ACT.Exp, scale=-0.5).then_inc(wv("ors"), 1)

        def wv_dve(dve, p, more):
            V, STT = nc.vector.tensor_tensor, nc.vector.scalar_tensor_tensor
            for i in range(LEVELS):
                for f in range(2):
                    dve.wait_ge(wv("ym"), 10 * p + 2 * i + f + 1)
                    if i < LEVELS - 1:
                        V(xh_(T_X, f), xh_(T_X, f), bank(2 + f)[:, 0:SEQ // 2], ALU.subtract)
                    m = V(wh(T_Y, f), wh(T_Y, f), bank(4 + f), ALU.subtract)
                    if i < LEVELS - 1 or f:
                        m.then_inc(wv("xy"), 1)
                if more and i < 4:
                    dve_inputs(dve, p + 1, i)
            if more:
                dve_inputs(dve, p + 1, 4)
            dve.wait_ge(wv("pq"), 2 * p + 2)
            nc.vector.tensor_scalar(two(ws(T_Q, 2)), banks(4), -1.0, None, ALU.mult).then_inc(wv("q_sb"), 1)
            if more:
                dve_inputs(dve, p + 1, 5)
            dve.wait_ge(wv("fg"), 3 * p + 1)
            V(by_mat(ws(T_F, 2)), mats8("ident"), bm(0), ALU.subtract)
            dve.wait_ge(wv("fg"), 3 * p + 2)
            V(ws(T_REFF), ws(T_RR), bank(2), ALU.subtract)
            dve.wait_ge(wv("fg"), 3 * p + 3)
            V(by_mat(ws(T_GG, 2)), bm(6), DEC.unsqueeze(2).to_broadcast([P, NCH, P]), ALU.mult)
            dve.drain().then_inc(wv("fgr"), 1)
            for c in range(1, NCH - 1):
                dve.wait_ge(wv("hop"), 6 * p + c)
                STT(wc(T_S, c + 1), bank(c % 2)[:, 0:P], DEC[:, c:c + 1], wc(T_GG, c), ALU.mult,
                    ALU.add).then_inc(wv("st"), 1)
                if more and c == 1:
                    dve_rr(dve, p + 1)
            if more:
                dve_first_blocks(dve, p + 1)
            dve.wait_ge(wv("omean"), p + 1)
            V(ws(T_O), ws(T_O), bank(2), ALU.subtract).then_inc(wv("oc"), 1)
            if more:
                dve_masks(dve, p + 1)
            dve.wait_ge(wv("ors"), p + 1)
            STT(ws(T_O), ws(T_O), col("gn_w", p), ws(T_O2), ALU.mult, ALU.mult)
            dve.drain()
            STT(ws(T_O), ws(T_O), col("gn_b", p), ws(T_BV), ALU.add, ALU.add)
            dve.drain()
            V(tile(WK, p), ws(T_O), ws(T_GS), ALU.mult).then_inc(wv("done"), 1)
            if more:
                dve.drain()
                dve_last_inputs(dve, p + 1)

        RSET = TBL[:, 0:SEQ]
        s("reset_in")
        s("out_stored")

        @block.sync
        def _(sp):
            sp.dma_start(COL[:, :], cols_d).then_inc(cols_in, 16)
            for k in range(SLOTS):
                sp.dma_start(WK[:, k * 4 * SEQ:(k + 1) * 4 * SEQ], ada_d[0, k]).then_inc(ada_in[k], 16)
            sp.dma_start(MAT[:, :], mats_d).then_inc(consts_in, 16)
            sp.dma_start(CI[:, :], causal_i_d).then_inc(consts_in, 16)
            sp.dma_start(MASK.bitcast(I32)[:, 0:SEQ], positions).then_inc(consts_in, 16)
            for q in range(4):
                sp.dma_start(X[:, q * 4 * SEQ:(q + 1) * 4 * SEQ].rearrange("p (k n) -> p k n", n=SEQ),
                             xT.rearrange("(k p) n -> p k n", p=P)[:, q * 4:(q + 1) * 4, :]).then_inc(x_in, 16)

            with sp.Fori(1, ADA_GROUPS) as cg:
                for k in range(SLOTS):
                    sp.wait_ge(ada_used, SLOTS * (cg - 1) + (k + 1))
                    sp.wait_ge(ada_added, SLOTS * (cg - 1) + (k + 1))
                    sp.dma_start(WK[:, k * 4 * SEQ:(k + 1) * 4 * SEQ],
                                 ada_d[bass.ds(cg, 1), k, :, :].rearrange("a p n -> (a p) n")
                                 ).then_inc(ada_in[k], 16)

            for k in range(SLOTS):
                wait(sp, wl_ready, k - 1)
                sp.dma_start(RAW[k % 2][:, :], w_d[0, k]).then_inc(raw_in[k % 2], 16)
            def w_load(G):
                for k in range(SLOTS):
                    sp.wait_ge(wl_ready, SLOTS * G + (k - 1))
                    sp.dma_start(RAW[k % 2][:, :], w_d[bass.ds(G, 1), k, :, :].rearrange("a p n -> (a p) n")
                                 ).then_inc(raw_in[k % 2], 16)

            with sp.Fori(1, G_OUT3) as G:
                w_load(G)
            sp.wait_ge(s("rk_stored"), 256)
            sp.wait_ge(wl_ready, SLOTS * G_OUT3)
            sp.wait_ge(slot_done, SLOTS * G_OUT3)
            wv_load(sp, 0)
            wv_load_lora(sp, 0)
            with sp.Fori(0, PAIRS - 1) as p:
                sp.wait_ge(wv("lora"), p + 1)
                wv_load_lora(sp, p + 1)
                sp.wait_ge(wv("free"), p + 1)
                wv_load(sp, p + 1)
            sp.wait_ge(wv("done"), PAIRS)
            with sp.Fori(G_OUT3, GROUPS) as G:
                w_load(G)
            for kt in range(KT):
                sp.wait_ge(s("ln_out"), KT + kt + 1)
                sp.dma_start(out[kt], tile(X, kt)).then_inc(s("out_stored"), 16)
            sp.wait_ge(s("out_stored"), 16 * KT)

        @block.gpsimd
        def _(pool):
            pool.wait_ge(ix("roped"), 2)
            pool.dma_start(RESET, rows_d[:, 0:SEQ]).then_inc(table_in, 16)
            pool.wait_ge(s("mix_done"), HEADS)
            pool.dma_start(BAND, band_d).then_inc(band_in, 16)
            pool.wait_ge(s("mix_done"), 2 * HEADS)
            for g in range(4):
                wait(pool, s("res_added"), g)
                src = xT.rearrange("(k p) n -> p k n", p=P)
                pool.dma_start(blocks4(wk(0, 4)), src[:, 4 * g:4 * g + 4, :]).then_inc(s("res_in"), 16)
                pool.wait_ge(s("res_added"), g + 1)
                pool.dma_start(x1_d[4 * g:4 * g + 4].rearrange("k p n -> p k n"),
                               blocks4(X[:, 4 * g * SEQ:4 * (g + 1) * SEQ])).then_inc(s("res_stored"), 16)
            for g in range(4):
                pool.wait_ge(s("mix_done"), PBASE if g == 0 else PBASE + g)
                pool.dma_start(WP, wpool_d[g]).then_inc(pk("w_in"), 16)
            pool.wait_ge(s("mix_done"), PBASE + 4)
            pool.wait_ge(s("res_stored"), 64)
            for g in range(4):
                wait(pool, s("res_added"), 4 + g)
                pool.dma_start(blocks4(wk(0, 4)), x1_d[4 * g:4 * g + 4].rearrange("k p n -> p k n")
                               ).then_inc(s("res_in"), 16)
            for n in range(16):
                m, g = n // 4, n % 4
                pool.wait_ge(evac_a, G_RW + n + 1)
                pool.wait_ge(evac_d, G_RW + n + 1)
                pool.dma_start(rkvg_d[m, 4 * g:4 * g + 4].rearrange("k p n -> p k n"),
                               blocks4(wk(0, 4))).then_inc(s("rk_stored"), 16)
            pool.wait_ge(s("rk_stored"), 256)
            pool.wait_ge(wl_ready, SLOTS * G_OUT3)
            pool.wait_ge(slot_done, SLOTS * G_OUT3)
            pool.dma_start(RSET, rows_d[:, 0:SEQ]).then_inc(s("reset_in"), 16)
            nc.gpsimd.memset(ws(T_K, 8), 0.0).then_inc(wv("zero"), 1)
            nc.gpsimd.memset(ws(T_W, 2), 0.0).then_inc(wv("zero"), 1)
            with pool.Fori(0, PAIRS) as p:
                wv_pool(pool, p)

        @block.tensor
        def _(pe):
            pe.wait_ge(silu_c, 1)
            pe.wait_ge(ones_set, 1)
            for cg in range(6):
                if cg == 1:
                    pe.wait_ge(consts_in, 48)
                ada_pe(pe, cg, cg % 2, squares=1 <= cg <= 4)
            with pe.Fori(3, ADA_GROUPS // 2) as i:
                for b in range(2):
                    ada_pe(pe, 2 * i + b, b)
            ada_columns(pe, ADA_GROUPS - 1, 1)

            pe_group(pe, G_KW, refill=0, tiles=2)
            pe_group(pe, G_QI, steps=lambda k: kw_pe(pe, k))
            pe_group(pe, G_QI + 1, steps=lambda k: qi_pe(pe, 0, k))
            pe_group(pe, G_ATT, steps=lambda k: qi_pe(pe, 1, k))
            with pe.Fori(1, HEADS) as h:
                pe_group(pe, G_ATT + h, steps=lambda k: att_pe(pe, h - 1, k))
            pe_group(pe, G_HG, steps=lambda k: att_pe(pe, HEADS - 1, k))
            with pe.Fori(1, HEADS) as h:
                pe_group(pe, G_HG + h, steps=lambda k: hg_pe(pe, h - 1, k))

            def pe_out(G0, refill, steps=None):
                pe_group(pe, G0, refill=refill, bank=PJ, ago=1, steps=steps)
                pe_group(pe, G0 + 1, bank=AB, ago=1)
                with pe.Fori(1, 2) as i:
                    pe_group(pe, G0 + 2 * i, bank=PJ, ago=1)
                    pe_group(pe, G0 + 2 * i + 1, bank=AB, ago=1)

            def last_hg_pe(k):
                for j in ((0, 1), (2, 3, 4), (), (), ())[k]:
                    hg_pe(pe, HEADS - 1, j)
            pe_out(G_OUT1, 1, last_hg_pe)
            pe_group(pe, G_EVA, refill=2)
            with pe.Fori(1, HEADS) as h:
                pe_group(pe, G_EVA + h, steps=lambda k: sb_pe(pe, h - 1, k))
            pe_group(pe, G_POOL, steps=lambda k: sb_pe(pe, HEADS - 1, k))
            with pe.Fori(1, 4) as g:
                pe_group(pe, G_POOL + g, steps=lambda k: pool_pe(pe, g - 1, k))
            for k in range(5):
                pool_pe(pe, 3, k)
            pe_out(G_OUT2, 3)
            ln_pe(pe, 0)
            pe_group(pe, G_LORA, refill=4, tiles=1)
            pe_group(pe, G_LORA + 1, refill=5, tiles=1, bank=AB, ago=1)
            with pe.Fori(0, 4) as m:
                for g in range(4):
                    pe_group(pe, G_RW + 4 * m + g, refill=6 + m if g == 0 else None, bank=(PJ, AB)[g % 2], ago=1)
            pe.wait_ge(evac_a, G_OUT3)
            pe.wait_ge(evac_d, G_OUT3)
            for i in range(LEVELS):
                pe_inputs(pe, 0, i)
            for i in range(9):
                pe_matrices(pe, 0, i)
            with pe.Fori(0, PAIRS - 1) as p:
                wv_pe(pe, p, True)
            wv_pe(pe, PAIRS - 1, False)
            pe_out(G_OUT3, 10)
            ln_pe(pe, 1)

        @block.scalar
        def _(act):
            act.wait_ge(cols_in, 16)
            nc.scalar.activation(SILU, COL[:, COLS["c"]:COLS["c"] + KT], ACT.Silu).then_inc(silu_c, 1)
            ada_act(act, 0, 0)
            for kt in range(KT):
                if kt % 4 == 0:
                    act.wait_ge(x_in, 64)
                wait(act, x_sq_used, kt - 1)
                nc.scalar.activation(wk(16 + kt % 2), tile(X, kt), ACT.Square).then_inc(x_sq, 1)
                if kt % 4 == 3:
                    ada_act(act, kt // 4 + 1, (kt // 4 + 1) % 2)
            act.wait_ge(angles, 1)
            for j, t in enumerate((COS, SIN, COSI, SINI)):
                nc.scalar.activation(t, t, ACT.Sin)
            nc.scalar.drain().then_inc(angles, 1)
            act.wait_ge(x_sq_used, KT)
            nc.scalar.activation(wk(16), AB[:, 0, :], ACT.Sqrt, bias=SC[:, 0:1]).then_inc(x_sd, 1)
            nc.scalar.activation(SMALL[:, 64:80], COL[:, COLS["lb0"]:COLS["lb0"] + 16], ACT.Exp)
            nc.scalar.drain().then_inc(mod_done, 1)
            ada_act(act, 5, 1)
            with act.Fori(3, ADA_GROUPS // 2) as i:
                for b in range(2):
                    ada_act(act, 2 * i + b, b)
            act.wait_ge(consts_in, 48)
            for k in range(2):
                act_split(act, 0, k)
            act_refill(act, 0, lambda kt: tile(X, kt), 0)
            act_group(act, G_KW, evac_act_plain(0, 1), pre=lambda: kw_act_pre(act))
            act_group(act, G_QI, evac_act_plain(0, 2), steps=lambda k: kw_act(act, k))
            act_group(act, G_QI + 1, evac_act_plain(0, 2), steps=lambda k: qi_act(act, 0, k))
            act_group(act, G_ATT, evac_act_plain(0, 2), steps=lambda k: qi_act(act, 1, k),
                      pre=lambda: att_act_pre(act, 0, G_ATT))
            with act.Fori(1, HEADS) as h:
                act_group(act, G_ATT + h, evac_act_plain(0, 2), steps=lambda k: att_act(act, h - 1, k),
                          pre=lambda: att_act_pre(act, h, G_ATT + h))
            act_group(act, G_HG, evac_act_plain(0, 2), steps=lambda k: att_act(act, HEADS - 1, k),
                      pre=lambda: hg_act_pre(act, 0, G_HG))
            with act.Fori(1, HEADS) as h:
                act_group(act, G_HG + h, evac_act_plain(0, 2), steps=lambda k: hg_act(act, h - 1, k),
                          pre=lambda: hg_act_pre(act, h, G_HG + h))
            for k in range(3):
                act_refill(act, 1, lambda kt: tile(X, kt), G_OUT1, range(SKT * k, SKT * (k + 1)))
                if k == 0:
                    hg_act(act, HEADS - 1, 0)
                hg_act(act, HEADS - 1, k + 1)
            hg_act(act, HEADS - 1, 4)

            def act_out(G0, done, gate):
                with act.Fori(0, 2) as i:
                    for j, bank in enumerate((PJ, AB)):
                        act_group(act, G0 + 2 * i + j, out_act(act, done + 2 * i + j, 8 * i + 4 * j, gate, bank))

            act_refill(act, 1, lambda kt: tile(X, kt), G_OUT1, range(KT - SKT, KT))
            act_out(G_OUT1, 0, True)
            act_refill(act, 2, lambda kt: tile(X, kt), G_EVA)
            act_group(act, G_EVA, evac_act_plain(0, 2, ATT_SCALE), pre=lambda: sb_act_pre(act, 0, G_EVA))
            with act.Fori(1, HEADS) as h:
                act_group(act, G_EVA + h, evac_act_plain(0, 2, ATT_SCALE), steps=lambda k: sb_act(act, h - 1, k),
                          pre=lambda: sb_act_pre(act, h, G_EVA + h))
            act_group(act, G_POOL, evac_act_plain(0, 2), steps=lambda k: sb_act(act, HEADS - 1, k),
                      pre=lambda: pool_act_pre(act, 0, G_POOL))
            with act.Fori(1, 4) as g:
                act_group(act, G_POOL + g, evac_act_plain(0, 2), steps=lambda k: pool_act(act, g - 1, k),
                          pre=lambda: pool_act_pre(act, g, G_POOL + g))
            for k in range(5):
                pool_act(act, 3, k)
            act_refill(act, 3, lambda kt: tile(X, kt), G_OUT2)
            act_out(G_OUT2, 4, False)
            ln_act(act, 0)
            act.drain()
            for k in range(SLOTS):
                mix_act(act, 4, k, G_LORA)
            act_group(act, G_LORA, lambda: nc.scalar.activation(TW, PJ[:, 0, :], ACT.Tanh).then_inc(evac_a, 1),
                      steps=lambda k: k < SLOTS and mix_act(act, 5, k, G_LORA + 1))
            act_group(act, G_LORA + 1, lambda: nc.scalar.drain().then_inc(evac_a, 1),
                      steps=lambda k: k < SLOTS and mix_act(act, 6, k, G_RW))
            with act.Fori(0, 3) as m:
                for g in range(4):
                    act_group(act, G_RW + 4 * m + g, rw_act(act, 4 * m + g, (PJ, AB)[g % 2]),
                              steps=(lambda k: k < SLOTS and mix_act(act, 7 + m, k, G_RW + 4 * m + 4)) if g == 3
                              else None)
            for g in range(4):
                act_group(act, G_RW + 12 + g, rw_act(act, 12 + g, (PJ, AB)[g % 2]), last=g == 3)
            act.wait_ge(wv("zero"), 2)
            for i in range(LEVELS):
                act_inputs(act, 0, i)
            act_matrices(act, 0)
            with act.Fori(0, PAIRS - 1) as p:
                wv_act(act, p, True)
            wv_act(act, PAIRS - 1, False)
            act.wait_ge(wv("done"), PAIRS)
            for k in range(2):
                act_split(act, G_OUT3, k)
            act_refill(act, 10, lambda kt: wk(kt), G_OUT3)
            with act.Fori(0, 1) as i:
                for j, b in enumerate((PJ, AB)):
                    act_group(act, G_OUT3 + 2 * i + j, out_act(act, 8 + 2 * i + j, 8 * i + 4 * j, False, b))
            for j, b in enumerate((PJ, AB)):
                act_group(act, G_OUT3 + 2 + j, out_act(act, 10 + j, 8 + 4 * j, False, b), last=j == 1)
            ln_act(act, 1)

        @block.vector
        def _(dve):
            nc.vector.memset(SC[:, 0:1], RMS_EPS)
            nc.vector.memset(SC[:, 1:2], LN_EPS)
            nc.vector.memset(SC[:, 2:3], GN_EPS)
            nc.vector.memset(SC[:, 3:4], 1.0).then_inc(ones_set, 1)
            nc.vector.memset(SC[:, 4:5], 0.5 * 20 * math.log(2))
            nc.vector.memset(SC[:, 5:6], 0.0)
            dve.wait_ge(cols_in, 16)
            nc.vector.tensor_scalar(OMU[:, :], COL[:, COLS["mu"]:COLS["mu"] + 6 * KT], -1.0, 1.0, ALU.mult, ALU.add)
            dve.wait_ge(silu_c, 1)
            ada_dve(dve, 0, 0)
            dve.wait_ge(consts_in, 48)
            nc.vector.tensor_copy(MASK[:, SEQ:2 * SEQ], MASK.bitcast(I32)[:, 0:SEQ])
            dve.drain()
            pos, turns = MASK[:, SEQ:2 * SEQ], MASK[:, 0:SEQ]
            for cg, (t, f, quarter) in enumerate(((COS, 0, 0.25), (SIN, 0, 0.0), (COSI, 1, 0.25), (SINI, 1, 0.0))):
                if cg:
                    ada_dve(dve, cg, cg % 2)
                nc.vector.tensor_scalar(t, pos, col("freq", f), None, ALU.mult)
                dve.drain()
                nc.vector.tensor_scalar(turns, t, 1.0 / (2 * math.pi), quarter, ALU.mult, ALU.add)
                dve.drain()
                nc.vector.tensor_scalar(turns, turns, 12582912.0, None, ALU.add)
                dve.drain()
                nc.vector.tensor_scalar(turns, turns, 12582912.0, None, ALU.subtract)
                dve.drain()
                for part in TWO_PI:
                    nc.vector.scalar_tensor_tensor(t, turns, -part, t, ALU.mult, ALU.add)
                    dve.drain()
                if quarter:
                    nc.vector.tensor_scalar(t, t, math.pi / 2, None, ALU.add)
                    dve.drain()
                nc.vector.tensor_scalar(t, t, PI_IN, -PI_IN, ALU.min, ALU.max)
            dve.drain().then_inc(angles, 1)
            ada_dve(dve, 4, 0)
            for cg in range(5, 9):
                ada_dve(dve, cg, cg % 2)
                if cg == 5:
                    dve.wait_ge(x_sd, 1)
                    nc.vector.reciprocal(wk(16), wk(16))
                    dve.drain()
                for kt in range(4 * (cg - 5), 4 * (cg - 4)):
                    nc.vector.tensor_tensor(tile(X, kt), tile(X, kt), wk(16), ALU.mult)
            ada_dve(dve, 9, 1)
            with dve.Fori(5, ADA_GROUPS // 2) as i:
                for b in range(2):
                    ada_dve(dve, 2 * i + b, b)
            nc.vector.drain().then_inc(x_sd, 1)
            dve.wait_ge(mod_done, 1)
            nc.vector.tensor_tensor(LB[:, :], SMALL[:, 64:72], SMALL[:, 72:80], ALU.add)
            dve.drain()
            nc.vector.reciprocal(LB[:, :], LB[:, :])
            dve.drain()
            nc.vector.tensor_tensor(LB[:, :], LB[:, :], SMALL[:, 64:72], ALU.mult)
            dve.drain()
            nc.vector.tensor_scalar(OMLB[:, :], LB[:, :], -1.0, 1.0, ALU.mult, ALU.add)
            dve.wait_ge(row_used, ADA_GROUPS)
            nc.vector.tensor_tensor(MOD[:, :], AB[:, 1, 0:48], COL[:, COLS["ada_b"]:COLS["ada_b"] + 48], ALU.add)
            dve.drain()
            nc.vector.scalar_tensor_tensor(MOD[:, 16:32], MOD[:, 16:32], 1.0,
                                           COL[:, COLS["norm_g"]:COLS["norm_g"] + 16], ALU.add, ALU.mult)
            dve.drain()
            for k in range(2):
                dve_split(dve, 0, k)
            for k in range(SLOTS):
                tiles = range(SKT * k, SKT * (k + 1))
                for kt in tiles:
                    nc.vector.tensor_scalar(tile(X, kt), tile(X, kt), MOD[:, 16 + kt:17 + kt], MOD[:, kt:kt + 1],
                                            ALU.mult, ALU.add).then_inc(src_ready, 1)
                dve_refill(dve, 0, lambda kt: tile(X, kt), tiles)
            dve_group(dve, G_KW, evac_dve_plain(1, 2))
            dve_group(dve, G_QI, evac_dve_plain(2, 4), steps=lambda k: kw_dve(dve, k))
            dve_group(dve, G_QI + 1, evac_dve_plain(2, 4), steps=lambda k: qi_dve(dve, 0, k))
            for k in range(3):
                if k:
                    dve_split(dve, G_ATT, k + 1)
                qi_dve(dve, 1, k)
            select_dve(dve)
            dve_group(dve, G_ATT + 1, evac_dve_plain(2, 4), steps=lambda k: k and att_dve(dve, 0, k))
            with dve.Fori(2, HEADS) as h:
                dve_group(dve, G_ATT + h, evac_dve_plain(2, 4), steps=lambda k: att_dve(dve, h - 1, k))
            dve_group(dve, G_HG, evac_dve_plain(2, 4), steps=lambda k: att_dve(dve, HEADS - 1, k),
                      pre=lambda: hg_dve_pre(dve, 0))
            with dve.Fori(1, HEADS) as h:
                dve_group(dve, G_HG + h, evac_dve_plain(2, 4), steps=lambda k: hg_dve(dve, h - 1, k),
                          pre=lambda: hg_dve_pre(dve, h))
            dve.drain().then_inc(src_ready, KT - 1)
            for k in range(3):
                dve_refill(dve, 1, lambda kt: tile(X, kt), range(SKT * k, SKT * (k + 1)))
                if k == 0:
                    hg_dve(dve, HEADS - 1, 0)
                hg_dve(dve, HEADS - 1, k + 1)
            hg_dve(dve, HEADS - 1, 4)

            def dve_out(G0, done, kind):
                with dve.Fori(0, 2) as i:
                    for j, bank in enumerate((PJ, AB)):
                        G = G0 + 2 * i + j
                        dve_group(dve, G, out_dve(dve, done + 2 * i + j, 8 * i + 4 * j, kind, bank, G))

            dve.drain().then_inc(src_ready, 1)
            dve_refill(dve, 1, lambda kt: tile(X, kt), range(KT - SKT, KT))
            dve_out(G_OUT1, 0, 1)
            dve.drain().then_inc(src_ready, KT)
            dve_refill(dve, 2, lambda kt: tile(X, kt))
            dve_group(dve, G_EVA, evac_dve_plain(2, 4))
            with dve.Fori(1, HEADS) as h:
                dve_group(dve, G_EVA + h, evac_dve_plain(2, 4), steps=lambda k: sb_dve(dve, h - 1, k))
            dve_group(dve, G_POOL, evac_dve_plain(2, 4), steps=lambda k: sb_dve(dve, HEADS - 1, k))
            with dve.Fori(1, 4) as g:
                dve_group(dve, G_POOL + g, evac_dve_plain(2, 4), steps=lambda k: pool_dve(dve, g - 1, k))
            for k in range(5):
                pool_dve(dve, 3, k)
            dve.drain().then_inc(src_ready, KT)
            dve_refill(dve, 3, lambda kt: tile(X, kt))
            nc.vector.memset(SUM, 0.0)
            dve.drain()
            dve_out(G_OUT2, 4, 2)
            ln_dve(dve, 0)
            for k in range(SLOTS):
                mix_dve(dve, 4, k)
            dve.wait_ge(s("ln_out"), KT)
            dve_group(dve, G_LORA, lambda: dve.drain().then_inc(evac_d, 1),
                      steps=lambda k: k < SLOTS and mix_dve(dve, 5, k))
            dve_group(dve, G_LORA + 1, lambda: nc.vector.tensor_copy(TA, AB[:, 0, :]).then_inc(evac_d, 1),
                      steps=lambda k: k < SLOTS and mix_dve(dve, 6, k))
            with dve.Fori(0, 3) as m:
                for g in range(4):
                    dve_group(dve, G_RW + 4 * m + g, rw_dve(dve, 4 * m + g, (PJ, AB)[g % 2]),
                              steps=(lambda k: k < SLOTS and mix_dve(dve, 7 + m, k)) if g == 3 else None)
            for g in range(4):
                dve_group(dve, G_RW + 12 + g, rw_dve(dve, 12 + g, (PJ, AB)[g % 2]), last=g == 3)
            dve.wait_ge(s("reset_in"), 16)
            dve.wait_ge(wv("zero"), 2)
            for i in range(6):
                dve_inputs(dve, 0, i)
            dve_rr(dve, 0)
            dve_first_blocks(dve, 0)
            dve_masks(dve, 0)
            dve_last_inputs(dve, 0)
            with dve.Fori(0, PAIRS - 1) as p:
                wv_dve(dve, p, True)
            wv_dve(dve, PAIRS - 1, False)
            nc.vector.memset(SUM, 0.0)
            dve.drain().then_inc(src_ready, KT)
            for k in range(2):
                dve_split(dve, G_OUT3, k)
            dve_refill(dve, 10, lambda kt: wk(kt))
            with dve.Fori(0, 1) as i:
                for j, b in enumerate((PJ, AB)):
                    G = G_OUT3 + 2 * i + j
                    dve_group(dve, G, out_dve(dve, 8 + 2 * i + j, 8 * i + 4 * j, 3, b, G))
            for j, b in enumerate((PJ, AB)):
                G = G_OUT3 + 2 + j
                dve_group(dve, G, out_dve(dve, 10 + j, 8 + 4 * j, 3, b, G), last=j == 1)
            ln_dve(dve, 1)


def constants():
    i = np.arange(P)
    k, m = i[:, None], i[None, :]
    same64 = (k // 64 == m // 64)
    f = {
        "ident": k == m, "mean128": np.full((P, P), 1 / 128), "mean64": same64 / 64, "ones64": same64 * 1.0,
        "mean2048": np.full((P, P), 1 / D),
        "swap128": np.where(k == m - 64, 1.0, 0) - np.where(k == m + 64, 1.0, 0),
        "swap64": same64 * (np.where(k == m - 32, 1.0, 0) - np.where(k == m + 32, 1.0, 0)),
        "neg_suffix": (k >= m) * -1.0, "neg_ones": -np.ones((P, P)),
        "later_only": (k < m) * 1.0, "later_neg": np.where(k < m, 0.0, NEG),
        "strict64": same64 & (k < m), "incl_each": k % 64 <= m % 64,
    }
    for l in range(1, 7):
        low = (k >> l == m >> l) & ((k >> (l - 1)) % 2 == 1) & ((m >> (l - 1)) % 2 == 0)
        f[f"lev{l}"], f[f"lev{l}t"] = low, low.T
    mats = np.concatenate([f[n].astype(np.float32) for n in MATS], axis=1)
    level = [(k // w == m // w) & (k % w < w // 2) & (m % w >= w // 2) for w in (CH, CH // 2)]
    level.append((k // (CH // 4) == m // (CH // 4)) & (k <= m))
    causal = np.concatenate(level, axis=1).astype(np.int32)
    t = np.arange(SEQ)
    reset = np.broadcast_to((t % CH != 0).astype(np.float32), (P, SEQ))
    band = np.zeros((P, 4, 2, BAND_W), np.float32)
    for g, w in enumerate((2, 4, 8, 16)):
        for first in range(2):
            q = np.arange(BAND_W)[None, :]
            inside = (q >= k) & (q - k < w)
            count = np.minimum(q + 1, w) if first == 0 else w
            band[:, g, first] = inside / count - (q == k)
    freq = np.zeros((P, 2), np.float32)
    for j, half in enumerate((64, 32)):
        inv = (10000.0 ** (-np.arange(half, dtype=np.float32) / np.float32(half)).astype(np.float64)).astype(np.float32)
        freq[:, j] = inv[i % half]
    return mats, causal, np.ascontiguousarray(reset), band.reshape(P, -1), freq


def by_channel(v):
    return np.ascontiguousarray(np.asarray(v).reshape(-1, P).T)


def pack_group(w):
    return w.reshape(SLOTS, SKT, P, GC).transpose(0, 2, 1, 3).reshape(SLOTS, P, SKT * GC)


def pack(x, c, positions, ada_w, ada_b, norm_g, w_in, q_norm_g, k_norm_g, idx_k_norm_g, hgrn_lb_logits,
         hgrn_norm_g, w_out, ev_w_in_2, ev_w_pool_2, ev_pool_scale_2, ev_w_out_2, od_mu_2, od_w_r_2, od_w_k_2,
         od_w_v_2, od_w_g_2, od_w0_2, od_w1_2, od_w2_2, od_a0_2, od_a1_2, od_a2_2, od_k_k_2, od_k_a_2,
         od_r_k_2, od_gn_w_2, od_gn_b_2, od_w_o_2, ln_g_2, ln_b_2):
    mats, causal, reset, band, freq = constants()
    cols = np.concatenate(
        [by_channel(c), by_channel(ada_b), by_channel(norm_g), by_channel(q_norm_g), by_channel(k_norm_g),
         by_channel(np.tile(np.asarray(idx_k_norm_g).reshape(-1), 2)), by_channel(hgrn_lb_logits),
         by_channel(hgrn_norm_g), by_channel(ev_pool_scale_2),
         by_channel(np.asarray(od_mu_2)[0][[1, 4, 0, 2, 3, 5]]), by_channel(od_w0_2),
         by_channel(od_a0_2), by_channel(od_k_k_2), by_channel(od_k_a_2), by_channel(od_r_k_2),
         by_channel(od_gn_w_2), by_channel(od_gn_b_2), by_channel(ln_g_2), by_channel(ln_b_2), freq], axis=1)
    w = np.empty((GROUPS, SLOTS, P, SKT * GC), np.float32)
    w_in, ev, at = np.asarray(w_in)[0], np.asarray(ev_w_in_2)[0], 0

    def put(columns):
        nonlocal at
        w[at] = pack_group(columns)
        at += 1

    def padded(*parts):
        z = np.zeros((D, GC), np.float32)
        for first, a in parts:
            z[:, first:first + a.shape[1]] = a
        return z

    iq = 4 * 1024
    ik, iw, rq = iq + 1024, iq + 1088, iq + 1104
    put(padded((0, w_in[:, ik:iw]), (64, w_in[:, ik:iw]), (128, w_in[:, iw:rq])))
    for g in range(2):
        put(w_in[:, iq + GC * g:iq + GC * (g + 1)])
    for base in (0, rq):
        for h in range(HEADS):
            put(np.concatenate([w_in[:, base + 1024 * i + P * h:base + 1024 * i + P * (h + 1)] for i in range(4)],
                               axis=1))
    for g in range(4):
        put(np.asarray(w_out)[0][:, GC * g:GC * (g + 1)])
    for h in range(HEADS):
        put(np.concatenate([ev[:, 1024 * i + P * h:1024 * i + P * (h + 1)] for i in range(4)], axis=1))
    for g in range(4):
        put(np.concatenate([ev[:, b + 256 * g:b + 256 * (g + 1)] for b in (4096, 5120)], axis=1))
    for g in range(4):
        put(np.asarray(ev_w_out_2)[0][:, GC * g:GC * (g + 1)])
    for m in (od_w1_2, od_a1_2):
        put(padded((0, np.asarray(m)[0])))
    for m in (od_w_r_2, od_w_k_2, od_w_v_2, od_w_g_2, od_w_o_2):
        for g in range(4):
            put(np.asarray(m)[0][:, GC * g:GC * (g + 1)])
    assert at == GROUPS
    ada = np.stack([pack_group(np.asarray(ada_w)[0][:, GC * g:GC * (g + 1)]) for g in range(ADA_GROUPS)])
    lora = np.concatenate([np.asarray(od_w2_2)[0], np.asarray(od_a2_2)[0]], axis=1)
    wpool = np.asarray(ev_w_pool_2)[0].reshape(4, 2, P, 256).transpose(0, 2, 1, 3).reshape(4, P, SEQ)
    return {
        "xT": np.ascontiguousarray(np.asarray(x)[0].T),
        "positions": np.ascontiguousarray(np.broadcast_to(np.asarray(positions), (P, SEQ))),
        "cols": np.ascontiguousarray(cols), "mats": mats, "causal": causal, "rows": reset, "band": band,
        "wpool": np.ascontiguousarray(wpool), "lora": np.ascontiguousarray(lora), "ada": ada, "w": w,
    }


def kernel(**inputs):
    import concourse.bacc as _bacc
    from concourse.bass_utils import run_bass_kernel_spmd as _run

    nc = _bacc.Bacc("TRN2", target_bir_lowering=False, num_devices=1)
    arrays = pack(**{k: np.asarray(v) for k, v in inputs.items()})
    args = [nc.dram_tensor(n, a.shape, mybir.dt.from_np(a.dtype), kind="ExternalInput").ap()
            for n, a in arrays.items()]
    out = nc.dram_tensor("out", (KT, P, SEQ), F32, kind="ExternalOutput").ap()
    build(nc, *args, out)
    r = _run(nc, [arrays], core_ids=[0])
    return np.ascontiguousarray(r.results[0]["out"].reshape(D, SEQ).T)[None]
```
